# Optimizing a Trainium2 kernel written in Bass

```python
import jax, jax.numpy as jnp
from jax import lax
import numpy as np

D_MODEL = 1024
BATCH = 1
SEQ = 256
DEPTH = 2
DEC_BATCH = 8
DEC_SEQ = 4
PAST_LEN = 2048
PAGE_SIZE = 128

N_EVEN = (DEPTH + 1) // 2
N_ODD = DEPTH // 2
CHUNK = 128
EPS = 1e-6
SGU_GROUPS = 4
SGU_DIM = 128
SGU_WIDTH = SGU_GROUPS * SGU_DIM
SC_WIDTH = 512
SC_CONV = 3
EVEN_IN = 2 * SGU_WIDTH + 3 * SC_WIDTH
EVEN_OUT = SGU_WIDTH + SC_WIDTH
RET_HEADS = D_MODEL // 256
RET_DK = 256
RET_DV = 512
ODD_IN = 2 * RET_HEADS * RET_DK + 2 * RET_HEADS * RET_DV
ODD_OUT = RET_HEADS * RET_DV
ROPE_BASE = 10000.0
N_MEM = 256
X_HEADS = 4
X_HD = D_MODEL // X_HEADS
D_FF = 2816
FFN_CONV = 3

kernel_name = 'hybrid_sgu_shortconv_retention_decoder_step'

def rms_norm(x, g):
    xf = x.astype(jnp.float32)
    y = xf * lax.rsqrt(jnp.mean(xf * xf, axis=-1, keepdims=True) + EPS)
    return (y * g.astype(jnp.float32)).astype(x.dtype)

def causal_dwconv(z, prev, w):
    K = w.shape[0]
    T = z.shape[1]
    zp = jnp.concatenate([prev.astype(z.dtype), z], axis=1)
    y = sum(w[j] * zp[:, j:j + T] for j in range(K))
    return y, zp[:, zp.shape[1] - (K - 1):]

def rope(x, pos):
    half = x.shape[-1] // 2
    inv = ROPE_BASE ** (-jnp.arange(half, dtype=jnp.float32) / half)
    ang = pos.astype(jnp.float32)[:, None] * inv[None, :]
    cos = jnp.cos(ang)[None, :, None, :]
    sin = jnp.sin(ang)[None, :, None, :]
    x1, x2 = x[..., :half], x[..., half:]
    return jnp.concatenate([x1 * cos - x2 * sin, x1 * sin + x2 * cos], axis=-1)

def spatial_gating(u, v, w_s, b_s):
    B, T, G, C = v.shape
    L = min(T, CHUNK)
    n = T // L
    mask = jnp.tril(jnp.ones((L, L), dtype=bool))
    w = jnp.where(mask[None], w_s[:, :L, :L], 0).astype(v.dtype)
    vc = v.reshape(B, n, L, G, C)
    mixed = jnp.einsum('gts,bnsgc->bntgc', w, vc) + b_s[:, :L].T.astype(v.dtype)[None, None, :, :, None]
    return u * mixed.reshape(B, T, G, C)

def retention_block(q, k, v, s_prev, log_g):
    L = q.shape[1]
    i = jnp.arange(L, dtype=jnp.float32)
    diff = i[:, None] - i[None, :]
    dmat = jnp.where(diff[None] >= 0, jnp.exp(log_g[:, None, None] * jnp.maximum(diff, 0.0)[None]), 0.0)
    scores = jnp.einsum('bihd,bjhd->bhij', q, k) * dmat[None]
    o = jnp.einsum('bhij,bjhe->bihe', scores, v)
    q_decay = jnp.exp(log_g[None, :] * (i[:, None] + 1.0))
    o = o + jnp.einsum('bihd,bhde->bihe', q, s_prev) * q_decay[None, :, :, None]
    k_decay = jnp.exp(log_g[None, :] * (L - 1.0 - i)[:, None])
    s_new = jnp.exp(log_g * L)[None, :, None, None] * s_prev + jnp.einsum('bjhd,bjhe->bhde', k * k_decay[None, :, :, None], v)
    return o, s_new

def retention(q, k, v, s0, log_g):
    B, T = q.shape[0], q.shape[1]
    L = min(T, CHUNK)
    n = T // L

    def split(a):
        return jnp.moveaxis(a.reshape(B, n, L, *a.shape[2:]), 1, 0)

    def step(s, qkv):
        qc, kc, vc = qkv
        o, s = retention_block(qc, kc, vc, s, log_g)
        return s, o

    s_T, o = lax.scan(step, s0, (split(q), split(k), split(v)))
    o = jnp.moveaxis(o, 0, 1).reshape(B, T, *o.shape[3:])
    return o, s_T

def setup_inputs(seed: int = 0) -> dict:
    key = jax.random.key(seed)
    keys = jax.random.split(key, 64)
    ctr = [0]

    def nk():
        ctr[0] += 1
        return keys[ctr[0] - 1]

    def nrm(shape, scale=1.0):
        return jax.random.normal(nk(), shape, jnp.float32) * scale

    def gain(shape):
        return 1.0 + 0.05 * nrm(shape)

    D = D_MODEL
    return {
        'x_prompt': nrm((BATCH, SEQ, D)),
        'x_sample': nrm((DEC_BATCH, DEC_SEQ, D)),
        'mem_prompt': nrm((BATCH, N_MEM, D)),
        'cache_mem_k': nrm((DEPTH, DEC_BATCH, N_MEM, X_HEADS, X_HD)),
        'cache_mem_v': nrm((DEPTH, DEC_BATCH, N_MEM, X_HEADS, X_HD)),
        'state_shortconv': nrm((N_EVEN, DEC_BATCH, SC_CONV - 1, SC_WIDTH)),
        'state_retention': nrm((N_ODD, DEC_BATCH, RET_HEADS, RET_DK, RET_DV)),
        'state_ffn_conv': nrm((DEPTH, DEC_BATCH, FFN_CONV - 1, 2 * D_FF)),
        'norm_mix_pre': gain((DEPTH, D)),
        'norm_mix_post': gain((DEPTH, D)),
        'w_in_even': nrm((N_EVEN, D, EVEN_IN), D ** -0.5),
        'sgu_vnorm': gain((N_EVEN, SGU_WIDTH)),
        'sgu_w': nrm((N_EVEN, SGU_GROUPS, CHUNK, CHUNK), CHUNK ** -0.5),
        'sgu_b': 1.0 + 0.1 * nrm((N_EVEN, SGU_GROUPS, CHUNK)),
        'conv_short': nrm((N_EVEN, SC_CONV, SC_WIDTH), SC_CONV ** -0.5),
        'w_out_even': nrm((N_EVEN, EVEN_OUT, D), EVEN_OUT ** -0.5),
        'w_in_odd': nrm((N_ODD, D, ODD_IN), D ** -0.5),
        'w_out_odd': nrm((N_ODD, ODD_OUT, D), ODD_OUT ** -0.5),
        'norm_x_pre': gain((DEPTH, D)),
        'norm_x_post': gain((DEPTH, D)),
        'norm_mem': gain((DEPTH, D)),
        'w_xq': nrm((DEPTH, D, D), D ** -0.5),
        'w_xk': nrm((DEPTH, D, D), D ** -0.5),
        'w_xv': nrm((DEPTH, D, D), D ** -0.5),
        'w_xo': nrm((DEPTH, D, D), D ** -0.5),
        'norm_ffn_pre': gain((DEPTH, D)),
        'norm_ffn_post': gain((DEPTH, D)),
        'w_ffn_up': nrm((DEPTH, D, 2 * D_FF), D ** -0.5),
        'conv_ffn': nrm((DEPTH, FFN_CONV, 2 * D_FF), FFN_CONV ** -0.5),
        'w_ffn_down': nrm((DEPTH, D_FF, D), D_FF ** -0.5),
    }

def reference(x_prompt, x_sample, mem_prompt, cache_mem_k, cache_mem_v, state_shortconv, state_retention, state_ffn_conv,
              norm_mix_pre, norm_mix_post, w_in_even, sgu_vnorm, sgu_w, sgu_b, conv_short, w_out_even, w_in_odd, w_out_odd,
              norm_x_pre, norm_x_post, norm_mem, w_xq, w_xk, w_xv, w_xo, norm_ffn_pre, norm_ffn_post, w_ffn_up, conv_ffn, w_ffn_down):
    f32 = jnp.float32

    def even_mixer(e, h, conv_prev):
        B, T, _ = h.shape
        z = h @ w_in_even[e]
        u, v, bg, cg, hin = jnp.split(z, [SGU_WIDTH, 2 * SGU_WIDTH, 2 * SGU_WIDTH + SC_WIDTH, 2 * SGU_WIDTH + 2 * SC_WIDTH], axis=-1)
        u = jax.nn.gelu(u, approximate=True)
        v = rms_norm(jax.nn.gelu(v, approximate=True), sgu_vnorm[e])
        a = spatial_gating(u.reshape(B, T, SGU_GROUPS, SGU_DIM), v.reshape(B, T, SGU_GROUPS, SGU_DIM), sgu_w[e], sgu_b[e]).reshape(B, T, SGU_WIDTH)
        cz, conv_new = causal_dwconv(cg * hin, conv_prev, conv_short[e])
        out = jnp.concatenate([a, bg * cz], axis=-1) @ w_out_even[e]
        return out, conv_new, v

    def odd_mixer(o, h, s_prev, pos):
        B, T, _ = h.shape
        nq = RET_HEADS * RET_DK
        nv = RET_HEADS * RET_DV
        z = h @ w_in_odd[o]
        q, k, v, g = jnp.split(z, [nq, 2 * nq, 2 * nq + nv], axis=-1)
        q = rope(q.reshape(B, T, RET_HEADS, RET_DK).astype(f32), pos) * (RET_DK ** -0.5)
        k = rope(k.reshape(B, T, RET_HEADS, RET_DK).astype(f32), pos)
        v = v.reshape(B, T, RET_HEADS, RET_DV).astype(f32)
        log_g = jnp.log1p(-jnp.exp2(-5.0 - jnp.arange(RET_HEADS, dtype=f32)))
        r, s_new = retention(q, k, v, s_prev.astype(f32), log_g)
        mu = jnp.mean(r, axis=-1, keepdims=True)
        var = jnp.mean(jnp.square(r - mu), axis=-1, keepdims=True)
        r = ((r - mu) * lax.rsqrt(var + EPS)).reshape(B, T, nv).astype(h.dtype)
        out = (jax.nn.silu(g) * r) @ w_out_odd[o]
        return out, s_new.astype(h.dtype)

    def cross_attn(l, h, mk, mv):
        B, T, _ = h.shape
        q = (h @ w_xq[l]).reshape(B, T, X_HEADS, X_HD).astype(f32)
        s = jnp.einsum('bthd,bmhd->bhtm', q, mk.astype(f32)) * (X_HD ** -0.5)
        p = jax.nn.softmax(s, axis=-1)
        o = jnp.einsum('bhtm,bmhd->bthd', p, mv.astype(f32)).reshape(B, T, D_MODEL).astype(h.dtype)
        return o @ w_xo[l]

    def ffn(l, h, prev):
        up = h @ w_ffn_up[l]
        up, new = causal_dwconv(up, prev, conv_ffn[l])
        gt, val = jnp.split(up, [D_FF], axis=-1)
        return (jax.nn.gelu(gt, approximate=True) * val) @ w_ffn_down[l], new

    def trunk(x, pos0, mem_k, mem_v, conv_prev, ret_prev, ffn_prev):
        T = x.shape[1]
        pos = pos0 + jnp.arange(T, dtype=jnp.int32)
        new_conv, new_sgu, new_ret, new_ffn = [], [], [], []
        for l in range(DEPTH):
            h = rms_norm(x, norm_mix_pre[l])
            if l % 2 == 0:
                m, c, vrows = even_mixer(l // 2, h, conv_prev[l // 2])
                new_conv.append(c)
                new_sgu.append(vrows)
            else:
                m, s = odd_mixer(l // 2, h, ret_prev[l // 2], pos)
                new_ret.append(s)
            x = x + rms_norm(m, norm_mix_post[l])
            h = rms_norm(x, norm_x_pre[l])
            x = x + rms_norm(cross_attn(l, h, mem_k[l], mem_v[l]), norm_x_post[l])
            h = rms_norm(x, norm_ffn_pre[l])
            f, c = ffn(l, h, ffn_prev[l])
            new_ffn.append(c)
            x = x + rms_norm(f, norm_ffn_post[l])
        return x, jnp.stack(new_conv), jnp.stack(new_sgu), jnp.stack(new_ret), jnp.stack(new_ffn)

    Bp = x_prompt.shape[0]
    mks, mvs = [], []
    for l in range(DEPTH):
        mn = rms_norm(mem_prompt, norm_mem[l])
        mks.append((mn @ w_xk[l]).reshape(Bp, N_MEM, X_HEADS, X_HD))
        mvs.append((mn @ w_xv[l]).reshape(Bp, N_MEM, X_HEADS, X_HD))
    mem_k_prompt = jnp.stack(mks)
    mem_v_prompt = jnp.stack(mvs)
    dt = x_prompt.dtype
    zero_conv = jnp.zeros((N_EVEN, Bp, SC_CONV - 1, SC_WIDTH), dt)
    zero_ret = jnp.zeros((N_ODD, Bp, RET_HEADS, RET_DK, RET_DV), f32)
    zero_ffn = jnp.zeros((DEPTH, Bp, FFN_CONV - 1, 2 * D_FF), dt)
    y_prompt, shortconv_prompt, _, retention_prompt, ffn_conv_prompt = trunk(
        x_prompt, 0, mem_k_prompt, mem_v_prompt, zero_conv, zero_ret, zero_ffn)

    y_sample, shortconv_sample, sgu_v_sample, retention_sample, ffn_conv_sample = trunk(
        x_sample, PAST_LEN, cache_mem_k, cache_mem_v, state_shortconv, state_retention, state_ffn_conv)

    return (y_prompt, y_sample, mem_k_prompt, mem_v_prompt, shortconv_prompt, shortconv_sample, sgu_v_sample,
            retention_prompt, retention_sample, ffn_conv_prompt, ffn_conv_sample)


_drawn_inputs = setup_inputs


def setup_inputs(seed=0):
    import zlib

    import numpy as np

    out = dict(_drawn_inputs(seed))
    spreads = {}
    factors = {}
    for name, (base, spread) in spreads.items():
        noise = np.random.default_rng([zlib.crc32(name.encode()), seed]).standard_normal(out[name].shape)
        drawn = base * np.exp(spread * noise) if base else spread * noise
        out[name] = __import__('jax').numpy.asarray(drawn.astype(out[name].dtype))
    for name, factor in factors.items():
        out[name] = (out[name] * factor).astype(out[name].dtype)
    return out
```

```python
from contextlib import ExitStack

import numpy as np
import concourse.bass as bass
from concourse import mybir

F32 = mybir.dt.float32
F32R = mybir.dt.float32r
ACT = mybir.ActivationFunctionType
ALU = mybir.AluOpType
AX = mybir.AxisListType

P = 128
D = 1024
DT = D // P
SEQ, DEC_B, DEC_T = 256, 8, 4
NS = DEC_B * DEC_T
T = SEQ + NS
GRP = T // DEC_T
PG = SEQ // DEC_T
PAD = DEC_T + 2
CHUNK = 128
EPS = 1e-6
DEPTH = 2
N_MEM, XH, XD = 256, 4, 256
DFF = 2816
FT = DFF // P
RH, RDK, RDV = 4, 256, 512
PAST = 2048
CREDIT = 4
CW = 256


class Gemm:

    def __init__(self, name, w, ks, first, cols=None):
        self.name, self.w, self.ks, self.first = name, w, ks, first
        self.nk = len(ks)
        self.per = 2 * self.nk
        self.ncols = w.shape[1]
        self.steps = self.ncols // (2 * CW)
        self.chunks = self.steps * self.per
        self.cols = cols or (lambda i, half: 2 * CW * i + CW * half)
        self.next = None

    def rows(self, idx):
        kc = idx % self.nk
        return sum(self.ks[:kc]), self.ks[kc]


def build(nc, a, outs):
    (y_prompt, y_sample, mem_k, mem_v, sc_prompt, sc_sample, sgu_v, ret_prompt, ret_sample,
     fc_prompt, fc_sample) = outs

    order = []

    def gemm(name, w, ks=(8,), cols=None):
        g = Gemm(name, w, list(ks), sum(x.chunks for x in order), cols)
        if order:
            order[-1].next = g
        order.append(g)
        return g

    G = {}
    for l in range(DEPTH):
        if l % 2 == 0:
            G["in", l] = gemm("in_even", a["w_in_even"][l // 2])
            G["out", l] = gemm("out_even", a["w_out_even"][l // 2])
        else:
            G["in", l] = gemm("in_odd", a["w_in_odd"][l // 2])
            G["out", l] = gemm("out_odd", a["w_out_odd"][l // 2], (8, 8))
        G["k", l] = gemm("xk", a["w_xk"][l])
        G["v", l] = gemm("xv", a["w_xv"][l])
        G["q", l] = gemm("xq", a["w_xq"][l])
        G["o", l] = gemm("xo", a["w_xo"][l])
        G["up", l] = gemm("up", a["w_ffn_up"][l], (8,), lambda i, half: CW * i + DFF * half)
        G["down", l] = gemm("down", a["w_ffn_down"][l], (6, 6, 5, 5))

    ctx = ExitStack()
    with ctx:
        def sb(name, shape, dt=F32, scope=ctx):
            return scope.enter_context(nc.sbuf_tensor(name, [P] + shape, dt))

        def sem(name):
            return ctx.enter_context(nc.semaphore(name))

        raw = sb("raw", [4, 8, CW])
        wh = sb("wh", [2, 8, CW], F32R)
        wl = sb("wl", [2, 8, CW], F32R)
        xT = sb("xT", [DT, T])
        hh = sb("hh", [DT, T], F32R)
        hl = sb("hl", [DT, T], F32R)
        mT = sb("mT", [DT, T])
        sq = sb("sq", [DT, T])
        acc = sb("acc", [2, T])
        root = sb("root", [T])
        rstd = sb("rstd", [T])
        ident = sb("ident", [P])
        ones = sb("ones", [P])
        rowsn = sb("rowsn", [P])
        gT = sb("gT", [P])
        cwT = sb("cwT", [3 * P])
        small = sb("small", [64])

        ev = ExitStack()
        xn = sb("xn", [3, D], F32, ev)
        cwn = sb("cwn", [3, P], F32, ev)
        u = sb("u", [4, T], F32, ev)
        v = sb("v", [4, T], F32, ev)
        bg = sb("bg", [4, T], F32, ev)
        cg = sb("cg", [4, T], F32, ev)
        zz = sb("zz", [4, GRP, PAD], F32, ev)
        cv = sb("cv", [4, T], F32, ev)
        av = sb("av", [4, T], F32, ev)
        vnat = sb("vnat", [3, 4 * P], F32, ev)
        sgn = sb("sgn", [4, P], F32, ev)
        sgT = sb("sgT", [4, P], F32, ev)
        bdn = sb("bdn", [4, NS], F32, ev)
        bdT = sb("bdT", [4, NS], F32, ev)
        sbias = sb("sbias", [4, T], F32, ev)
        scn = sb("scn", [P], F32, ev)
        scT = sb("scT", [64], F32, ev)
        sctP = sb("sctP", [4, 2], F32, ev)
        sctS = sb("sctS", [4, 16], F32, ev)
        sco = sb("sco", [2, P], F32, ev)
        ev.close()

        at = ExitStack()
        kt = ExitStack()
        kT = sb("kT", [DT, N_MEM], F32, kt)
        kt.close()
        pB = sb("pB", [2, DEC_B * (P + DEC_T)], F32, at)
        vN = sb("vN", [2, D], F32, at)
        ring = sb("ring", [4, 2, D], F32, at)
        qB = sb("qB", [DT, DEC_B * (NS + DEC_T)], F32, at)
        pS = sb("pS", [N_MEM], F32, at)
        kv = ExitStack()
        memn = sb("memn", [2, D], F32, kv)
        kN = sb("kN", [2, D], F32, kv)
        mh = sb("mh", [DT, N_MEM], F32R, kv)
        ml = sb("ml", [DT, N_MEM], F32R, kv)
        kv.close()
        pr = sb("pr", [8, N_MEM], F32, at)
        prT = sb("prT", [4, 2, SEQ], F32, at)
        kTb = sb("kTb", [2, DT, N_MEM], F32, at)
        at.close()

        ff = ExitStack()
        aH = sb("aH", [FT, T], F32R, ff)
        aL = sb("aL", [FT, T], F32R, ff)
        zb = sb("zb", [4, GRP, PAD], F32, ff)
        cb = sb("cb", [4, T], F32, ff)
        ge = sb("ge", [2, T], F32, ff)
        pd = sb("pd", [2, T], F32, ff)
        stn = sb("stn", [6, P], F32, ff)
        stT = sb("stT", [2 * FT, 16], F32, ff)
        tlS = sb("tlS", [48, 16], F32, ff)
        tlP = sb("tlP", [2 * FT, 2], F32, ff)
        tlo = sb("tlo", [7, P], F32, ff)
        ff.close()

        od = ExitStack()
        gS = sb("gS", [16, T], F32, od)
        h2h = sb("h2h", [8, T], F32R, od)
        h2l = sb("h2l", [8, T], F32R, od)
        V4 = sb("V4", [RH * RDV], F32R, od)
        rp = ExitStack()
        vR = sb("vR", [2, RH * RDV], F32, rp)
        kR = sb("kR", [2, RH * RDK], F32, rp)
        cR = sb("cR", [8 * P + 4], F32, rp)
        gp = ExitStack()
        cs = sb("cs", [2, T], F32, gp)
        rA = sb("rA", [2, T], F32, gp)
        rB = sb("rB", [2, T], F32, gp)
        vt = sb("vt", [4, T], F32, gp)
        vhS = sb("vhS", [4, NS], F32R, gp)
        v4T = sb("v4T", [4, 4, NS], F32, gp)
        gp.close()
        S1 = sb("S1", [2, RDV], F32, rp)
        S2 = sb("S2", [2, RDV], F32, rp)
        scr = sb("scr", [2, P], F32, rp)
        qd = sb("qd", [2, P], F32, rp)
        rn = sb("rn", [RDV], F32, rp)
        rg = sb("rg", [4, P], F32, rp)
        rp.close()
        rs = ExitStack()
        QM = sb("QM", [8, DEC_B, NS], F32, rs)
        K4 = sb("K4", [RH * RDK], F32, rs)
        K4m = sb("K4m", [2, RH * RDK], F32R, rs)
        kd = sb("kd", [8, NS], F32, rs)
        kdh = sb("kdh", [8, NS], F32R, rs)
        k4T = sb("k4T", [8, 4, NS], F32, rs)
        SR = sb("SR", [2, 4, RDV], F32, rs)
        cS = sb("cS", [12 * NS + 8], F32, rs)
        scS = sb("scS", [4, NS], F32, rs)
        rnS = sb("rnS", [RDV], F32, rs)
        rgS = sb("rgS", [4, NS], F32, rs)
        rs.close()
        od.close()
        fin = ExitStack()
        yn = sb("yn", [3, D], F32, fin)
        fin.close()

        ps = ctx.enter_context(nc.psum_tensor("ps", [P, 8, 512], F32))
        BN = 4

        landed = [sem("landed_even"), sem("landed_odd")]
        hi_ready, lo_ready, w_used = sem("hi_ready"), sem("lo_ready"), sem("w_used")
        sq_ready, sum_step, ssq_ready = sem("sq_ready"), sem("sum_step"), sem("ssq_ready")
        root_ready, rstd_ready = sem("root_ready"), sem("rstd_ready")
        m_ready, scaled, x_ready = sem("m_ready"), sem("scaled"), sem("x_ready")
        hn_ready, h_hi, h_lo = sem("hn_ready"), sem("h_hi"), sem("h_lo")
        S = {}

        def s(name):
            if name not in S:
                S[name] = sem(name)
            return S[name]

        def load_weights(e, g):
            w = g.w

            def step(i):
                cols = [g.cols(i, half) for half in range(2)]
                even = ((i + g.first // 2) % 2) * 2
                if not isinstance(i, int):
                    cols, even = [e.snap(x) for x in cols], e.snap(even)
                for idx in range(g.per):
                    c = g.first + idx
                    r0, kn = g.rows(idx)
                    src = w[r0 * P:(r0 + kn) * P, bass.ds(cols[idx // g.nk], CW)] \
                        .rearrange("(t p) n -> p t n", p=P)
                    e.wait_ge(lo_ready, i * g.per + c - 4 + CREDIT + 1)
                    e.wait_ge(landed[c % 2], i * (8 * g.per) + 16 * (c // 2) + 16)
                    slot = even + c % 2 if g.per % 4 else c % 4
                    e.dma_start(raw[:, slot, 0:kn, :], src).then_inc(landed[c % 2], 16)
            if g.steps > 2:
                with e.Fori(0, g.steps) as i:
                    step(i)
            else:
                for i in range(g.steps):
                    step(i)

        def target(g, i, idx, last):
            idx += 2
            if idx < g.per:
                return g, i, idx
            if not last:
                return g, i + 1, idx - g.per
            return (g.next, 0, idx - g.per) if g.next else (None, 0, 0)

        def split(e, g, i, idx, high):
            if g is None:
                return
            c, kn = g.first + idx, g.rows(idx)[1]
            slot = (((i + c // 2) % 2) * 2 + c % 2) if g.per % 4 else c % 4
            src = raw[:, slot, 0:kn, :]
            if high:
                e.wait_ge(landed[c % 2], i * (8 * g.per) + 16 * (c // 2) + 32)
                e.wait_ge(w_used, i * (2 * g.per) + 2 * c - 2 + CREDIT)
                e.activation(wh[:, c % 2, 0:kn, :], src, ACT.Copy).then_inc(hi_ready, 1)
            else:
                e.wait_ge(hi_ready, i * g.per + c + 1)
                e.tensor_tensor(wl[:, c % 2, 0:kn, :], src, wh[:, c % 2, 0:kn, :].bitcast(F32),
                                ALU.subtract).then_inc(lo_ready, 1)

        def tiles_ready(e, g, i, half, j):
            c = g.first + half * g.nk + g.nk - 1
            e.wait_ge(w_used, i * (2 * g.per) + 2 * c + j + 1 + CREDIT)

        def run(e, g, high, evac, i0=0, i1=None):
            i1 = g.steps if i1 is None else i1

            def step(i, last):
                for idx in range(g.per):
                    split(e, *target(g, i, idx, last), high)
                    if idx % g.nk == g.nk - 1:
                        evac(i, idx // g.nk)
            end = i1 == g.steps
            n = i1 - end
            if n - i0 > 1:
                with e.Fori(i0, n) as i:
                    step(i, False)
            elif n - i0 == 1:
                step(i0, False)
            if end:
                step(g.steps - 1, True)

        def products(pe, g, pairs, freed, base, natural=False, i0=0, i1=None, drained=False):
            i1 = g.steps if i1 is None else i1

            def step(i):
                for idx in range(g.per):
                    half, kc = divmod(idx, g.nk)
                    r0, kn = g.rows(idx)
                    c = g.first + idx
                    pe.wait_ge(lo_ready, i * g.per + c + 1 + CREDIT)
                    for j in range(2):
                        t = 2 * half + j
                        if kc == 0 and not drained:
                            pe.wait_ge(freed, i * 4 + base + t - 3)
                        for k in range(kn):
                            xh, xl = pairs(r0 + k)
                            if natural:
                                w_h, w_l = wh[:, c % 2, k, :], wl[:, c % 2, k, :]
                                cut = slice(j * P, (j + 1) * P)
                                trio = ((xh[:, cut], w_h), (xl[:, cut], w_h), (xh[:, cut], w_l))
                                out = ps[:, t, 0:CW]
                            else:
                                w_h = wh[:, c % 2, k, j * P:(j + 1) * P]
                                w_l = wl[:, c % 2, k, j * P:(j + 1) * P]
                                trio = ((w_h, xh), (w_h, xl), (w_l, xh))
                                out = ps[:, t, 0:T]
                            for n, (lhsT, rhs) in enumerate(trio):
                                mm = pe.matmul(out, lhsT, rhs, start=(kc == 0 and k == 0 and n == 0),
                                               stop=(kc == g.nk - 1 and k == kn - 1 and n == 2))
                        mm.then_inc(w_used, 1)
            if i1 - i0 > 1:
                with pe.Fori(i0, i1) as i:
                    step(i)
            else:
                step(i0)

        def square_x(act, n):
            q = n // 2
            if n:
                act.wait_ge(sum_step, 3 * n)
            for t in range(DT):
                act.wait_ge(x_ready, DT * q + t + 1)
                act.activation(sq[:, t, :], xT[:, t, :], ACT.Square).then_inc(sq_ready, 1)

        def sums(dve, n):
            if n:
                dve.wait_ge(ssq_ready, n)
            dve.wait_ge(sq_ready, CREDIT + 8 * n + 4)
            dve.tensor_tensor(acc[:], sq[:, 0:2, :], sq[:, 2:4, :], ALU.add).then_inc(sum_step, 1)
            for r in (1, 2):
                dve.wait_ge(sq_ready, CREDIT + 8 * n + 4 + 2 * r)
                dve.wait_ge(sum_step, 3 * n + r)
                dve.tensor_tensor(acc[:], acc[:], sq[:, 2 * r + 2:2 * r + 4, :],
                                  ALU.add).then_inc(sum_step, 1)

        def ssq(pe, n):
            pe.wait_ge(sum_step, 3 * n + 3)
            if n:
                pe.wait_ge(root_ready, n)
            pe.matmul(ps[:, BN, 0:T], ones[:], acc[:, 0, :], start=True, stop=False)
            pe.matmul(ps[:, BN, 0:T], ones[:], acc[:, 1, :], start=False,
                      stop=True).then_inc(ssq_ready, 1)

        def take_root(act, n):
            act.wait_ge(ssq_ready, n + 1)
            act.activation(root[:], ps[:, BN, 0:T], ACT.Sqrt, bias=eps_col, scale=1.0 / D).then_inc(root_ready, 1)

        def invert(dve, n):
            dve.wait_ge(root_ready, n + 1)
            dve.reciprocal(rstd[:], root[:]).then_inc(rstd_ready, 1)

        def add_branch(dve, q):
            dve.wait_ge(rstd_ready, 2 * q + 2)
            gain = gcol("post", q)
            for t in range(DT + 1):
                if t < DT:
                    dve.wait_ge(m_ready, DT * q + t + 1)
                    dve.tensor_tensor(mT[:, t, :], mT[:, t, :], rstd[:], ALU.mult).then_inc(scaled, 1)
                if t > 0:
                    dve.wait_ge(scaled, DT * q + t)
                    dve.scalar_tensor_tensor(out=xT[:, t - 1, :], in0=mT[:, t - 1, :], scalar=gain(t - 1),
                                             in1=xT[:, t - 1, :], op0=ALU.mult,
                                             op1=ALU.add).then_inc(x_ready, 1)

        def normed_x(dve, q):
            dve.wait_ge(rstd_ready, 2 * q + 1)
            for t in range(DT):
                dve.tensor_tensor(mT[:, t, :], xT[:, t, :], rstd[:], ALU.mult).then_inc(hn_ready, 1)

        def normed_high(act, q):
            gain = gcol("pre", q)
            for t in range(DT):
                act.wait_ge(hn_ready, DT * q + t + 1)
                act.activation(hh[:, t, :], mT[:, t, :], ACT.Copy, scale=gain(t)).then_inc(h_hi, 1)

        def normed_low(dve, q):
            gain = gcol("pre", q)
            for t in range(DT):
                dve.wait_ge(h_hi, DT * q + t + 1)
                dve.scalar_tensor_tensor(out=hl[:, t, :], in0=mT[:, t, :], scalar=gain(t),
                                         in1=hh[:, t, :].bitcast(F32), op0=ALU.mult,
                                         op1=ALU.subtract).then_inc(h_lo, 1)

        GROWS = {("pre", 0): 0, ("post", 0): 8, ("pre", 1): 16, ("post", 1): 24, ("pre", 2): 32,
                 ("post", 2): 40}
        GB = 56

        def gcol(kind, q):
            l, br = divmod(q, 3)
            return lambda t: gT[:, GB * l + GROWS[kind, br] + t:GB * l + GROWS[kind, br] + t + 1]

        def memgain(l, t):
            return gT[:, GB * l + 48 + t:GB * l + 49 + t]

        def vgain(t):
            return gT[:, 112 + t:113 + t]

        def sctap(j, t):
            return gT[:, 116 + 4 * j + t:117 + 4 * j + t]

        def ftap(l, j, t):
            c = (3 * l + j) * 2 * FT
            return cwT[:, bass.ds(t + c, 1)]

        eps_col = small[:, 0:1]

        def pre_pe(pe, q):
            ssq(pe, 2 * q)

        def pre_act(act, q):
            square_x(act, 2 * q)
            take_root(act, 2 * q)
            normed_high(act, q)

        def pre_dve(dve, q):
            sums(dve, 2 * q)
            invert(dve, 2 * q)
            normed_x(dve, q)
            normed_low(dve, q)

        def post_act(act, q):
            take_root(act, 2 * q + 1)

        def post_dve(dve, q):
            sums(dve, 2 * q + 1)
            invert(dve, 2 * q + 1)
            add_branch(dve, q)

        def branch_out_act(act, g, q):
            n = 2 * q + 1

            def evac(i, half):
                if not isinstance(i, int) or i == 0:
                    act.wait_ge(sum_step, 3 * n)
                for j in range(2):
                    t = i * 4 + 2 * half + j
                    tiles_ready(act, g, i, half, j)
                    src = ps[:, 2 * half + j, 0:T]
                    act.activation(mT[:, t, :], src, ACT.Copy).then_inc(m_ready, 1)
                    act.activation(sq[:, t, :], src, ACT.Square).then_inc(sq_ready, 1)
            run(act, g, True, evac)

        def nothing(i, half):
            pass

        def normed(k):
            return hh[:, k, :], hl[:, k, :]

        def groups(x):
            return x.rearrange("p (g t) -> p g t", t=DEC_T)

        def transpose(pe, out, x, rows=P):
            return pe.transpose(out, x, ident[0:rows, 0:rows])

        L = range(DEPTH)
        stores = [0]
        dmat = lambda h: cR[:, h * P:(h + 1) * P]
        qdec = lambda h: cR[:, (4 + h) * P:(5 + h) * P]
        kdec = lambda h: cR[:, 8 * P + h:8 * P + h + 1]
        dmatS = cS[:, 0:4 * NS].rearrange("p (h i) -> p h i", h=RH)
        qdecS = cS[:, 4 * NS:8 * NS].rearrange("p (h o i) -> p h o i", h=RH, o=1)
        kdecS = cS[:, 8 * NS:12 * NS].rearrange("p (h o i) -> p h o i", h=RH, o=1)
        maskS = lambda b: cS[:, 12 * NS + b:12 * NS + b + 1]
        gam = [float(np.float32(1) - np.float32(2.0) ** np.float32(-5 - h)) for h in range(RH)]
        UNITS = [(h, c) for h in range(RH) for c in range(2)]

        def pool_retention(pool, store):
            pool.wait_ge(s("a_free"), 1)
            pool.dma_start(cs[:], a["c_rope"]).then_inc(s("rope_in"), 16)
            pool.dma_start(cR[:], a["c_ret"]).then_inc(s("ret_in"), 16)
            for h in range(RH):
                pool.wait_ge(s("S2_ready"), 2 * h + 2)
                store(ret_prompt[0, 0, h].rearrange("(t p) e -> p t e", p=P), S2[:])
                pool.wait_ge(s("stored"), stores[0])
                pool.sem_inc(s("S2_stored"), 1)
            pool.wait_ge(s("rg_lo"), 8)
            pool.dma_start(cS[:], a["c_retS"]).then_inc(s("retS_in"), 16)
            for n in range(2 * DEC_B):
                b, hp = divmod(n, 2)
                if n >= 2:
                    pool.wait_ge(s("SR_new"), 4 * (n - 1))
                    pb = (n - 2) // 2
                    store(ret_sample[0, pb, 2 * hp:2 * hp + 2].rearrange("h (t p) e -> p (h t) e", p=P), SR[:, hp])
                    pool.wait_ge(s("stored"), stores[0])
                pool.dma_start(SR[:, hp], a["state_retention"][0, b, 2 * hp:2 * hp + 2]
                               .rearrange("h (t p) e -> p (h t) e", p=P)).then_inc(s(f"SR_in{hp}"), 16)
            for hp in range(2):
                pool.wait_ge(s("SR_new"), 4 * (15 + hp))
                store(ret_sample[0, DEC_B - 1, 2 * hp:2 * hp + 2].rearrange("h (t p) e -> p (h t) e", p=P), SR[:, hp])
            pool.wait_ge(s("stored"), stores[0])

        def act_even(act, l):
            g = G["in", l]

            def evac(i, half):
                for j in range(2):
                    t = 2 * half + j
                    tiles_ready(act, g, i, half, j)
                    src = ps[:, t, 0:T]
                    if i == 0:
                        act.activation(u[:, t, :], src, ACT.Gelu_apprx_tanh).then_inc(s("in_even"), 1)
                    elif i == 1:
                        act.activation(v[:, t, :], src, ACT.Gelu_apprx_tanh).then_inc(s("in_even"), 1)
                    elif i == 2:
                        act.activation(bg[:, t, :], src, ACT.Copy).then_inc(s("in_even"), 1)
                    elif i == 3:
                        act.activation(cg[:, t, :], src, ACT.Copy).then_inc(s("in_even"), 1)
                    if i == 1:
                        act.wait_ge(s("in_even"), CREDIT + 4 + t + 1)
                        act.wait_ge(sum_step, 3)
                        act.activation(sq[:, t, :], v[:, t, :], ACT.Square).then_inc(s("v_sq"), 1)
            for i in range(g.steps):
                for idx in range(2):
                    split(act, *target(g, i, idx, i == g.steps - 1), True)
                    if i < 4:
                        evac(i, idx)
            act.wait_ge(s("v_ssq"), 1)
            act.activation(root[:], ps[:, BN, 0:T], ACT.Sqrt, bias=eps_col, scale=1.0 / (4 * P)).then_inc(s("v_root"), 1)
            for c in range(3):
                n = P if c < 2 else NS
                act.wait_ge(s("v_ps"), c + 1)
                act.activation(vnat[0:n, c, :], ps[0:n, 5 + c, :], ACT.Copy).then_inc(s("vnat_ready"), 1)
            act.wait_ge(s("sct_ps"), 1)
            act.activation(sco[0:8, 0, :], ps[0:8, BN, 0:P], ACT.Copy)
            act.activation(sco[0:64, 1, :], ps[0:64, BN, P:2 * P], ACT.Copy).then_inc(s("sco_ready"), 1)
            for t in range(4):
                act.wait_ge(s("b_ready"), t + 1)
                act.activation(hh[:, 4 + t, :], cv[:, t, :], ACT.Copy).then_inc(s("even_hi"), 1)
            for t in range(4):
                act.wait_ge(s("av_ready"), t + 1)
                act.activation(hh[:, t, :], av[:, t, :], ACT.Copy).then_inc(s("even_hi"), 1)

        def act_odd(act, l):
            g = G["in", l]

            def keep(i, half):
                for j in range(2):
                    t = 2 * half + j
                    tiles_ready(act, g, i, half, j)
                    act.wait_ge(s("vt_used"), i * 4 + 2 * half + 2)
                    act.activation(vt[:, t, :], ps[:, t, 0:T], ACT.Copy).then_inc(s("z_ready"), 1)

            def gates(i, half):
                for j in range(2):
                    t = 2 * half + j
                    tiles_ready(act, g, i, half, j)
                    act.activation(gS[:, i * 4 + (t - 32), :], ps[:, t, 0:T], ACT.Silu).then_inc(s("z_ready"), 1)
            run(act, g, True, keep, 0, 4)
            for i in range(4, 8):
                for idx in range(2):
                    split(act, *target(g, i, idx, False), True)
                    keep(i, idx)
                for t in range(4):
                    e = 4 * (i - 4) + t
                    act.wait_ge(s("vR_ps"), e + 1)
                    act.activation(vR[:, :, e * P:(e + 1) * P],
                                   ps[:, 5 + e % 2, 0:2 * P].rearrange("p (c e) -> p c e", c=2), ACT.Copy)
                    act.activation(V4[:, e * P:(e + 1) * P], ps[:, 5 + e % 2, 2 * P:3 * P], ACT.Copy).then_inc(s("vR_ready"), 1)
            run(act, g, True, gates, 8, 12)
            act.wait_ge(s("ret_in"), 16)
            for n in range(4):
                c, hf = divmod(n, 2)
                act.wait_ge(s("kR_ps"), n + 1)
                for k in range(2):
                    h = 2 * hf + k
                    ins = act.activation(kR[:, c, h * RDK:(h + 1) * RDK], ps[:, 5 + n % 2, k * RDK:(k + 1) * RDK],
                                         ACT.Copy, scale=kdec(h))
                ins.then_inc(s("kR_ready"), 1)
            for n, (h, c) in enumerate(UNITS):
                if c == 0:
                    act.wait_ge(s("S_ps"), 2 * n + 2)
                    if h:
                        act.wait_ge(s("S1_used"), h)
                    act.activation(S1[:], ps[:, 0:2, :], ACT.Copy).then_inc(s("S1_ready"), 1)
                act.wait_ge(s("ro_mv"), n + 1)
                act.activation(small[:, 12:13], small[:, 11:12], ACT.Sqrt, bias=eps_col).then_inc(s("ro_root"), 1)
                act.wait_ge(s("rg_ready"), n + 1)
                (dh, o) = (hh, 4 * h) if h < 2 else (h2h, 4 * h - 8)
                act.activation(dh[:, o:o + 4, c * CHUNK:(c + 1) * CHUNK], rg[:], ACT.Copy).then_inc(s("rg_hi"), 1)
            act.wait_ge(s("k4T_full"), 1)
            for r in range(2):
                act.wait_ge(s("k4_ps"), r + 1)
                act.activation(K4[:, 512 * r:512 * r + 512], ps[:, 5 + r, :], ACT.Copy).then_inc(s("K4_ready"), 1)
            act.wait_ge(s("K4_ready"), 2)
            for b in range(DEC_B):
                if b >= 2:
                    act.wait_ge(s("SU_ps"), 8 * (b - 1))
                act.activation(K4m[:, b % 2, :], K4[:], ACT.Copy, scale=maskS(b)).then_inc(s("K4m_ready"), 1)
            for h in range(RH):
                act.wait_ge(s("ro_mv"), 8 + h + 1)
                act.activation(small[0:NS, 12:13], small[0:NS, 11:12], ACT.Sqrt, bias=eps_col[0:NS]).then_inc(s("ro_root"), 1)
                act.wait_ge(s("rg_ready"), 8 + h + 1)
                (dh, o) = (hh, 4 * h) if h < 2 else (h2h, 4 * h - 8)
                act.activation(dh[:, o:o + 4, SEQ:T], rgS[:], ACT.Copy).then_inc(s("rg_hi"), 1)

        KBANKS = (4, 6, 7)

        def own_tokens(row, width):
            return row.rearrange("p (b x) -> p b x", b=DEC_B)[:, :, 0:width].rearrange("p b (h i) -> p b h i", i=NS)[:, :, :, 0:DEC_T]

        def sample_heads(x):
            return x[:, :, SEQ:T].rearrange("p (h d) i -> p h d i", d=2)

        def take_keys(e, l, b, act):
            for r in (0, 2) if act else (1, 3):
                n = 4 * b + r
                e.wait_ge(s("kTb_ps"), 32 * l + n + 1)
                if b >= 2:
                    e.wait_ge(s("sS_mm"), 8 * l + b - 1)
                src = ps[:, KBANKS[n % 3], :].rearrange("p (t m) -> p t m", t=2)
                if act:
                    e.activation(kTb[:, b % 2, 2 * r:2 * r + 2, :], src, ACT.Copy).then_inc(s("kTb_act"), 1)
                else:
                    e.tensor_copy(kTb[:, b % 2, 2 * r:2 * r + 2, :], src).then_inc(s("kTb_dve"), 1)

        def act_attention(act, l):
            def exps(h):
                act.wait_ge(s("nm_ready"), 5 * l + h + 1)
                for n in (2 * h, 2 * h + 1):
                    act.activation(pr[:, n, :], ps[:, h, (n % 2) * N_MEM:(n % 2 + 1) * N_MEM], ACT.Exp, scale=XD ** -0.5,
                                   bias=small[:, 24 + n:25 + n], accum_out=small[:, 32 + n:33 + n]).then_inc(s("exp_ready"), 1)

            def turned(h):
                act.wait_ge(s("pT_ps"), 5 * l + h + 1)
                act.activation(prT[:, h, :, :], ps[:, h, :].rearrange("p (m t) -> p m t", m=2), ACT.Copy).then_inc(s("pT_ready"), 1)

            def heads_high(h):
                act.wait_ge(s("o_ps"), 5 * l + h + 1)
                act.activation(hh[:, 2 * h:2 * h + 2, 0:SEQ], ps[:, h, :].rearrange("p (d t) -> p d t", d=2), ACT.Copy).then_inc(s("oh_hi"), 1)

            for b in range(DEC_B):
                take_keys(act, l, b, True)
                if b < 4:
                    exps(b)
                if b == 5:
                    act.wait_ge(s("kv_stored"), 32 * l + 32)
                if b >= 5:
                    turned(b - 5)
                if b >= 6:
                    heads_high(b - 6)
            turned(3)
            act.wait_ge(s("nm_ready"), 5 * l + 5)
            act.activation(pS[:], ps[:, 5, 0:N_MEM], ACT.Exp, scale=XD ** -0.5, bias=small[:, 49:50],
                           accum_out=small[:, 50:51]).then_inc(s("exp_ready"), 1)
            heads_high(2)
            act.wait_ge(s("pT_ps"), 5 * l + 5)
            act.wait_ge(s("own_zero"), 2 * l + 2)
            act.activation(own_tokens(pB[:, 0, :], P), ps[:, 7, 0:P].rearrange("p (h b t) -> p b h t", h=XH, t=DEC_T),
                           ACT.Copy).then_inc(s("pB_act"), 1)
            heads_high(3)
            act.wait_ge(s("oS_mm"), 8 * l + 8)
            act.activation(pS[:], ps[:, 6, 0:XD], ACT.Copy).then_inc(s("oS_out"), 1)
            act.wait_ge(s("o_ps"), 5 * l + 5)
            act.activation(sample_heads(hh), ps[:, 7, 0:XD].rearrange("p (d h i) -> p h d i", d=2, h=XH),
                           ACT.Copy).then_inc(s("oh_hi"), 1)

        def dve_even(dve, l):
            g = G["in", l]
            for i in range(g.steps):
                for idx in range(2):
                    split(dve, *target(g, i, idx, i == g.steps - 1), False)
                    if i < 4:
                        continue
                    for j in range(2):
                        t = 2 * idx + j
                        tiles_ready(dve, g, i, idx, j)
                        dve.wait_ge(s("in_even"), CREDIT + 12 + t + 1)
                        dve.tensor_tensor(zz[:, t, :, 2:PAD], groups(cg[:, t, :]), groups(ps[:, t, 0:T]),
                                          ALU.mult).then_inc(s("zz_main"), 1)
            dve.wait_ge(s("v_sq"), 4)
            dve.wait_ge(ssq_ready, 1)
            dve.tensor_tensor(acc[:], sq[:, 0:2, :], sq[:, 2:4, :], ALU.add).then_inc(s("v_sum"), 1)
            dve.wait_ge(s("zz_main"), 4)
            dve.tensor_copy(zz[:, :, 1:PG, 0:2], zz[:, :, 0:PG - 1, 4:6]).then_inc(s("zz_pre"), 1)
            dve.tensor_copy(zz[:, :, PG:, 0:2], scT[:].rearrange("p (t b j) -> p t b j", t=4, j=2)).then_inc(s("zz_pre"), 1)
            dve.tensor_copy(sctP[:], zz[:, :, PG - 1, 4:6]).then_inc(s("sct_ready"), 1)
            dve.tensor_copy(sctS[:].rearrange("p t (b j) -> p t b j", j=2), zz[:, :, PG:, 4:6]).then_inc(s("sct_ready"), 1)
            dve.wait_ge(s("v_root"), 1)
            dve.reciprocal(rstd[:], root[:]).then_inc(s("v_inv"), 1)
            dve.wait_ge(s("v_inv"), 1)
            for t in range(4):
                dve.scalar_tensor_tensor(out=v[:, t, :], in0=v[:, t, :], scalar=vgain(t), in1=rstd[:],
                                         op0=ALU.mult, op1=ALU.mult).then_inc(s("vn_ready"), 1)
            dve.wait_ge(s("zz_pre"), 2)
            for t in range(4):
                dve.tensor_scalar(groups(cv[:, t, :]), zz[:, t, :, 2:PAD], sctap(2, t), None, ALU.mult).then_inc(s("cv"), 1)
            for j in (1, 0):
                for t in range(4):
                    dve.wait_ge(s("cv"), 4 * (2 - j) + t)
                    dve.wait_ge(s("cv"), 4 * (1 - j) + t + 1)
                    dve.scalar_tensor_tensor(out=groups(cv[:, t, :]), in0=zz[:, t, :, j:j + 4], scalar=sctap(j, t),
                                             in1=groups(cv[:, t, :]), op0=ALU.mult, op1=ALU.add).then_inc(s("cv"), 1)
            for t in range(4):
                dve.wait_ge(s("cv"), 8 + t + 1)
                dve.tensor_tensor(cv[:, t, :], cv[:, t, :], bg[:, t, :], ALU.mult).then_inc(s("b_ready"), 1)
            for t in range(4):
                dve.wait_ge(s("even_hi"), t + 1)
                dve.tensor_tensor(hl[:, 4 + t, :], cv[:, t, :], hh[:, 4 + t, :].bitcast(F32), ALU.subtract).then_inc(s("even_lo"), 1)
            dve.wait_ge(s("bias_in"), 160)
            for t in range(4):
                dve.wait_ge(s("mix_ps"), t + 1)
                dve.tensor_tensor(av[:, t, :], sbias[:, t, :], ps[:, t, 0:T], ALU.add).then_inc(s("mixed"), 1)
            for t in range(4):
                dve.wait_ge(s("mixed"), t + 1)
                dve.tensor_tensor(av[:, t, :], av[:, t, :], u[:, t, :], ALU.mult).then_inc(s("av_ready"), 1)
            for t in range(4):
                dve.wait_ge(s("even_hi"), 4 + t + 1)
                dve.tensor_tensor(hl[:, t, :], av[:, t, :], hh[:, t, :].bitcast(F32), ALU.subtract).then_inc(s("even_lo"), 1)

        def dve_odd(dve, l):
            g = G["in", l]

            def turn(dst, i0):
                def evac(i, half):
                    if half == 0:
                        dve.wait_ge(s("rope_in"), 16)
                    pair = vt[:, 2 * half:2 * half + 2, :]
                    dve.wait_ge(s("z_ready"), CREDIT + i * 4 + 2 * half + 2)
                    dve.wait_ge(s("turned"), i * 4 + 2 * half + CREDIT)
                    dve.tensor_tensor(rA[:], pair, cs[:, 0, :].unsqueeze(1).to_broadcast([P, 2, T]), ALU.mult).then_inc(s("vt_used"), 1)
                    dve.tensor_tensor(rB[:], pair, cs[:, 1, :].unsqueeze(1).to_broadcast([P, 2, T]), ALU.mult).then_inc(s("vt_used"), 1)
                    dve.wait_ge(s("vt_used"), CREDIT + i * 4 + 2 * half + 2)
                    dve.tensor_tensor(dst[:, i * 4 + (2 * half - 4 * i0), :], rA[:, 0, :], rB[:, 1, :], ALU.subtract).then_inc(s("turned"), 1)
                    dve.tensor_tensor(dst[:, i * 4 + (2 * half + 1 - 4 * i0), :], rB[:, 0, :], rA[:, 1, :], ALU.add).then_inc(s("turned"), 1)
                return evac
            run(dve, g, False, turn(mT, 0), 0, 2)
            run(dve, g, False, turn(sq, 2), 2, 4)
            for i in range(4, 8):
                for idx in range(2):
                    split(dve, *target(g, i, idx, False), False)
                    for j in range(2):
                        t = 2 * idx + j
                        e = 4 * (i - 4) + t
                        dve.wait_ge(s("z_ready"), CREDIT + 4 * i + t + 1)
                        if e >= 4:
                            dve.wait_ge(s("vR_ps"), e - 3)
                        dve.tensor_copy(vhS[:, t, :], vt[:, t, SEQ:T]).then_inc(s("vh"), 1)
                        dve.wait_ge(s("vh"), e + 1)
                        both = vhS[:, t, :].bitcast(F32).unsqueeze(1).to_broadcast([P, 2, NS])
                        dve.tensor_copy(v4T[:, t, 0:4:2, :], both)
                        dve.tensor_tensor(v4T[:, t, 1:4:2, :], vt[:, t, SEQ:T].unsqueeze(1).to_broadcast([P, 2, NS]),
                                          both, ALU.subtract).then_inc(s("v4T_ready"), 1)
            run(dve, g, False, nothing, 8, 12)
            for n, (h, c) in enumerate(UNITS):
                tok = slice(c * CHUNK, (c + 1) * CHUNK)
                dve.wait_ge(s("rs_ps"), n + 1)
                if n >= 2:
                    dve.wait_ge(s("ro_ps"), n - 1)
                dve.tensor_tensor(scr[:, n % 2, :], dmat(h), ps[:, 5, 0:P], ALU.mult).then_inc(s("rs_ready"), 1)
                if c == 1:
                    dve.tensor_tensor(qd[:], mT[:, 2 * h:2 * h + 2, tok],
                                      qdec(h).unsqueeze(1).to_broadcast([P, 2, P]), ALU.mult).then_inc(s("qd_ready"), 1)
                dve.wait_ge(s("ro_ps"), n + 1)
                head_norm(dve, n, ps[:, 6, :], rn[:], P)
                if c == 1:
                    for dt in range(2):
                        dve.wait_ge(s("S_ps"), 2 * n + dt + 1)
                        if h and dt == 0:
                            dve.wait_ge(s("S2_stored"), h)
                        dve.scalar_tensor_tensor(out=S2[:, dt, :], in0=S1[:, dt, :], scalar=gL(h, CHUNK),
                                                 in1=ps[:, dt, :], op0=ALU.mult, op1=ALU.add).then_inc(s("S2_ready"), 1)
                    dve.wait_ge(s("S2_ready"), 2 * h + 2)
                    dve.sem_inc(s("S1_used"), 1)
                dve.wait_ge(s("rT_ps"), n + 1)
                dve.tensor_tensor(rg[:], gS[:, 4 * h:4 * h + 4, tok], ps[:, 7, :].rearrange("p (e i) -> p e i", e=4),
                                  ALU.mult).then_inc(s("rg_ready"), 1)
                (dh, dl, o) = (hh, hl, 4 * h) if h < 2 else (h2h, h2l, 4 * h - 8)
                dve.wait_ge(s("rg_hi"), n + 1)
                dve.tensor_tensor(dl[:, o:o + 4, tok], rg[:], dh[:, o:o + 4, tok].bitcast(F32), ALU.subtract).then_inc(s("rg_lo"), 1)
            kS = sq[:, :, SEQ:T]
            four = lambda x: x.rearrange("p (h d) i -> p h d i", d=2)
            dve.wait_ge(s("retS_in"), 16)
            dve.tensor_copy(k4T[:, :, 0:2, :], kS.unsqueeze(2).to_broadcast([P, 8, 2, NS])).then_inc(s("kdup"), 1)
            dve.memset(QM[:], 0.0).then_inc(s("QM_step"), 1)
            dve.tensor_tensor(four(kd[:]), four(mT[:, :, SEQ:T]), qdecS.to_broadcast([P, RH, 2, NS]), ALU.mult).then_inc(s("QM_step"), 1)
            dve.wait_ge(s("QM_step"), 2)
            for b in range(DEC_B):
                r = slice(DEC_T * b, DEC_T * b + DEC_T)
                dve.tensor_copy(QM[:, :, b, r], kd[:, :, r]).then_inc(s("QM_step"), 1)
            dve.wait_ge(s("scS_ps"), 1)
            dve.tensor_tensor(scS[0:64], dmatS[0:64], ps[0:64, 5, 0:4 * NS].rearrange("p (h i) -> p h i", h=RH),
                              ALU.mult).then_inc(s("scS_ready"), 1)
            dve.wait_ge(s("QM_step"), 10)
            dve.tensor_tensor(four(kd[:]), four(kS), kdecS.to_broadcast([P, RH, 2, NS]), ALU.mult).then_inc(s("kd"), 1)
            dve.wait_ge(s("kd"), 1)
            dve.tensor_copy(kdh[:], kd[:]).then_inc(s("kd"), 1)
            dve.wait_ge(s("kd"), 2)
            kh2 = kdh[:].bitcast(F32).unsqueeze(2).to_broadcast([P, 8, 2, NS])
            dve.tensor_copy(k4T[:, :, 0:2, :], kh2)
            dve.tensor_tensor(k4T[:, :, 2:4, :], kd[:].unsqueeze(2).to_broadcast([P, 8, 2, NS]), kh2,
                              ALU.subtract).then_inc(s("k4T_full"), 1)
            for b in range(DEC_B):
                for k in range(8):
                    n = 8 * b + k
                    h = k // 2
                    dve.wait_ge(s("SU_ps"), n + 1)
                    dve.scalar_tensor_tensor(out=SR[:, k // 4, k % 4, :], in0=SR[:, k // 4, k % 4, :], scalar=gL(h, DEC_T),
                                             in1=ps[:, 4 + k % 4, :], op0=ALU.mult, op1=ALU.add).then_inc(s("SR_new"), 1)
            for h in range(RH):
                if h == 0:
                    dve.wait_ge(s("oS_all"), 1)
                head_norm(dve, 8 + h, ps[0:NS, h, :], rnS[0:NS], NS)
                dve.wait_ge(s("rT_ps"), 8 + h + 1)
                dve.tensor_tensor(rgS[:], gS[:, 4 * h:4 * h + 4, SEQ:T], ps[:, 7, 0:4 * NS].rearrange("p (e i) -> p e i", e=4),
                                  ALU.mult).then_inc(s("rg_ready"), 1)
                (dh, dl, o) = (hh, hl, 4 * h) if h < 2 else (h2h, h2l, 4 * h - 8)
                dve.wait_ge(s("rg_hi"), 8 + h + 1)
                dve.tensor_tensor(dl[:, o:o + 4, SEQ:T], rgS[:], dh[:, o:o + 4, SEQ:T].bitcast(F32), ALU.subtract).then_inc(s("rg_lo"), 1)

        def gL(h, n):
            return float(np.exp(np.float32(np.log1p(-np.exp2(np.float32(-5 - h)))) * np.float32(n)))

        def head_norm(dve, n, src, dst, rows):
            dve.bn_stats(small[0:rows, 52:58], src).then_inc(s("ro_st"), 1)
            dve.wait_ge(s("ro_st"), n + 1)
            dve.bn_aggr(small[0:rows, 10:12], small[0:rows, 52:58]).then_inc(s("ro_mv"), 1)
            dve.wait_ge(s("ro_root"), n + 1)
            dve.reciprocal(small[0:rows, 13:14], small[0:rows, 12:13]).then_inc(s("ro_inv"), 1)
            dve.wait_ge(s("ro_inv"), n + 1)
            if n:
                dve.wait_ge(s("rT_ps"), n)
            dve.tensor_scalar(dst, src, small[0:rows, 10:11], small[0:rows, 13:14], ALU.subtract,
                              ALU.mult).then_inc(s("rn_ready"), 1)

        def dve_attention(dve, l):
            def maxima(h):
                if h == XH:
                    dve.wait_ge(s("sS_mm"), 8 * l + 8)
                    src, mx, nm = ps[:, 5, 0:N_MEM], small[:, 48:49], small[:, 49:50]
                else:
                    dve.wait_ge(s("sc_ps"), 4 * l + h + 1)
                    src = ps[:, h, :].rearrange("p (t m) -> p t m", t=2)
                    mx, nm = small[:, 16 + 2 * h:18 + 2 * h], small[:, 24 + 2 * h:26 + 2 * h]
                dve.tensor_reduce(mx, src, AX.X, ALU.max).then_inc(s("mx_ready"), 1)
                dve.wait_ge(s("mx_ready"), 5 * l + h + 1)
                dve.tensor_scalar(nm, mx, -XD ** -0.5, None, ALU.mult).then_inc(s("nm_ready"), 1)

            def shares(h):
                sample = h == XH
                dve.wait_ge(s("exp_ready"), 9 * l + (9 if sample else 2 * h + 2))
                sm, rc = (small[:, 50:51], small[:, 51:52]) if sample else \
                    (small[:, 32 + 2 * h:34 + 2 * h], small[:, 40 + 2 * h:42 + 2 * h])
                dve.reciprocal(rc, sm).then_inc(s("rc_ready"), 1)
                dve.wait_ge(s("rc_ready"), 5 * l + h + 1)
                if sample:
                    dve.tensor_scalar(pS[:], pS[:], rc, None, ALU.mult).then_inc(s("p_ready"), 1)
                    return
                for n in (2 * h, 2 * h + 1):
                    dve.tensor_scalar(pr[:, n, :], pr[:, n, :], small[:, 40 + n:41 + n], None, ALU.mult).then_inc(s("p_ready"), 1)

            def heads_low(h):
                dve.wait_ge(s("oh_hi"), 5 * l + h + 1)
                dve.tensor_tensor(hl[:, 2 * h:2 * h + 2, 0:SEQ], ps[:, h, :].rearrange("p (d t) -> p d t", d=2),
                                  hh[:, 2 * h:2 * h + 2, 0:SEQ].bitcast(F32), ALU.subtract).then_inc(s("oh_lo"), 1)

            dve.wait_ge(s("q_ready"), CREDIT + 8 * l + 8)
            dve.wait_ge(s("own_zero"), 2 * l + 1)
            dve.tensor_copy(qB[:].rearrange("p k (b x) -> p k b x", b=DEC_B)[:, :, :, 0:DEC_T],
                            mT[:, :, SEQ:T].rearrange("p k (b t) -> p k b t", t=DEC_T)).then_inc(s("own_dve"), 1)
            for b in range(DEC_B):
                take_keys(dve, l, b, False)
                if b < 4:
                    maxima(b)
                if 1 <= b <= 4:
                    shares(b - 1)
                if b == 7:
                    heads_low(0)
            maxima(XH)
            heads_low(1)
            shares(XH)
            heads_low(2)
            dve.wait_ge(s("pB_act"), l + 1)
            dve.tensor_copy(own_tokens(pB[:, 1, :], P), ps[:, 7, P:2 * P].rearrange("p (h b t) -> p b h t", h=XH, t=DEC_T)) \
                .then_inc(s("own_dve"), 1)
            heads_low(3)
            dve.wait_ge(s("oh_hi"), 5 * l + 5)
            dve.tensor_tensor(sample_heads(hl), ps[:, 7, 0:XD].rearrange("p (d h i) -> p h d i", d=2, h=XH),
                              sample_heads(hh).bitcast(F32), ALU.subtract).then_inc(s("oh_lo"), 1)

        def pe_even(pe, l):
            g = G["in", l]
            products(pe, g, normed, s("in_even"), CREDIT, i1=4)
            pe.wait_ge(s("in_even"), CREDIT + 16)
            products(pe, g, normed, s("in_even"), CREDIT, i0=4, i1=5, drained=True)
            pe.wait_ge(s("v_sum"), 1)
            pe.wait_ge(root_ready, 1)
            pe.matmul(ps[:, BN, 0:T], ones[:], acc[:, 0, :], start=True, stop=False)
            pe.matmul(ps[:, BN, 0:T], ones[:], acc[:, 1, :], start=False, stop=True).then_inc(s("v_ssq"), 1)
            pe.wait_ge(s("sct_ready"), 2)
            pe.wait_ge(s("v_root"), 1)
            transpose(pe, ps[0:8, BN, 0:P], sctP[:].rearrange("p t j -> p (t j)"))
            transpose(pe, ps[0:64, BN, P:2 * P], sctS[:].rearrange("p t r -> p (t r)")).then_inc(s("sct_ps"), 1)
            pe.wait_ge(s("gT_ready"), 5)
            pe.wait_ge(s("vn_ready"), 4)
            for c in range(3):
                n = P if c < 2 else NS
                for t in range(4):
                    tr = transpose(pe, ps[0:n, 5 + c, t * P:(t + 1) * P], v[:, t, c * P:c * P + n])
                tr.then_inc(s("v_ps"), 1)
            pe.wait_ge(s("vnat_ready"), 3)
            pe.wait_ge(s("zz_main"), 4)
            for t in range(4):
                cut = slice(t * P, (t + 1) * P)
                for c in range(2):
                    pe.matmul(ps[:, t, c * CHUNK:(c + 1) * CHUNK], vnat[:, c, cut], sgT[:, t, :], start=True, stop=True)
                pe.matmul(ps[:, t, SEQ:T], vnat[0:NS, 2, cut], bdT[0:NS, t, :], start=True, stop=True).then_inc(s("mix_ps"), 1)
            pe.wait_ge(s("even_lo"), 8)
            pe.sem_inc(s("even_act"), 1)

        def pe_odd(pe, l):
            g = G["in", l]
            products(pe, g, normed, s("z_ready"), CREDIT, i0=0, i1=4)
            for i in range(4, 8):
                products(pe, g, normed, s("z_ready"), CREDIT, i0=i, i1=i + 1)
                for t in range(4):
                    e = 4 * (i - 4) + t
                    pe.wait_ge(s("v4T_ready"), e + 1)
                    if e >= 2:
                        pe.wait_ge(s("vR_ready"), e - 1)
                    bank = 5 + e % 2
                    for c in range(2):
                        transpose(pe, ps[:, bank, c * P:(c + 1) * P], vt[:, t, c * P:(c + 1) * P])
                    transpose(pe, ps[:, bank, 2 * P:3 * P], v4T[:, t, :, :].rearrange("p r i -> p (r i)")).then_inc(s("vR_ps"), 1)
                pe.wait_ge(s("vR_ps"), 4 * (i - 4) + 4)
                pe.sem_inc(s("vt_used"), 4)
            products(pe, g, normed, s("z_ready"), CREDIT, i0=8, i1=12)
            pe.wait_ge(s("vR_ready"), 16)
            pe.wait_ge(s("turned"), CREDIT + 16)
            for n in range(4):
                c, hf = divmod(n, 2)
                if n >= 2:
                    pe.wait_ge(s("kR_ready"), n - 1)
                for k in range(4):
                    t = 4 * hf + k
                    tr = transpose(pe, ps[:, 5 + n % 2, k * P:(k + 1) * P], sq[:, t, c * P:(c + 1) * P])
                tr.then_inc(s("kR_ps"), 1)
            pe.wait_ge(s("z_ready"), CREDIT + 48)
            pe.wait_ge(s("kR_ready"), 4)
            for n, (h, c) in enumerate(UNITS):
                tok = slice(c * CHUNK, (c + 1) * CHUNK)
                if n:
                    pe.wait_ge(s("rs_ready"), n)
                for dt in range(2):
                    mm = pe.matmul(ps[:, 5, 0:P], sq[:, 2 * h + dt, tok], mT[:, 2 * h + dt, tok], start=dt == 0, stop=dt == 1)
                mm.then_inc(s("rs_ps"), 1)
                if n:
                    if c == 1:
                        pe.wait_ge(s("S1_ready"), h + 1)
                    else:
                        pe.wait_ge(s("S2_ready"), 2 * h)
                for dt in range(2):
                    pe.matmul(ps[:, dt, :], kR[:, c, h * RDK + dt * P:h * RDK + dt * P + P], vR[:, c, h * RDV:(h + 1) * RDV],
                              start=True, stop=True).then_inc(s("S_ps"), 1)
                pe.wait_ge(s("rs_ready"), n + 1)
                if n:
                    pe.wait_ge(s("rn_ready"), n)
                mm = pe.matmul(ps[:, 6, :], scr[:, n % 2, :], vR[:, c, h * RDV:(h + 1) * RDV], start=True, stop=c == 0)
                if c == 1:
                    pe.wait_ge(s("qd_ready"), h + 1)
                    pe.wait_ge(s("S1_ready"), h + 1)
                    for dt in range(2):
                        mm = pe.matmul(ps[:, 6, :], qd[:, dt, :], S1[:, dt, :], start=False, stop=dt == 1)
                mm.then_inc(s("ro_ps"), 1)
                pe.wait_ge(s("rn_ready"), n + 1)
                if n:
                    pe.wait_ge(s("rg_ready"), n)
                for k in range(4):
                    tr = transpose(pe, ps[:, 7, k * P:(k + 1) * P], rn[:, k * P:(k + 1) * P])
                tr.then_inc(s("rT_ps"), 1)
            pe.wait_ge(s("kdup"), 1)
            pe.wait_ge(s("rg_ready"), 8)
            for h in range(RH):
                for dt in range(2):
                    mm = pe.matmul(ps[0:64, 5, h * NS:(h + 1) * NS], k4T[:, 2 * h + dt, 0:2, :].rearrange("p r i -> p (r i)"),
                                   mT[:, 2 * h + dt, SEQ:T], start=dt == 0, stop=dt == 1)
            mm.then_inc(s("scS_ps"), 1)
            pe.wait_ge(s("scS_ready"), 1)
            pe.wait_ge(s("S2_ready"), 8)
            for h in range(RH):
                pe.matmul(ps[0:NS, h, :], scS[0:64, h, :], V4[0:64, h * RDV:(h + 1) * RDV].bitcast(F32),
                          start=True, stop=False, skip_group_check=True)
            pe.wait_ge(s("k4T_full"), 1)
            for r in range(2):
                for k in range(4):
                    tr = transpose(pe, ps[:, 5 + r, k * P:(k + 1) * P], k4T[:, 4 * r + k, :, :].rearrange("p r i -> p (r i)"))
                tr.then_inc(s("k4_ps"), 1)
            pe.wait_ge(s("K4_ready"), 2)
            for b in range(DEC_B):
                for k in range(8):
                    h, dt = divmod(k, 2)
                    n = 8 * b + k
                    if k % 4 == 0:
                        pe.wait_ge(s(f"SR_in{k // 4}"), 16 * b + 16)
                    pe.matmul(ps[0:NS, h, :], QM[:, k, b, :], SR[:, k // 4, k % 4, :], start=False,
                              stop=b == DEC_B - 1 and dt == 1, skip_group_check=True)
                    if k == 0:
                        pe.wait_ge(s("K4m_ready"), b + 1)
                    if n >= 4:
                        pe.wait_ge(s("SR_new"), n - 3)
                    pe.matmul(ps[:, 4 + k % 4, :], K4m[:, b % 2, k * P:(k + 1) * P], V4[:, h * RDV:(h + 1) * RDV],
                              start=True, stop=True).then_inc(s("SU_ps"), 1)
            pe.wait_ge(s("SU_ps"), 64)
            pe.sem_inc(s("oS_all"), 1)
            for h in range(RH):
                pe.wait_ge(s("rn_ready"), 8 + h + 1)
                if h == 0:
                    pe.wait_ge(s("SR_new"), 64)
                else:
                    pe.wait_ge(s("rg_ready"), 8 + h)
                for k in range(4):
                    tr = transpose(pe, ps[:, 7, k * NS:(k + 1) * NS], rnS[0:NS, k * P:(k + 1) * P], NS)
                tr.then_inc(s("rT_ps"), 1)
            pe.wait_ge(s("rg_lo"), 12)
            pe.sem_inc(s("odd_act"), 1)

        def pe_attention(pe, l):
            def keys(b):
                pe.wait_ge(s(f"cache{b % 4}"), 64 * l + 16 * (b // 4) + 16)
                for r in range(4):
                    n = 4 * b + r
                    if n >= 3:
                        pe.wait_ge(s("kTb_dve" if (n - 3) % 2 else "kTb_act"), 16 * l + (n - 3) // 2 + 1)
                    for t in (2 * r, 2 * r + 1):
                        for m in range(2):
                            c = (t % 2) * N_MEM + m * P
                            tr = transpose(pe, ps[:, KBANKS[n % 3], c:c + P], ring[:, b % 4, m, t * P:(t + 1) * P])
                    tr.then_inc(s("kTb_ps"), 1)

            def sample_scores(b):
                pe.wait_ge(s("kTb_act"), 16 * l + 2 * b + 2)
                pe.wait_ge(s("kTb_dve"), 16 * l + 2 * b + 2)
                if b == 0:
                    pe.wait_ge(s("own_dve"), 2 * l + 1)
                for t in range(DT):
                    h = t // 2
                    mm = pe.matmul(ps[h * NS:(h + 1) * NS, 5, 0:N_MEM], qB[:, t, b * NS:(b + 1) * NS], kTb[:, b % 2, t, :],
                                   start=b == 0 and t % 2 == 0, stop=b == DEC_B - 1 and t % 2 == 1,
                                   skip_group_check=True, tile_position=(0, h * NS))
                mm.then_inc(s("sS_mm"), 1)

            def turn_shares(h):
                pe.wait_ge(s("p_ready"), 9 * l + 2 * h + 2)
                for m in range(2):
                    for tt in range(2):
                        tr = transpose(pe, ps[:, h, m * SEQ + tt * P:m * SEQ + (tt + 1) * P], pr[:, 2 * h + tt, m * P:(m + 1) * P])
                tr.then_inc(s("pT_ps"), 1)

            def values(h):
                pe.wait_ge(s("pT_ready"), 4 * l + h + 1)
                for dt in range(2):
                    for m in range(2):
                        mm = pe.matmul(ps[:, h, dt * SEQ:(dt + 1) * SEQ], vN[:, m, (2 * h + dt) * P:(2 * h + dt + 1) * P],
                                       prT[:, h, m, :], start=m == 0, stop=m == 1)
                mm.then_inc(s("o_ps"), 1)

            pe.wait_ge(s("q_ready"), CREDIT + 8 * l + 8)
            pe.wait_ge(s("kT_ready"), 4 * l + 4)
            for h in range(XH):
                for tt in range(2):
                    for dt in range(2):
                        mm = pe.matmul(ps[:, h, tt * N_MEM:(tt + 1) * N_MEM], mT[:, 2 * h + dt, tt * P:(tt + 1) * P],
                                       kT[:, 2 * h + dt, :], start=dt == 0, stop=dt == 1)
                mm.then_inc(s("sc_ps"), 1)
            keys(0)
            for b in range(DEC_B):
                if b < DEC_B - 1:
                    keys(b + 1)
                if b >= 4:
                    turn_shares(b - 4)
                sample_scores(b)
                if b >= 5:
                    values(b - 5)
            values(3)
            pe.wait_ge(s("p_ready"), 9 * l + 9)
            for m in range(2):
                tr = transpose(pe, ps[:, 7, m * P:(m + 1) * P], pS[:, m * P:(m + 1) * P])
            tr.then_inc(s("pT_ps"), 1)
            pe.wait_ge(s("pB_act"), l + 1)
            pe.wait_ge(s("own_dve"), 2 * l + 2)
            for b in range(DEC_B):
                n = DEC_B + b
                pe.wait_ge(s(f"cache{n % 4}"), 64 * l + 16 * (n // 4) + 16)
                for h in range(XH):
                    for m in range(2):
                        mm = pe.matmul(ps[h * NS:(h + 1) * NS, 6, 0:XD], pB[:, m, b * P + h * NS:b * P + (h + 1) * NS],
                                       ring[:, n % 4, m, h * XD:(h + 1) * XD], start=b == 0 and m == 0,
                                       stop=b == DEC_B - 1 and m == 1, skip_group_check=True, tile_position=(0, h * NS))
                mm.then_inc(s("oS_mm"), 1)
            pe.wait_ge(s("oS_out"), l + 1)
            for d in range(2):
                tr = transpose(pe, ps[:, 7, d * P:(d + 1) * P], pS[:, d * P:(d + 1) * P])
            tr.then_inc(s("o_ps"), 1)

        block = ctx.enter_context(nc.Block())

        @block.sync
        def _(sp):
            sp.dma_start(ident[:], a["c_ident"]).then_inc(s("ident_in"), 16)
            sp.dma_start(xn[:, 0:2, :], a["x_prompt"][0].rearrange("(r p) d -> p r d", p=P)).then_inc(s("x_in"), 16)
            sp.dma_start(xn[0:NS, 2, :], a["x_sample"].rearrange("b t d -> (b t) d")).then_inc(s("x_in"), 16)
            rows = 0
            for l in L:
                for name in ("norm_mix_pre", "norm_mix_post", "norm_x_pre", "norm_x_post",
                             "norm_ffn_pre", "norm_ffn_post", "norm_mem"):
                    sp.dma_start(rowsn[rows:rows + DT, :], a[name][l].rearrange("(t p) -> t p", p=P)).then_inc(s("gain_in"), 16)
                    rows += DT
            sp.dma_start(rowsn[rows:rows + 4, :], a["sgu_vnorm"][0].rearrange("(t p) -> t p", p=P)).then_inc(s("gain_in"), 16)
            for j in range(3):
                sp.dma_start(rowsn[rows + 4 + 4 * j:rows + 8 + 4 * j, :],
                             a["conv_short"][0, j].rearrange("(t p) -> t p", p=P)).then_inc(s("gain_in"), 16)
            sp.sem_inc(landed[0], 16)
            sp.sem_inc(landed[1], 16)
            for g in order:
                load_weights(sp, g)

        @block.gpsimd
        def _(pool):
            stores[0] = 0

            def store(dst, src):
                pool.dma_start(dst, src).then_inc(s("stored"), 16)
                stores[0] += 16

            cf = a["conv_ffn"].rearrange("l j (t p) -> (l j t) p", p=P)
            pool.dma_start(cwn[:, 0:2, :], cf[0:2 * P].rearrange("(r p) c -> p r c", p=P)).then_inc(s("taps_in"), 16)
            pool.dma_start(cwn[0:8, 2, :], cf[2 * P:2 * P + 8]).then_inc(s("taps_in"), 16)
            pool.dma_start(sgn[:], a["sgu_w"][0].rearrange("g t s -> t g s")).then_inc(s("sgu_in"), 16)
            pool.memset(bdn[0:NS], 0.0).then_inc(s("bd_zero"), 1)
            pool.wait_ge(s("bd_zero"), 1)
            for b in range(DEC_B):
                r = slice(DEC_T * b, DEC_T * b + DEC_T)
                pool.dma_start(bdn[r, :, r], a["sgu_w"][0, :, 0:DEC_T, 0:DEC_T]
                               .rearrange("g t s -> t g s")).then_inc(s("bd_in"), 16)
            bias = a["sgu_b"][0]
            for c in range(SEQ // CHUNK):
                pool.dma_start(sbias[:, :, c * CHUNK:(c + 1) * CHUNK],
                               bias.unsqueeze(0).to_broadcast([P, 4, CHUNK])).then_inc(s("bias_in"), 16)
            for b in range(DEC_B):
                c = SEQ + DEC_T * b
                pool.dma_start(sbias[:, :, c:c + DEC_T],
                               bias[:, 0:DEC_T].unsqueeze(0).to_broadcast([P, 4, DEC_T])).then_inc(s("bias_in"), 16)
            pool.dma_start(scn[0:64, :], a["state_shortconv"][0].rearrange("b j (t p) -> t (b j) p", p=P)).then_inc(s("sc_in"), 16)
            pool.wait_ge(s("sgu_in"), 16)
            pool.affine_select(out=sgn[:], in_=sgn[:], compare_op=ALU.is_ge, fill=0.0, base=0,
                               pattern=[[0, 4], [-1, P]], channel_multiplier=1).then_inc(s("sgu_masked"), 1)
            pool.wait_ge(s("bd_in"), 16 * DEC_B)
            pool.affine_select(out=bdn[0:NS], in_=bdn[0:NS], compare_op=ALU.is_ge, fill=0.0, base=0,
                               pattern=[[0, 4], [-1, NS]], channel_multiplier=1).then_inc(s("sgu_masked"), 1)

            pool.wait_ge(s("vnat_ready"), 3)
            store(sgu_v[0].rearrange("b t d -> (b t) d"), vnat[0:NS, 2, :])
            pool.wait_ge(s("sco_ready"), 1)
            store(sc_prompt[0, 0].rearrange("j (t p) -> t j p", p=P), sco[0:8, 0, :])
            store(sc_sample[0].rearrange("b j (t p) -> t (b j) p", p=P), sco[0:64, 1, :])

            for l in L:
                q = 3 * l + 1
                if l == 1:
                    pool_retention(pool, store)
                if l == 0:
                    pool.wait_ge(s("stored"), stores[0])
                    pool.wait_ge(s("even_act"), 1)
                else:
                    pool.wait_ge(w_used, CREDIT + 2 * (G["out", l].first + G["out", l].chunks))
                pool.dma_start(memn[:], a["mem_prompt"][0].rearrange("(r p) d -> p r d", p=P)).then_inc(s("mem_in"), 16)

                def cache(n):
                    src = a["cache_mem_k" if n < DEC_B else "cache_mem_v"][l, n % DEC_B]
                    pool.dma_start(ring[:, n % 4], src.rearrange("(r p) h d -> p r (h d)", p=P)).then_inc(s(f"cache{n % 4}"), 16)
                for n in range(4):
                    cache(n)
                pool.memset(qB[:], 0.0).then_inc(s("own_zero"), 1)
                pool.wait_ge(s("k_nat"), CREDIT + 8 * l + 8)
                pool.dma_start(mem_k[l, 0].rearrange("(r p) h d -> p r (h d)", p=P), kN[:]).then_inc(s("kv_stored"), 16)
                pool.wait_ge(s("v_nat"), CREDIT + 8 * l + 8)
                pool.dma_start(mem_v[l, 0].rearrange("(r p) h d -> p r (h d)", p=P), vN[:]).then_inc(s("kv_stored"), 16)
                pool.wait_ge(s("sc_ps"), 4 * l + 4)
                pool.memset(pB[:], 0.0).then_inc(s("own_zero"), 1)
                for n in range(4, 2 * DEC_B):
                    if n - 4 < DEC_B:
                        pool.wait_ge(s("kTb_ps"), 32 * l + 4 * (n - 3))
                    else:
                        pool.wait_ge(s("oS_mm"), 8 * l + n - 4 - DEC_B + 1)
                    cache(n)

                pool.wait_ge(s("oh_lo"), 5 * l + 5)
                pool.wait_ge(s("oS_mm"), 8 * l + 8)
                pool.wait_ge(s("kv_stored"), 32 * l + 32)
                rows = a["state_ffn_conv"][l].rearrange("b j (t p) -> t (b j) p", p=P)
                for r in range(6):
                    n = min(8, 2 * FT - 8 * r)
                    pool.dma_start(stn[0:16 * n, r, :], rows[8 * r:8 * r + n]).then_inc(s("st_in"), 16)
                pool.wait_ge(s("stT_ready"), 2 * l + 2)

                def prefix(i):
                    for t in range(4):
                        pool.wait_ge(s("conv_done"), i * 4 + 44 * l + t + 1)
                        pool.tensor_copy(zb[:, t, PG:, 0:2],
                                         stT[:, bass.ds(i * 2 + FT * (t // 2) + t % 2, 1), :]
                                         .rearrange("p o (b j) -> p (o b) j", j=2)).then_inc(s("prefix"), 1)
                    for t in range(4):
                        pool.wait_ge(s("conv_in"), CREDIT + i * 4 + 44 * l + t + 1)
                        col = i * 2 + FT * (t // 2) + t % 2
                        pool.tensor_copy(tlS[:, bass.ds(col, 1), :].rearrange("p o (b j) -> p (o b) j", j=2),
                                         zb[:, t, PG:, 4:6])
                        pool.tensor_copy(tlP[:, bass.ds(col, 1), :], zb[:, t, PG - 1:PG, 4:6]).then_inc(s("tails"), 1)
                with pool.Fori(0, G["up", l].steps) as i:
                    prefix(i)
                pool.wait_ge(s("tlo_ready"), 2 * l + 2)
                rows = fc_sample[l].rearrange("b j (t p) -> t (b j) p", p=P)
                for r in range(6):
                    n = min(8, 2 * FT - 8 * r)
                    store(rows[8 * r:8 * r + n], tlo[0:16 * n, r, :])
                store(fc_prompt[l, 0].rearrange("j (t p) -> t j p", p=P), tlo[0:4 * FT, 6, :])
                pool.wait_ge(s("stored"), stores[0])

            pool.wait_ge(s("y_ready"), 3)
            store(y_prompt[0].rearrange("(r p) d -> p r d", p=P), yn[:, 0:2, :])
            store(y_sample.rearrange("b t d -> (b t) d"), yn[0:NS, 2, :])
            pool.wait_ge(s("stored"), stores[0])

        @block.scalar
        def _(act):
            for t in range(DT):
                act.wait_ge(s("xt_ps"), t + 1)
                act.activation(xT[:, t, :], ps[:, t % 4, 0:T], ACT.Copy).then_inc(x_ready, 1)
            act.wait_ge(s("const_ps"), 1)
            act.activation(gT[:], ps[:, 5, 0:P], ACT.Copy).then_inc(s("gT_ready"), 1)
            act.wait_ge(s("const_ps"), 2)
            act.activation(cwT[:, 0:2 * P + 8], ps[:, 6, 0:2 * P + 8], ACT.Copy).then_inc(s("gT_ready"), 1)
            act.wait_ge(s("const_ps"), 3)
            act.activation(sgT[:], ps[:, 7, :].rearrange("p (g t) -> p g t", g=4), ACT.Copy).then_inc(s("gT_ready"), 1)
            act.wait_ge(s("const_ps"), 4)
            act.activation(bdT[0:NS], ps[0:NS, 5, 128:256].rearrange("p (g t) -> p g t", g=4), ACT.Copy).then_inc(s("gT_ready"), 1)
            act.activation(scT[:], ps[:, 5, 256:320], ACT.Copy).then_inc(s("gT_ready"), 1)
            act.wait_ge(s("eps_set"), 1)
            for c in range(2):
                split(act, order[0], 0, c, True)

            for l in L:
                q = 3 * l
                if l == 0:
                    act.wait_ge(s("gT_ready"), 1)
                pre_act(act, q)
                (act_even if l % 2 == 0 else act_odd)(act, l)
                branch_out_act(act, G["out", l], q)
                post_act(act, q)

                act.wait_ge(s("mem_in"), 16 * l + 16)
                for r in range(2):
                    act.activation(kN[:, r, :], memn[:, r, :], ACT.Square,
                                   accum_out=small[:, 1 + r:2 + r]).then_inc(s("mem_sq"), 1)
                act.wait_ge(s("mem_sq"), 2 * l + 2)
                act.activation(small[:, 3:5], small[:, 1:3], ACT.Sqrt, bias=eps_col, scale=1.0 / D).then_inc(s("mem_root"), 1)
                for t in range(DT):
                    act.wait_ge(s("memT_ps"), 4 * l + t // 2 + 1)
                    act.activation(mh[:, t, :], ps[:, 5 + t // 2 % 3, (t % 2) * N_MEM:(t % 2 + 1) * N_MEM],
                                   ACT.Copy, scale=memgain(l, t)).then_inc(s("mem_hi"), 1)
                for name, dst in (("k", kN), ("v", vN)):
                    def evac(i, half, g=G[name, l], dst=dst, name=name):
                        for j in range(2):
                            tiles_ready(act, g, i, half, j)
                            act.activation(dst[:, j, bass.ds(i * 2 * CW + half * CW, CW)],
                                           ps[:, 2 * half + j, 0:CW], ACT.Copy).then_inc(s(f"{name}_nat"), 1)
                    run(act, G[name, l], True, evac)
                    if name == "k":
                        pre_act(act, q + 1)
                for r in range(4):
                    act.wait_ge(s("kT_ps"), 4 * l + r + 1)
                    act.activation(kT[:, 2 * r:2 * r + 2, :],
                                   ps[:, 5 + r % 3, :].rearrange("p (t m) -> p t m", t=2), ACT.Copy).then_inc(s("kT_ready"), 1)

                def evac(i, half, g=G["q", l]):
                    if not isinstance(i, int) or i == 0:
                        act.wait_ge(h_lo, DT * (q + 2))
                    for j in range(2):
                        tiles_ready(act, g, i, half, j)
                        act.activation(mT[:, i * 4 + (2 * half + j), :], ps[:, 2 * half + j, 0:T],
                                       ACT.Copy).then_inc(s("q_ready"), 1)
                run(act, G["q", l], True, evac)
                act_attention(act, l)
                branch_out_act(act, G["o", l], q + 1)
                post_act(act, q + 1)

                act.wait_ge(s("kv_stored"), 32 * l + 32)
                pre_act(act, q + 2)
                for r in range(2):
                    act.wait_ge(s("stT_ps"), 2 * l + r + 1)
                    n = (32, 12)[r]
                    act.activation(stT[:, 32 * r:32 * r + n, :],
                                   ps[:, 5 + r, 0:16 * n].rearrange("p (t r) -> p t r", r=16), ACT.Copy).then_inc(s("stT_ready"), 1)

                def evac(i, half, g=G["up", l]):
                    for j in range(2):
                        t = 2 * half + j
                        tiles_ready(act, g, i, half, j)
                        act.wait_ge(s("conv_done"), i * 4 + 44 * l + t + 1)
                        act.wait_ge(s("tails"), i * 4 + 44 * l + t + 1)
                        act.wait_ge(s("prod"), i * 2 + 22 * l + 2)
                        src = groups(ps[:, t, 0:T])
                        act.activation(zb[:, t, :, 2:PAD], src, ACT.Copy)
                        act.activation(zb[:, t, 1:PG, 0:2], src[:, 0:PG - 1, 2:4], ACT.Copy)
                        act.activation(cb[:, t, :], ps[:, t, 0:T], ACT.Copy,
                                       scale=ftap(l, 2, i * 2 + FT * half + j)).then_inc(s("conv_in"), 1)
                    if half == 0:
                        return
                    for j in range(2):
                        act.wait_ge(s("conv_done"), CREDIT + i * 4 + 44 * l + j + 1)
                        act.activation(ge[:, j, :], cb[:, j, :], ACT.Gelu_apprx_tanh).then_inc(s("gelu"), 1)
                    for j in range(2):
                        act.wait_ge(s("prod"), i * 2 + 22 * l + j + 3)
                        act.activation(aH[:, i * 2 + j, :], pd[:, j, :], ACT.Copy).then_inc(s("a_hi"), 1)
                run(act, G["up", l], True, evac)
                for r in range(3):
                    act.wait_ge(s("tlo_ps"), 2 * l + min(r, 1) + 1)
                    if r == 0:
                        act.activation(tlo[:, 0:4, :], ps[:, 5, :].rearrange("p (r c) -> p r c", c=P), ACT.Copy)
                    elif r == 1:
                        act.activation(tlo[:, 4, :], ps[:, 6, 0:P], ACT.Copy)
                        act.activation(tlo[0:64, 5, :], ps[0:64, 6, P:2 * P], ACT.Copy).then_inc(s("tlo_ready"), 1)
                    else:
                        act.activation(tlo[0:4 * FT, 6, :], ps[0:4 * FT, 6, 2 * P:3 * P], ACT.Copy).then_inc(s("tlo_ready"), 1)
                branch_out_act(act, G["down", l], q + 2)
                post_act(act, q + 2)

            for r in range(3):
                n = P if r < 2 else NS
                for half in range(2):
                    act.wait_ge(s("y_ps"), 2 * r + half + 1)
                    ins = act.activation(yn[0:n, r, 512 * half:512 * half + 512], ps[0:n, 2 * (r % 2) + half, :], ACT.Copy)
                    ins.then_inc(s("y_out"), 1)
                act.wait_ge(s("y_out"), 2 * r + 2)
                act.sem_inc(s("y_ready"), 1)

        @block.vector
        def _(dve):
            dve.memset(ones[:], 1.0).then_inc(s("ones_set"), 1)
            dve.memset(small[:, 0:1], EPS).then_inc(s("eps_set"), 1)
            dve.memset(zz[:, :, 0, 0:2], 0.0).then_inc(s("zz_zero"), 1)
            dve.sem_inc(lo_ready, CREDIT)
            for c in range(2):
                split(dve, order[0], 0, c, False)
            for l in L:
                q = 3 * l
                if l == 0:
                    dve.wait_ge(s("gT_ready"), 5)
                pre_dve(dve, q)
                (dve_even if l % 2 == 0 else dve_odd)(dve, l)
                run(dve, G["out", l], False, nothing)
                post_dve(dve, q)

                dve.wait_ge(s("mem_root"), l + 1)
                dve.reciprocal(small[:, 5:7], small[:, 3:5]).then_inc(s("mem_inv"), 1)
                dve.wait_ge(s("mem_inv"), l + 1)
                for r in range(2):
                    dve.tensor_scalar(memn[:, r, :], memn[:, r, :], small[:, 5 + r:6 + r], None,
                                      ALU.mult).then_inc(s("mem_scaled"), 1)
                for t in range(DT):
                    dve.wait_ge(s("mem_hi"), 8 * l + 2 * (t // 2) + 2)
                    dve.scalar_tensor_tensor(out=ml[:, t, :], in0=ps[:, 5 + t // 2 % 3, (t % 2) * N_MEM:(t % 2 + 1) * N_MEM],
                                             scalar=memgain(l, t), in1=mh[:, t, :].bitcast(F32), op0=ALU.mult,
                                             op1=ALU.subtract).then_inc(s("mem_lo"), 1)
                run(dve, G["k", l], False, nothing)
                pre_dve(dve, q + 1)
                run(dve, G["v", l], False, nothing)
                run(dve, G["q", l], False, nothing)
                dve_attention(dve, l)
                run(dve, G["o", l], False, nothing)
                post_dve(dve, q + 1)

                pre_dve(dve, q + 2)
                dve.memset(zb[:, :, 0, 0:2], 0.0).then_inc(s("zb_zero"), 1)

                def evac(i, half):
                    for j in range(2):
                        t = 2 * half + j
                        tile = i * 2 + FT * half + j
                        if half == 0 and j == 0:
                            dve.wait_ge(s("zb_zero"), l + 1)
                        dve.wait_ge(s("conv_in"), CREDIT + i * 4 + 44 * l + t + 1)
                        dve.wait_ge(s("prefix"), i * 4 + 44 * l + t + 1)
                        dve.scalar_tensor_tensor(out=groups(cb[:, t, :]), in0=zb[:, t, :, 1:5], scalar=ftap(l, 1, tile),
                                                 in1=groups(cb[:, t, :]), op0=ALU.mult, op1=ALU.add).then_inc(s("conv_mid"), 1)
                    for j in range(2):
                        t = 2 * half + j
                        tile = i * 2 + FT * half + j
                        dve.wait_ge(s("conv_mid"), i * 4 + 44 * l + t + 1)
                        dve.scalar_tensor_tensor(out=groups(cb[:, t, :]), in0=zb[:, t, :, 0:4], scalar=ftap(l, 0, tile),
                                                 in1=groups(cb[:, t, :]), op0=ALU.mult, op1=ALU.add).then_inc(s("conv_done"), 1)
                    if half == 0:
                        return
                    for j in range(2):
                        dve.wait_ge(s("gelu"), i * 2 + 22 * l + j + 1)
                        dve.wait_ge(s("conv_done"), CREDIT + i * 4 + 44 * l + 3 + j)
                        dve.wait_ge(s("a_lo"), i * 2 + 22 * l + j + 1)
                        dve.tensor_tensor(pd[:, j, :], ge[:, j, :], cb[:, 2 + j, :], ALU.mult).then_inc(s("prod"), 1)
                    for j in range(2):
                        dve.wait_ge(s("a_hi"), i * 2 + 22 * l + j + 1)
                        dve.tensor_tensor(aL[:, i * 2 + j, :], pd[:, j, :], aH[:, i * 2 + j, :].bitcast(F32),
                                          ALU.subtract).then_inc(s("a_lo"), 1)
                run(dve, G["up", l], False, evac)
                run(dve, G["down", l], False, nothing)
                post_dve(dve, q + 2)

        @block.tensor
        def _(pe):
            for name in ("in_even", "q_ready", "k_nat", "v_nat", "z_ready"):
                pe.sem_inc(s(name), CREDIT)
            for name in ("conv_in", "conv_done", "tails", "vt_used", "turned"):
                pe.sem_inc(s(name), CREDIT)
            for name in ("prod", "a_lo"):
                pe.sem_inc(s(name), 2)
            pe.sem_inc(sq_ready, CREDIT)
            pe.sem_inc(w_used, CREDIT)
            pe.wait_ge(s("ident_in"), 16)
            pe.wait_ge(s("x_in"), 32)
            for t in range(DT):
                if t >= 4:
                    pe.wait_ge(x_ready, t - 3)
                for r in range(3):
                    n = P if r < 2 else NS
                    tr = transpose(pe, ps[:, t % 4, r * P:r * P + n], xn[0:n, r, t * P:(t + 1) * P], n)
                tr.then_inc(s("xt_ps"), 1)
            pe.wait_ge(s("gain_in"), 16 * 18)
            transpose(pe, ps[:, 5, 0:P], rowsn[:]).then_inc(s("const_ps"), 1)
            pe.wait_ge(s("taps_in"), 32)
            for r in range(3):
                n = P if r < 2 else 8
                tr = transpose(pe, ps[:, 6, r * P:r * P + n], cwn[0:n, r, :], n)
            tr.then_inc(s("const_ps"), 1)
            pe.wait_ge(s("sgu_masked"), 2)
            for g in range(4):
                tr = transpose(pe, ps[:, 7, g * P:(g + 1) * P], sgn[:, g, :])
            tr.then_inc(s("const_ps"), 1)
            pe.wait_ge(s("gT_ready"), 1)
            for g in range(4):
                transpose(pe, ps[0:NS, 5, P + g * NS:P + (g + 1) * NS], bdn[0:NS, g, :], NS)
            pe.wait_ge(s("sc_in"), 16)
            transpose(pe, ps[:, 5, 2 * P:2 * P + 64], scn[0:64, :], 64).then_inc(s("const_ps"), 1)
            pe.wait_ge(s("ones_set"), 1)

            for l in L:
                q = 3 * l
                pre_pe(pe, q)
                pe.wait_ge(h_lo, DT * (q + 1))
                if l == 0:
                    pe.wait_ge(x_ready, 8)
                (pe_even if l % 2 == 0 else pe_odd)(pe, l)
                if l % 2 == 0:
                    products(pe, G["out", l], normed, sq_ready, CREDIT + 8 * (2 * q + 1))
                else:
                    products(pe, G["out", l], lambda k: (hh[:, k, :], hl[:, k, :]) if k < 8 else
                             (h2h[:, k - 8, :], h2l[:, k - 8, :]), sq_ready, CREDIT + 8 * (2 * q + 1))
                ssq(pe, 2 * q + 1)

                pe.wait_ge(s("mem_scaled"), 2 * l + 2)
                for r in range(4):
                    if r == 3:
                        pe.wait_ge(s("mem_lo"), 8 * l + 2)
                    for t in (2 * r, 2 * r + 1):
                        for m in range(2):
                            c = (t % 2) * N_MEM + m * P
                            tr = transpose(pe, ps[:, 5 + r % 3, c:c + P], memn[:, m, t * P:(t + 1) * P])
                    tr.then_inc(s("memT_ps"), 1)
                pe.wait_ge(s("mem_lo"), 8 * l + 8)
                pe.wait_ge(sq_ready, CREDIT + 8 * (2 * q + 2))
                mem = lambda k: (mh[:, k, :], ml[:, k, :])
                products(pe, G["k", l], mem, s("k_nat"), CREDIT + 8 * l, natural=True)
                pre_pe(pe, q + 1)
                pe.wait_ge(s("k_nat"), CREDIT + 8 * l + 8)
                products(pe, G["v", l], mem, s("v_nat"), CREDIT + 8 * l, natural=True)
                for r in range(4):
                    if r == 3:
                        pe.wait_ge(s("kT_ready"), 4 * l + 1)
                    for t in (2 * r, 2 * r + 1):
                        for m in range(2):
                            c = (t % 2) * N_MEM + m * P
                            tr = transpose(pe, ps[:, 5 + r % 3, c:c + P], kN[:, m, t * P:(t + 1) * P])
                    tr.then_inc(s("kT_ps"), 1)

                pe.wait_ge(h_lo, DT * (q + 2))
                pe.wait_ge(s("v_nat"), CREDIT + 8 * l + 8)
                products(pe, G["q", l], normed, s("q_ready"), CREDIT + 8 * l)
                pe_attention(pe, l)
                pe.wait_ge(s("oh_lo"), 5 * l + 5)
                products(pe, G["o", l], normed, sq_ready, CREDIT + 8 * (2 * q + 3))
                ssq(pe, 2 * q + 3)

                for r in range(6):
                    n = min(8, 2 * FT - 8 * r) * 16
                    if r == 0:
                        pe.wait_ge(s("st_in"), 96 * l + 96)
                    tr = transpose(pe, ps[:, 5 + r // 4, (r % 4) * P:(r % 4) * P + n], stn[0:n, r, :], n)
                    if r in (3, 5):
                        tr.then_inc(s("stT_ps"), 1)
                pre_pe(pe, q + 2)
                pe.wait_ge(h_lo, DT * (q + 3))
                pe.wait_ge(sq_ready, CREDIT + 8 * (2 * q + 5))
                products(pe, G["up", l], normed, s("conv_in"), CREDIT + 44 * l)
                pe.wait_ge(s("a_lo"), 22 * l + 24)
                pe.wait_ge(s("tails"), CREDIT + 44 * l + 44)
                for r in range(7):
                    if r < 6:
                        n = min(8, 2 * FT - 8 * r) * 16
                        src = tlS[:, 8 * r:8 * r + n // 16, :].rearrange("p t r -> p (t r)")
                    else:
                        n = 4 * FT
                        src = tlP[:].rearrange("p t j -> p (t j)")
                    c = (r % 4) * P
                    tr = transpose(pe, ps[0:n, 5 + r // 4, c:c + P], src)
                    if r in (3, 6):
                        tr.then_inc(s("tlo_ps"), 1)
                pe.wait_ge(s("conv_in"), CREDIT + 44 * l + 44)
                products(pe, G["down", l], lambda k: (aH[:, k, :], aL[:, k, :]), sq_ready, CREDIT + 8 * (2 * q + 5))
                pe.wait_ge(w_used, CREDIT + 2 * (G["down", l].first + G["down", l].chunks))
                pe.sem_inc(s("a_free"), 1)
                ssq(pe, 2 * q + 5)

            pe.wait_ge(x_ready, 8 * 7)
            for r in range(3):
                n = P if r < 2 else NS
                for half in range(2):
                    if r == 2:
                        pe.wait_ge(s("y_out"), half + 1)
                    for t in range(4):
                        tr = transpose(pe, ps[0:n, 2 * (r % 2) + half, t * P:(t + 1) * P],
                                       xT[:, 4 * half + t, r * P:r * P + n])
                    tr.then_inc(s("y_ps"), 1)

def constants():
    f = np.float32
    half = RDK // 2
    pos = np.concatenate([np.arange(SEQ), np.tile(PAST + np.arange(DEC_T), DEC_B)]).astype(f)
    inv = f(10000.0) ** (-np.arange(half, dtype=f) / f(half))
    ang = inv[:, None] * pos[None, :]
    rope = np.stack([np.cos(ang), np.sin(ang)], axis=1).astype(f)
    lg = np.log1p(-np.exp2(f(-5) - np.arange(RH, dtype=f))).astype(f)
    sc = f(RDK ** -0.5)

    def decay(n, h):
        d = np.arange(n, dtype=f)[None, :] - np.arange(n, dtype=f)[:, None]
        return np.where(d >= 0, np.exp(lg[h] * np.maximum(d, 0)), 0).astype(f) * sc

    ret = np.zeros((P, 8 * P + 4), f)
    retS = np.zeros((P, 12 * NS + 8), f)
    tok = np.arange(NS)
    same = (tok[:, None] // DEC_T == tok[None, :] // DEC_T)
    for h in range(RH):
        ret[:, h * P:(h + 1) * P] = decay(CHUNK, h)
        ret[:, (4 + h) * P:(5 + h) * P] = np.exp(lg[h] * (np.arange(CHUNK, dtype=f) + 1)) * sc
        ret[:, 8 * P + h] = np.exp(lg[h] * (CHUNK - 1 - np.arange(CHUNK, dtype=f)))
        small = np.tile(decay(DEC_T, h), (DEC_B, DEC_B)) * same
        retS[0:2 * NS, h * NS:(h + 1) * NS] = np.tile(small, (2, 1))
        retS[:, (4 + h) * NS:(5 + h) * NS] = np.exp(lg[h] * (tok % DEC_T + 1).astype(f)) * sc
        retS[:, (8 + h) * NS:(9 + h) * NS] = np.exp(lg[h] * (DEC_T - 1 - tok % DEC_T).astype(f))
    for b in range(DEC_B):
        retS[:, 12 * NS + b] = (np.arange(P) % NS) // DEC_T == b
    return {"c_ident": np.eye(P, dtype=f), "c_rope": rope, "c_ret": ret, "c_retS": retS}


OUTS = [(1, SEQ, D), (DEC_B, DEC_T, D), (DEPTH, 1, N_MEM, XH, XD), (DEPTH, 1, N_MEM, XH, XD),
        (1, 1, 2, 512), (1, DEC_B, 2, 512), (1, DEC_B, DEC_T, 512), (1, 1, RH, RDK, RDV),
        (1, DEC_B, RH, RDK, RDV), (DEPTH, 1, 2, 2 * DFF), (DEPTH, DEC_B, 2, 2 * DFF)]


def kernel(**inputs):
    import concourse.bacc as bacc
    from concourse.bass_utils import run_bass_kernel_spmd

    nc = bacc.Bacc("TRN2", target_bir_lowering=False, num_devices=1)
    arrays = {k: np.ascontiguousarray(v) for k, v in inputs.items()}
    arrays.update(constants())
    a = {k: nc.dram_tensor(k, v.shape, F32, kind="ExternalInput").ap() for k, v in arrays.items()}
    outs = [nc.dram_tensor(f"out_{i}", shape, F32, kind="ExternalOutput").ap() for i, shape in enumerate(OUTS)]
    build(nc, a, outs)
    r = run_bass_kernel_spmd(nc, [arrays], core_ids=[0]).results[0]
    return tuple(r[f"out_{i}"] for i in range(len(OUTS)))
```

```python
from contextlib import ExitStack

import numpy as np
import concourse.bass as bass
from concourse import mybir

F32 = mybir.dt.float32
F32R = mybir.dt.float32r
ACT = mybir.ActivationFunctionType
ALU = mybir.AluOpType
AX = mybir.AxisListType

P = 128
D = 1024
DT = D // P
SEQ, DEC_B, DEC_T = 256, 8, 4
NS = DEC_B * DEC_T
T = SEQ + NS
GRP = T // DEC_T
PG = SEQ // DEC_T
PAD = DEC_T + 2
CHUNK = 128
EPS = 1e-6
DEPTH = 2
N_MEM, XH, XD = 256, 4, 256
DFF = 2816
FT = DFF // P
RH, RDK, RDV = 4, 256, 512
PAST = 2048
CREDIT = 4
CW = 256


class Gemm:

    def __init__(self, name, w, ks, first, cols=None):
        self.name, self.w, self.ks, self.first = name, w, ks, first
        self.nk = len(ks)
        self.per = 2 * self.nk
        self.ncols = w.shape[1]
        self.steps = self.ncols // (2 * CW)
        self.chunks = self.steps * self.per
        self.cols = cols or (lambda i, half: 2 * CW * i + CW * half)
        self.next = None

    def rows(self, idx):
        kc = idx % self.nk
        return sum(self.ks[:kc]), self.ks[kc]


def build(nc, a, outs):
    (y_prompt, y_sample, mem_k, mem_v, sc_prompt, sc_sample, sgu_v, ret_prompt, ret_sample,
     fc_prompt, fc_sample) = outs

    order = []

    def gemm(name, w, ks=(8,), cols=None):
        g = Gemm(name, w, list(ks), sum(x.chunks for x in order), cols)
        if order:
            order[-1].next = g
        order.append(g)
        return g

    G = {}
    for l in range(DEPTH):
        if l % 2 == 0:
            G["in", l] = gemm("in_even", a["w_in_even"][l // 2])
            G["out", l] = gemm("out_even", a["w_out_even"][l // 2])
        else:
            G["in", l] = gemm("in_odd", a["w_in_odd"][l // 2])
            G["out", l] = gemm("out_odd", a["w_out_odd"][l // 2], (8, 8))
        G["k", l] = gemm("xk", a["w_xk"][l])
        G["v", l] = gemm("xv", a["w_xv"][l])
        G["q", l] = gemm("xq", a["w_xq"][l])
        G["o", l] = gemm("xo", a["w_xo"][l])
        G["up", l] = gemm("up", a["w_ffn_up"][l], (8,), lambda i, half: CW * i + DFF * half)
        G["down", l] = gemm("down", a["w_ffn_down"][l], (6, 6, 5, 5))

    ctx = ExitStack()
    with ctx:
        def sb(name, shape, dt=F32, scope=ctx):
            return scope.enter_context(nc.sbuf_tensor(name, [P] + shape, dt))

        def sem(name):
            return ctx.enter_context(nc.semaphore(name))

        raw = sb("raw", [4, 8, CW])
        wh = sb("wh", [2, 8, CW], F32R)
        wl = sb("wl", [2, 8, CW], F32R)
        xT = sb("xT", [DT, T])
        hh = sb("hh", [DT, T], F32R)
        hl = sb("hl", [DT, T], F32R)
        mT = sb("mT", [DT, T])
        sq = sb("sq", [DT, T])
        acc = sb("acc", [2, T])
        root = sb("root", [T])
        rstd = sb("rstd", [T])
        ident = sb("ident", [P])
        ones = sb("ones", [P])
        rowsn = sb("rowsn", [P])
        gT = sb("gT", [P])
        cwT = sb("cwT", [3 * P])
        small = sb("small", [64])

        ev = ExitStack()
        xn = sb("xn", [3, D], F32, ev)
        cwn = sb("cwn", [3, P], F32, ev)
        u = sb("u", [4, T], F32, ev)
        v = sb("v", [4, T], F32, ev)
        bg = sb("bg", [4, T], F32, ev)
        cg = sb("cg", [4, T], F32, ev)
        zz = sb("zz", [4, GRP, PAD], F32, ev)
        cv = sb("cv", [4, T], F32, ev)
        av = sb("av", [4, T], F32, ev)
        vnat = sb("vnat", [3, 4 * P], F32, ev)
        sgn = sb("sgn", [4, P], F32, ev)
        sgT = sb("sgT", [4, P], F32, ev)
        bdn = sb("bdn", [4, NS], F32, ev)
        bdT = sb("bdT", [4, NS], F32, ev)
        sbias = sb("sbias", [4, T], F32, ev)
        scn = sb("scn", [P], F32, ev)
        scT = sb("scT", [64], F32, ev)
        sctP = sb("sctP", [4, 2], F32, ev)
        sctS = sb("sctS", [4, 16], F32, ev)
        sco = sb("sco", [2, P], F32, ev)
        ev.close()

        at = ExitStack()
        kt = ExitStack()
        kT = sb("kT", [DT, N_MEM], F32, kt)
        kt.close()
        pB = sb("pB", [2, DEC_B * (P + DEC_T)], F32, at)
        vN = sb("vN", [2, D], F32, at)
        ring = sb("ring", [4, 2, D], F32, at)
        qB = sb("qB", [DT, DEC_B * (NS + DEC_T)], F32, at)
        pS = sb("pS", [N_MEM], F32, at)
        kv = ExitStack()
        memn = sb("memn", [2, D], F32, kv)
        kN = sb("kN", [2, D], F32, kv)
        mh = sb("mh", [DT, N_MEM], F32R, kv)
        ml = sb("ml", [DT, N_MEM], F32R, kv)
        kv.close()
        pr = sb("pr", [8, N_MEM], F32, at)
        prT = sb("prT", [4, 2, SEQ], F32, at)
        kTb = sb("kTb", [2, DT, N_MEM], F32, at)
        at.close()

        ff = ExitStack()
        aH = sb("aH", [FT, T], F32R, ff)
        aL = sb("aL", [FT, T], F32R, ff)
        zb = sb("zb", [4, GRP, PAD], F32, ff)
        cb = sb("cb", [4, T], F32, ff)
        ge = sb("ge", [2, T], F32, ff)
        pd = sb("pd", [2, T], F32, ff)
        stn = sb("stn", [6, P], F32, ff)
        stT = sb("stT", [2 * FT, 16], F32, ff)
        tlS = sb("tlS", [48, 16], F32, ff)
        tlP = sb("tlP", [2 * FT, 2], F32, ff)
        tlo = sb("tlo", [7, P], F32, ff)
        ff.close()

        od = ExitStack()
        gs = ExitStack()
        gS = sb("gS", [16, T], F32, gs)
        gs.close()
        h2l = sb("h2l", [8, T], F32R, od)
        h2h = sb("h2h", [8, T], F32R, od)
        V4 = sb("V4", [RH * RDV], F32R, od)
        vR = sb("vR", [2, RH * RDV], F32, od)
        kR = sb("kR", [2, RH * RDK], F32, od)
        cR = sb("cR", [8 * P + 4], F32, od)
        cS = sb("cS", [12 * NS + 8], F32, od)
        QM = sb("QM", [8, DEC_B * (NS + DEC_T)], F32, od)
        K4 = sb("K4", [RH * RDK], F32, od)
        gp = ExitStack()
        cs = sb("cs", [2, T], F32, gp)
        rA = sb("rA", [2, T], F32, gp)
        rB = sb("rB", [2, T], F32, gp)
        vt = sb("vt", [4, T], F32, gp)
        vhS = sb("vhS", [4, NS], F32R, gp)
        v4T = sb("v4T", [4, 4, NS], F32, gp)
        gp.close()
        K4m = sb("K4m", [2, RH * RDK], F32R, od)
        ks = ExitStack()
        k4T = sb("k4T", [8, 4, NS], F32, ks)
        kd = sb("kd", [8, NS], F32, ks)
        kdh = sb("kdh", [8, NS], F32R, ks)
        ks.close()
        S1 = sb("S1", [2, RDV], F32, od)
        S2 = sb("S2", [2, RDV], F32, od)
        scr = sb("scr", [2, P], F32, od)
        qd = sb("qd", [2, P], F32, od)
        rn = sb("rn", [RDV], F32, od)
        rg = sb("rg", [4, P], F32, od)
        od.close()
        scS = rowsn[:].rearrange("p (h i) -> p h i", h=RH)

        def state(h):
            slot = (G["out", 1].first + 2 + h // 2) % 4
            return raw[:, slot, 4 * (h % 2):4 * (h % 2) + 4, :].rearrange("p (d x) n -> p d (x n)", d=2)

        fin = ExitStack()
        yn = sb("yn", [3, D], F32, fin)
        fin.close()

        ps = ctx.enter_context(nc.psum_tensor("ps", [P, 8, 512], F32))
        BN = 4

        landed = [sem("landed_even"), sem("landed_odd")]
        hi_ready, lo_ready, w_used = sem("hi_ready"), sem("lo_ready"), sem("w_used")
        sq_ready, sum_step, ssq_ready = sem("sq_ready"), sem("sum_step"), sem("ssq_ready")
        root_ready, rstd_ready = sem("root_ready"), sem("rstd_ready")
        m_ready, scaled, x_ready = sem("m_ready"), sem("scaled"), sem("x_ready")
        hn_ready, h_hi, h_lo = sem("hn_ready"), sem("h_hi"), sem("h_lo")
        S = {}

        def s(name):
            if name not in S:
                S[name] = sem(name)
            return S[name]

        def load_weights(e, g):
            w = g.w

            def step(i):
                cols = [g.cols(i, half) for half in range(2)]
                even = ((i + g.first // 2) % 2) * 2
                if not isinstance(i, int):
                    cols, even = [e.snap(x) for x in cols], e.snap(even)
                for idx in range(g.per):
                    c = g.first + idx
                    r0, kn = g.rows(idx)
                    src = w[r0 * P:(r0 + kn) * P, bass.ds(cols[idx // g.nk], CW)] \
                        .rearrange("(t p) n -> p t n", p=P)
                    if g is G["out", 1] and (i, idx) == (0, 2):
                        load_states(e, c)
                    e.wait_ge(lo_ready, i * g.per + c - 4 + CREDIT + 1)
                    e.wait_ge(landed[c % 2], i * (8 * g.per) + 16 * (c // 2) + 16)
                    slot = even + c % 2 if g.per % 4 else c % 4
                    e.dma_start(raw[:, slot, 0:kn, :], src).then_inc(landed[c % 2], 16)
            if g.steps > 2:
                with e.Fori(0, g.steps) as i:
                    step(i)
            else:
                for i in range(g.steps):
                    step(i)

        def load_states(e, c):
            for h in range(RH):
                e.wait_ge(lo_ready, CREDIT + c - 4 + h // 2 + 1)
                e.dma_start(state(h), a["state_retention"][0, 0, h].rearrange("(d p) e -> p d e", p=P)).then_inc(s(f"SR_in{h}"), 16)
            for b in range(1, DEC_B):
                for h in range(RH):
                    e.wait_ge(s(f"SR_out{h}"), 16 * b)
                    e.dma_start(state(h), a["state_retention"][0, b, h].rearrange("(d p) e -> p d e", p=P)).then_inc(s(f"SR_in{h}"), 16)
            for h in range(RH):
                e.wait_ge(s(f"SR_out{h}"), 16 * DEC_B)

        def target(g, i, idx, last):
            idx += 2
            if idx < g.per:
                return g, i, idx
            if not last:
                return g, i + 1, idx - g.per
            return (g.next, 0, idx - g.per) if g.next else (None, 0, 0)

        def split(e, g, i, idx, high):
            if g is None:
                return
            c, kn = g.first + idx, g.rows(idx)[1]
            slot = (((i + c // 2) % 2) * 2 + c % 2) if g.per % 4 else c % 4
            src = raw[:, slot, 0:kn, :]
            if high:
                e.wait_ge(landed[c % 2], i * (8 * g.per) + 16 * (c // 2) + 32)
                e.wait_ge(w_used, i * (2 * g.per) + 2 * c - 2 + CREDIT)
                e.activation(wh[:, c % 2, 0:kn, :], src, ACT.Copy).then_inc(hi_ready, 1)
            else:
                e.wait_ge(hi_ready, i * g.per + c + 1)
                e.tensor_tensor(wl[:, c % 2, 0:kn, :], src, wh[:, c % 2, 0:kn, :].bitcast(F32),
                                ALU.subtract).then_inc(lo_ready, 1)

        def tiles_ready(e, g, i, half, j):
            c = g.first + half * g.nk + g.nk - 1
            e.wait_ge(w_used, i * (2 * g.per) + 2 * c + j + 1 + CREDIT)

        def run(e, g, high, evac, i0=0, i1=None):
            i1 = g.steps if i1 is None else i1

            def step(i, last):
                for idx in range(g.per):
                    split(e, *target(g, i, idx, last), high)
                    if idx % g.nk == g.nk - 1:
                        evac(i, idx // g.nk)
            end = i1 == g.steps
            n = i1 - end
            if n - i0 > 1:
                with e.Fori(i0, n) as i:
                    step(i, False)
            elif n - i0 == 1:
                step(i0, False)
            if end:
                step(g.steps - 1, True)

        def products(pe, g, pairs, freed, base, natural=False, i0=0, i1=None, drained=False,
                     hook=None):
            i1 = g.steps if i1 is None else i1

            def step(i):
                for idx in range(g.per):
                    half, kc = divmod(idx, g.nk)
                    r0, kn = g.rows(idx)
                    c = g.first + idx
                    pe.wait_ge(lo_ready, i * g.per + c + 1 + CREDIT)
                    for j in range(2):
                        t = 2 * half + j
                        if kc == 0 and not drained:
                            pe.wait_ge(freed, i * 4 + base + t - 3)
                        for k in range(kn):
                            xh, xl = pairs(r0 + k)
                            if natural:
                                w_h, w_l = wh[:, c % 2, k, :], wl[:, c % 2, k, :]
                                cut = slice(j * P, (j + 1) * P)
                                trio = ((xh[:, cut], w_h), (xl[:, cut], w_h), (xh[:, cut], w_l))
                                out = ps[:, t, 0:CW]
                            else:
                                w_h = wh[:, c % 2, k, j * P:(j + 1) * P]
                                w_l = wl[:, c % 2, k, j * P:(j + 1) * P]
                                trio = ((w_h, xh), (w_h, xl), (w_l, xh))
                                out = ps[:, t, 0:T]
                            for n, (lhsT, rhs) in enumerate(trio):
                                mm = pe.matmul(out, lhsT, rhs, start=(kc == 0 and k == 0 and n == 0),
                                               stop=(kc == g.nk - 1 and k == kn - 1 and n == 2))
                        mm.then_inc(w_used, 1)
                    if hook:
                        hook(i, idx)
            if i1 - i0 > 1:
                with pe.Fori(i0, i1) as i:
                    step(i)
            else:
                step(i0)

        def square_x(act, n):
            q = n // 2
            if n:
                act.wait_ge(sum_step, 3 * n)
            for t in range(DT):
                act.wait_ge(x_ready, DT * q + t + 1)
                act.activation(sq[:, t, :], xT[:, t, :], ACT.Square).then_inc(sq_ready, 1)

        def sums(dve, n):
            if n:
                dve.wait_ge(ssq_ready, n)
            dve.wait_ge(sq_ready, CREDIT + 8 * n + 4)
            dve.tensor_tensor(acc[:], sq[:, 0:2, :], sq[:, 2:4, :], ALU.add).then_inc(sum_step, 1)
            for r in (1, 2):
                dve.wait_ge(sq_ready, CREDIT + 8 * n + 4 + 2 * r)
                dve.wait_ge(sum_step, 3 * n + r)
                dve.tensor_tensor(acc[:], acc[:], sq[:, 2 * r + 2:2 * r + 4, :],
                                  ALU.add).then_inc(sum_step, 1)

        def ssq(pe, n):
            pe.wait_ge(sum_step, 3 * n + 3)
            if n:
                pe.wait_ge(root_ready, n)
            pe.matmul(ps[:, BN, 0:T], ones[:], acc[:, 0, :], start=True, stop=False)
            pe.matmul(ps[:, BN, 0:T], ones[:], acc[:, 1, :], start=False,
                      stop=True).then_inc(ssq_ready, 1)

        def take_root(act, n):
            act.wait_ge(ssq_ready, n + 1)
            act.activation(root[:], ps[:, BN, 0:T], ACT.Sqrt, bias=eps_col, scale=1.0 / D).then_inc(root_ready, 1)

        def invert(dve, n):
            dve.wait_ge(root_ready, n + 1)
            dve.reciprocal(rstd[:], root[:]).then_inc(rstd_ready, 1)

        def add_branch(dve, q):
            dve.wait_ge(rstd_ready, 2 * q + 2)
            gain = gcol("post", q)
            for t in range(DT + 1):
                if t < DT:
                    dve.wait_ge(m_ready, DT * q + t + 1)
                    dve.tensor_tensor(mT[:, t, :], mT[:, t, :], rstd[:], ALU.mult).then_inc(scaled, 1)
                if t > 0:
                    dve.wait_ge(scaled, DT * q + t)
                    dve.scalar_tensor_tensor(out=xT[:, t - 1, :], in0=mT[:, t - 1, :], scalar=gain(t - 1),
                                             in1=xT[:, t - 1, :], op0=ALU.mult,
                                             op1=ALU.add).then_inc(x_ready, 1)

        def normed_x(dve, q):
            dve.wait_ge(rstd_ready, 2 * q + 1)
            for t in range(DT):
                dve.tensor_tensor(mT[:, t, :], xT[:, t, :], rstd[:], ALU.mult).then_inc(hn_ready, 1)

        def normed_high(act, q):
            gain = gcol("pre", q)
            for t in range(DT):
                act.wait_ge(hn_ready, DT * q + t + 1)
                act.activation(hh[:, t, :], mT[:, t, :], ACT.Copy, scale=gain(t)).then_inc(h_hi, 1)

        def normed_low(dve, q):
            gain = gcol("pre", q)
            for t in range(DT):
                dve.wait_ge(h_hi, DT * q + t + 1)
                dve.scalar_tensor_tensor(out=hl[:, t, :], in0=mT[:, t, :], scalar=gain(t),
                                         in1=hh[:, t, :].bitcast(F32), op0=ALU.mult,
                                         op1=ALU.subtract).then_inc(h_lo, 1)

        GROWS = {("pre", 0): 0, ("post", 0): 8, ("pre", 1): 16, ("post", 1): 24, ("pre", 2): 32,
                 ("post", 2): 40}
        GB = 56

        def gcol(kind, q):
            l, br = divmod(q, 3)
            return lambda t: gT[:, GB * l + GROWS[kind, br] + t:GB * l + GROWS[kind, br] + t + 1]

        def memgain(l, t):
            return gT[:, GB * l + 48 + t:GB * l + 49 + t]

        def vgain(t):
            return gT[:, 112 + t:113 + t]

        def sctap(j, t):
            return gT[:, 116 + 4 * j + t:117 + 4 * j + t]

        def ftap(l, j, t):
            c = (3 * l + j) * 2 * FT
            return cwT[:, bass.ds(t + c, 1)]

        eps_col = small[:, 0:1]

        def pre_pe(pe, q):
            ssq(pe, 2 * q)

        def pre_act(act, q):
            square_x(act, 2 * q)
            take_root(act, 2 * q)
            normed_high(act, q)

        def pre_dve(dve, q):
            sums(dve, 2 * q)
            invert(dve, 2 * q)
            normed_x(dve, q)
            normed_low(dve, q)

        def post_act(act, q):
            take_root(act, 2 * q + 1)

        def post_dve(dve, q):
            sums(dve, 2 * q + 1)
            invert(dve, 2 * q + 1)
            add_branch(dve, q)

        def branch_out_act(act, g, q):
            n = 2 * q + 1

            def evac(i, half):
                if not isinstance(i, int) or i == 0:
                    act.wait_ge(sum_step, 3 * n)
                for j in range(2):
                    t = i * 4 + 2 * half + j
                    tiles_ready(act, g, i, half, j)
                    src = ps[:, 2 * half + j, 0:T]
                    act.activation(mT[:, t, :], src, ACT.Copy).then_inc(m_ready, 1)
                    act.activation(sq[:, t, :], src, ACT.Square).then_inc(sq_ready, 1)
            run(act, g, True, evac)

        def nothing(i, half):
            pass

        def normed(k):
            return hh[:, k, :], hl[:, k, :]

        def groups(x):
            return x.rearrange("p (g t) -> p g t", t=DEC_T)

        def transpose(pe, out, x, rows=P):
            return pe.transpose(out, x, ident[0:rows, 0:rows])

        L = range(DEPTH)
        stores = [0]
        dmat = lambda h: cR[:, h * P:(h + 1) * P]
        qdec = lambda h: cR[:, (4 + h) * P:(5 + h) * P]
        kdec = lambda h: cR[:, 8 * P + h:8 * P + h + 1]
        dmatS = cS[:, 0:4 * NS].rearrange("p (h i) -> p h i", h=RH)
        qdecS = cS[:, 4 * NS:8 * NS].rearrange("p (h o i) -> p h o i", h=RH, o=1)
        kdecS = cS[:, 8 * NS:12 * NS].rearrange("p (h o i) -> p h o i", h=RH, o=1)
        maskS = lambda b: cS[:, 12 * NS + b:12 * NS + b + 1]
        gam = [float(np.float32(1) - np.float32(2.0) ** np.float32(-5 - h)) for h in range(RH)]
        UNITS = [(h, c) for h in range(RH) for c in range(2)]

        def pool_retention(pool, store):
            pool.wait_ge(s("a_free"), 1)
            pool.dma_start(cs[:], a["c_rope"]).then_inc(s("ret_in"), 16)
            pool.dma_start(cR[:], a["c_ret"]).then_inc(s("ret_in"), 16)
            pool.dma_start(cS[:], a["c_retS"]).then_inc(s("ret_in"), 16)
            for n, (hp, c) in enumerate(UNITS):
                for h in range(RH):
                    pool.wait_ge(s("SR_new"), 8 * n + 2 * h + 2)
                    pool.dma_start(ret_sample[0, n, h].rearrange("(d p) e -> p d e", p=P), state(h)).then_inc(s(f"SR_out{h}"), 16)
                    if c == 1 and h == 1:
                        pool.wait_ge(s("S2_ready"), 2 * hp + 2)
                        pool.dma_start(ret_prompt[0, 0, hp].rearrange("(t p) e -> p t e", p=P), S2[:]).then_inc(s("S2_stored"), 16)
            pool.wait_ge(s("S2_stored"), 16 * RH)

        def act_even(act, l):
            g = G["in", l]

            def evac(i, half):
                for j in range(2):
                    t = 2 * half + j
                    tiles_ready(act, g, i, half, j)
                    src = ps[:, t, 0:T]
                    if i == 0:
                        act.activation(u[:, t, :], src, ACT.Gelu_apprx_tanh).then_inc(s("in_even"), 1)
                    elif i == 1:
                        act.activation(v[:, t, :], src, ACT.Gelu_apprx_tanh).then_inc(s("in_even"), 1)
                    elif i == 2:
                        act.activation(bg[:, t, :], src, ACT.Copy).then_inc(s("in_even"), 1)
                    elif i == 3:
                        act.activation(cg[:, t, :], src, ACT.Copy).then_inc(s("in_even"), 1)
                    if i == 1:
                        act.wait_ge(s("in_even"), CREDIT + 4 + t + 1)
                        act.wait_ge(sum_step, 3)
                        act.activation(sq[:, t, :], v[:, t, :], ACT.Square).then_inc(s("v_sq"), 1)
            for i in range(g.steps):
                for idx in range(2):
                    split(act, *target(g, i, idx, i == g.steps - 1), True)
                    if i < 4:
                        evac(i, idx)
            act.wait_ge(s("v_ps"), 1)
            act.activation(root[:], ps[:, BN, 0:T], ACT.Sqrt, bias=eps_col, scale=1.0 / (4 * P)).then_inc(s("v_sq"), 1)
            for c in range(3):
                n = P if c < 2 else NS
                act.wait_ge(s("v_ps"), c + 3)
                act.activation(vnat[0:n, c, :], ps[0:n, 5 + c, :], ACT.Copy).then_inc(s("vnat_ready"), 1)
            act.wait_ge(s("v_ps"), 2)
            act.activation(sco[0:8, 0, :], ps[0:8, BN, 0:P], ACT.Copy)
            act.activation(sco[0:64, 1, :], ps[0:64, BN, P:2 * P], ACT.Copy).then_inc(s("sco_ready"), 1)
            for t in range(4):
                act.wait_ge(s("b_ready"), t + 1)
                act.activation(hh[:, 4 + t, :], cv[:, t, :], ACT.Copy).then_inc(s("even_hi"), 1)
            for t in range(4):
                act.wait_ge(s("av_ready"), t + 1)
                act.activation(hh[:, t, :], av[:, t, :], ACT.Copy).then_inc(s("even_hi"), 1)

        def act_odd(act, l):
            g = G["in", l]
            act.wait_ge(s("ret_in"), 48)

            def keep(i, half):
                for j in range(2):
                    t = 2 * half + j
                    tiles_ready(act, g, i, half, j)
                    act.wait_ge(s("vt_used"), i * 4 + 2 * half + 2)
                    act.activation(vt[:, t, :], ps[:, t, 0:T], ACT.Copy).then_inc(s("z_ready"), 1)

            def gates(i, half):
                for j in range(2):
                    t = 2 * half + j
                    tiles_ready(act, g, i, half, j)
                    act.activation(gS[:, i * 4 + (t - 32), :], ps[:, t, 0:T], ACT.Silu).then_inc(s("z_ready"), 1)
            run(act, g, True, keep, 0, 4)
            def naturals(i):
                for t in range(4):
                    e = 4 * (i - 4) + t
                    act.wait_ge(s("vR_ps"), e + 1)
                    act.activation(vR[:, :, e * P:(e + 1) * P],
                                   ps[:, 5 + e % 2, 0:2 * P].rearrange("p (c e) -> p c e", c=2), ACT.Copy)
                    act.activation(V4[:, e * P:(e + 1) * P], ps[:, 5 + e % 2, 2 * P:3 * P], ACT.Copy).then_inc(s("vR_ready"), 1)
            for i in range(4, 9):
                for idx in range(2):
                    split(act, *target(g, i, idx, False), True)
                    if idx == 0 and i > 4:
                        naturals(i - 1)
                    (keep if i < 8 else gates)(i, idx)
            run(act, g, True, gates, 9, 10)
            run(act, g, True, gates, 10, 11)
            for r in range(2):
                act.wait_ge(s("k4_ps"), r + 1)
                act.activation(K4[:, 512 * r:512 * r + 512], ps[:, 5 + r, :], ACT.Copy).then_inc(s("K4_ready"), 1)
            run(act, g, True, gates, 11, 12)

            def own_keys(b):
                if b >= 2:
                    act.wait_ge(s("SU_ps"), 8 * (b - 1))
                act.activation(K4m[:, b % 2, :], K4[:], ACT.Copy, scale=maskS(b)).then_inc(s("K4m_ready"), 1)

            act.wait_ge(s("K4_ready"), 2)
            own_keys(0)
            act.wait_ge(s("ret_in"), 48)
            for n in range(4):
                c, hf = divmod(n, 2)
                act.wait_ge(s("kR_ps"), n + 1)
                for k in range(2):
                    h = 2 * hf + k
                    ins = act.activation(kR[:, c, h * RDK:(h + 1) * RDK], ps[:, 5 + n % 2, k * RDK:(k + 1) * RDK],
                                         ACT.Copy, scale=kdec(h))
                ins.then_inc(s("kR_ready"), 1)

            def high(n):
                h, c = UNITS[n]
                act.wait_ge(s("rg_ready"), n + 1)
                (dh, o) = (hh, 4 * h) if h < 2 else (h2h, 4 * h - 8)
                act.activation(dh[:, o:o + 4, c * CHUNK:(c + 1) * CHUNK], rg[:], ACT.Copy).then_inc(s("rg_hi"), 1)

            for n, (h, c) in enumerate(UNITS):
                if n:
                    high(n - 1)
                if c == 0:
                    act.wait_ge(s("S_ps"), 2 * n + 2)
                    if h:
                        act.wait_ge(s("S2_ready"), 2 * h)
                    act.activation(S1[:], ps[:, 0:2, :], ACT.Copy).then_inc(s("S1_ready"), 1)
                if n < DEC_B - 1:
                    own_keys(n + 1)
                act.wait_ge(s("ro_mv"), n + 1)
                act.activation(small[:, 12:13], small[:, 11:12], ACT.Sqrt, bias=eps_col).then_inc(s("ro_root"), 1)
            high(7)
            act.wait_ge(s("ro_mv"), 9)
            act.activation(small[:, 12:13], small[:, 11:12], ACT.Sqrt, bias=eps_col).then_inc(s("ro_root"), 1)
            act.wait_ge(s("rg_ready"), 9)
            for dh, h in ((hh, 0), (h2h, 2)):
                act.activation(sample_gates(dh), sample_rows(h), ACT.Copy).then_inc(s("rg_hi"), 1)

        def sample_gates(x):
            return x[:, :, SEQ:T].rearrange("p (h e) i -> p e h i", e=4)

        def sample_rows(h):
            return rg[:].rearrange("p e (h i) -> p e h i", h=RH)[:, :, h:h + 2]

        KBANKS = (4, 6, 7)

        def own_tokens(row, width):
            return row.rearrange("p (b x) -> p b x", b=DEC_B)[:, :, 0:width].rearrange("p b (h i) -> p b h i", i=NS)[:, :, :, 0:DEC_T]

        def sample_heads(x):
            return x[:, :, SEQ:T].rearrange("p (h d) i -> p h d i", d=2)

        def take_keys(e, l, b, act):
            for r in (0, 2) if act else (1, 3):
                n = 4 * b + r
                e.wait_ge(s("kTb_ps"), 32 * l + n + 1)
                if b >= 2:
                    e.wait_ge(s("sS_mm"), 8 * l + b - 1)
                src = ps[:, KBANKS[n % 3], :].rearrange("p (t m) -> p t m", t=2)
                if act:
                    e.activation(kTb[:, b % 2, 2 * r:2 * r + 2, :], src, ACT.Copy).then_inc(s("kTb_act"), 1)
                else:
                    e.tensor_copy(kTb[:, b % 2, 2 * r:2 * r + 2, :], src).then_inc(s("kTb_dve"), 1)

        def act_attention(act, l):
            def exps(h):
                act.wait_ge(s("nm_ready"), 5 * l + h + 1)
                for n in (2 * h, 2 * h + 1):
                    act.activation(pr[:, n, :], ps[:, h, (n % 2) * N_MEM:(n % 2 + 1) * N_MEM], ACT.Exp, scale=XD ** -0.5,
                                   bias=small[:, 24 + n:25 + n], accum_out=small[:, 32 + n:33 + n]).then_inc(s("exp_ready"), 1)

            def turned(h):
                act.wait_ge(s("pT_ps"), 5 * l + h + 1)
                act.activation(prT[:, h, :, :], ps[:, h, :].rearrange("p (m t) -> p m t", m=2), ACT.Copy).then_inc(s("pT_ready"), 1)

            def heads_high(h):
                act.wait_ge(s("o_ps"), 5 * l + h + 1)
                act.activation(hh[:, 2 * h:2 * h + 2, 0:SEQ], ps[:, h, :].rearrange("p (d t) -> p d t", d=2), ACT.Copy).then_inc(s("oh_hi"), 1)

            for b in range(DEC_B):
                take_keys(act, l, b, True)
                if b < 4:
                    exps(b)
                if b == 5:
                    act.wait_ge(s("kv_stored"), 32 * l + 32)
                if b >= 5:
                    turned(b - 5)
                if b >= 6:
                    heads_high(b - 6)
            turned(3)
            act.wait_ge(s("nm_ready"), 5 * l + 5)
            act.activation(pS[:], ps[:, 5, 0:N_MEM], ACT.Exp, scale=XD ** -0.5, bias=small[:, 49:50],
                           accum_out=small[:, 50:51]).then_inc(s("exp_ready"), 1)
            heads_high(2)
            act.wait_ge(s("pT_ps"), 5 * l + 5)
            act.wait_ge(s("own_zero"), 2 * l + 2)
            act.activation(own_tokens(pB[:, 0, :], P), ps[:, 7, 0:P].rearrange("p (h b t) -> p b h t", h=XH, t=DEC_T),
                           ACT.Copy).then_inc(s("pB_act"), 1)
            heads_high(3)
            act.wait_ge(s("oS_mm"), 8 * l + 8)
            act.activation(pS[:], ps[:, 6, 0:XD], ACT.Copy).then_inc(s("oS_out"), 1)
            act.wait_ge(s("o_ps"), 5 * l + 5)
            act.activation(sample_heads(hh), ps[:, 7, 0:XD].rearrange("p (d h i) -> p h d i", d=2, h=XH),
                           ACT.Copy).then_inc(s("oh_hi"), 1)

        def dve_even(dve, l):
            g = G["in", l]
            for i in range(g.steps):
                for idx in range(2):
                    split(dve, *target(g, i, idx, i == g.steps - 1), False)
                    if i < 4:
                        continue
                    for j in range(2):
                        t = 2 * idx + j
                        tiles_ready(dve, g, i, idx, j)
                        dve.wait_ge(s("in_even"), CREDIT + 12 + t + 1)
                        dve.tensor_tensor(zz[:, t, :, 2:PAD], groups(cg[:, t, :]), groups(ps[:, t, 0:T]),
                                          ALU.mult).then_inc(s("zz_main"), 1)
            dve.wait_ge(s("v_sq"), 4)
            dve.wait_ge(ssq_ready, 1)
            dve.tensor_tensor(acc[:], sq[:, 0:2, :], sq[:, 2:4, :], ALU.add).then_inc(s("vn_ready"), 1)
            dve.wait_ge(s("zz_main"), 4)
            dve.tensor_copy(zz[:, :, 1:PG, 0:2], zz[:, :, 0:PG - 1, 4:6]).then_inc(s("zz_pre"), 1)
            dve.tensor_copy(zz[:, :, PG:, 0:2], scT[:].rearrange("p (t b j) -> p t b j", t=4, j=2)).then_inc(s("zz_pre"), 1)
            dve.tensor_copy(sctP[:], zz[:, :, PG - 1, 4:6]).then_inc(s("sct_ready"), 1)
            dve.tensor_copy(sctS[:].rearrange("p t (b j) -> p t b j", j=2), zz[:, :, PG:, 4:6]).then_inc(s("sct_ready"), 1)
            dve.wait_ge(s("v_sq"), 5)
            dve.reciprocal(rstd[:], root[:]).then_inc(s("vn_ready"), 1)
            dve.wait_ge(s("vn_ready"), 2)
            for t in range(4):
                dve.scalar_tensor_tensor(out=v[:, t, :], in0=v[:, t, :], scalar=vgain(t), in1=rstd[:],
                                         op0=ALU.mult, op1=ALU.mult).then_inc(s("vn_ready"), 1)
            dve.wait_ge(s("zz_pre"), 2)
            for t in range(4):
                dve.tensor_scalar(groups(cv[:, t, :]), zz[:, t, :, 2:PAD], sctap(2, t), None, ALU.mult).then_inc(s("cv"), 1)
            for j in (1, 0):
                for t in range(4):
                    dve.wait_ge(s("cv"), 4 * (2 - j) + t)
                    dve.wait_ge(s("cv"), 4 * (1 - j) + t + 1)
                    dve.scalar_tensor_tensor(out=groups(cv[:, t, :]), in0=zz[:, t, :, j:j + 4], scalar=sctap(j, t),
                                             in1=groups(cv[:, t, :]), op0=ALU.mult, op1=ALU.add).then_inc(s("cv"), 1)
            for t in range(4):
                dve.wait_ge(s("cv"), 8 + t + 1)
                dve.tensor_tensor(cv[:, t, :], cv[:, t, :], bg[:, t, :], ALU.mult).then_inc(s("b_ready"), 1)
            for t in range(4):
                dve.wait_ge(s("even_hi"), t + 1)
                dve.tensor_tensor(hl[:, 4 + t, :], cv[:, t, :], hh[:, 4 + t, :].bitcast(F32), ALU.subtract).then_inc(s("even_lo"), 1)
            dve.wait_ge(s("bias_in"), 160)
            for t in range(4):
                dve.wait_ge(s("mix_ps"), t + 1)
                dve.tensor_tensor(av[:, t, :], sbias[:, t, :], ps[:, t, 0:T], ALU.add).then_inc(s("mixed"), 1)
            for t in range(4):
                dve.wait_ge(s("mixed"), t + 1)
                dve.tensor_tensor(av[:, t, :], av[:, t, :], u[:, t, :], ALU.mult).then_inc(s("av_ready"), 1)
            for t in range(4):
                dve.wait_ge(s("even_hi"), 4 + t + 1)
                dve.tensor_tensor(hl[:, t, :], av[:, t, :], hh[:, t, :].bitcast(F32), ALU.subtract).then_inc(s("even_lo"), 1)

        def dve_odd(dve, l):
            g = G["in", l]

            def turn(dst, i0):
                def evac(i, half):
                    if half == 0:
                        dve.wait_ge(s("ret_in"), 48)
                    pair = vt[:, 2 * half:2 * half + 2, :]
                    dve.wait_ge(s("z_ready"), CREDIT + i * 4 + 2 * half + 2)
                    dve.wait_ge(s("turned"), i * 4 + 2 * half + CREDIT)
                    dve.tensor_tensor(rA[:], pair, cs[:, 0, :].unsqueeze(1).to_broadcast([P, 2, T]), ALU.mult).then_inc(s("vt_used"), 1)
                    dve.tensor_tensor(rB[:], pair, cs[:, 1, :].unsqueeze(1).to_broadcast([P, 2, T]), ALU.mult).then_inc(s("vt_used"), 1)
                    dve.wait_ge(s("vt_used"), CREDIT + i * 4 + 2 * half + 2)
                    dve.tensor_tensor(dst[:, i * 4 + (2 * half - 4 * i0), :], rA[:, 0, :], rB[:, 1, :], ALU.subtract).then_inc(s("turned"), 1)
                    dve.tensor_tensor(dst[:, i * 4 + (2 * half + 1 - 4 * i0), :], rB[:, 0, :], rA[:, 1, :], ALU.add).then_inc(s("turned"), 1)
                return evac
            run(dve, g, False, turn(mT, 0), 0, 2)
            run(dve, g, False, turn(sq, 2), 2, 4)
            for i in range(4, 8):
                for idx in range(2):
                    split(dve, *target(g, i, idx, False), False)
                    for j in range(2):
                        t = 2 * idx + j
                        e = 4 * (i - 4) + t
                        dve.wait_ge(s("z_ready"), CREDIT + 4 * i + t + 1)
                        if e >= 4:
                            dve.wait_ge(s("vR_ps"), e - 3)
                        dve.tensor_copy(vhS[:, t, :], vt[:, t, SEQ:T]).then_inc(s("vh"), 1)
                        dve.wait_ge(s("vh"), e + 1)
                        both = vhS[:, t, :].bitcast(F32).unsqueeze(1).to_broadcast([P, 2, NS])
                        dve.tensor_copy(v4T[:, t, 0:4:2, :], both)
                        dve.tensor_tensor(v4T[:, t, 1:4:2, :], vt[:, t, SEQ:T].unsqueeze(1).to_broadcast([P, 2, NS]),
                                          both, ALU.subtract).then_inc(s("v4T_ready"), 1)
            run(dve, g, False, nothing, 8, 9)
            kS = sq[:, :, SEQ:T]
            four = lambda x: x.rearrange("p (h d) i -> p h d i", d=2)
            dve.wait_ge(s("ret_in"), 48)
            dve.wait_ge(s("vR_ps"), 16)
            dve.wait_ge(s("turned"), CREDIT + 16)
            dve.tensor_copy(k4T[:, :, 0:2, :], kS.unsqueeze(2).to_broadcast([P, 8, 2, NS])).then_inc(s("kdup"), 1)
            dve.memset(QM[:], 0.0).then_inc(s("QM_step"), 1)
            dve.tensor_tensor(four(kd[:]), four(mT[:, :, SEQ:T]), qdecS.to_broadcast([P, RH, 2, NS]), ALU.mult).then_inc(s("QM_step"), 1)
            run(dve, g, False, nothing, 9, 10)
            dve.wait_ge(s("QM_step"), 2)
            dve.tensor_copy(QM[:].rearrange("p k (b x) -> p k b x", b=DEC_B)[:, :, :, 0:DEC_T],
                            kd[:].rearrange("p k (b t) -> p k b t", t=DEC_T)).then_inc(s("QM_step"), 1)
            dve.wait_ge(s("scS_ps"), 1)
            dve.tensor_tensor(scS[0:64], dmatS[0:64], ps[0:64, 7, 0:4 * NS].rearrange("p (h i) -> p h i", h=RH),
                              ALU.mult).then_inc(s("scS_ready"), 1)
            dve.wait_ge(s("QM_step"), 3)
            dve.tensor_tensor(four(kd[:]), four(kS), kdecS.to_broadcast([P, RH, 2, NS]), ALU.mult).then_inc(s("kd"), 1)
            dve.wait_ge(s("kd"), 1)
            dve.tensor_copy(kdh[:], kd[:]).then_inc(s("kd"), 1)
            dve.wait_ge(s("kd"), 2)
            kh2 = kdh[:].bitcast(F32).unsqueeze(2).to_broadcast([P, 8, 2, NS])
            dve.tensor_copy(k4T[:, :, 0:2, :], kh2)
            dve.tensor_tensor(k4T[:, :, 2:4, :], kd[:].unsqueeze(2).to_broadcast([P, 8, 2, NS]), kh2,
                              ALU.subtract).then_inc(s("k4T_full"), 1)
            run(dve, g, False, nothing, 10, 11)
            run(dve, g, False, nothing, 11, 12)

            def update(b, k):
                dve.wait_ge(s("SU_ps"), 8 * b + k + 1)
                st = state(k // 2)[:, k % 2, :]
                dve.scalar_tensor_tensor(out=st, in0=st, scalar=gL(k // 2, DEC_T), in1=ps[:, 2 + k % 2, :],
                                         op0=ALU.mult, op1=ALU.add).then_inc(s("SR_new"), 1)

            def gated(n):
                h, c = UNITS[n]
                dve.wait_ge(s("rT_ps"), n + 1)
                if n:
                    dve.wait_ge(s("rg_lo"), n)
                dve.tensor_tensor(rg[:], gS[:, 4 * h:4 * h + 4, c * CHUNK:(c + 1) * CHUNK],
                                  ps[:, 7, :].rearrange("p (e i) -> p e i", e=4), ALU.mult).then_inc(s("rg_ready"), 1)

            def low(n):
                h, c = UNITS[n]
                tok = slice(c * CHUNK, (c + 1) * CHUNK)
                (dh, dl, o) = (hh, hl, 4 * h) if h < 2 else (h2h, h2l, 4 * h - 8)
                dve.wait_ge(s("rg_hi"), n + 1)
                dve.tensor_tensor(dl[:, o:o + 4, tok], rg[:], dh[:, o:o + 4, tok].bitcast(F32), ALU.subtract).then_inc(s("rg_lo"), 1)

            for n, (h, c) in enumerate(UNITS):
                tok = slice(c * CHUNK, (c + 1) * CHUNK)
                dve.wait_ge(s("rs_ps"), n + 1)
                dve.tensor_tensor(scr[:, n % 2, :], dmat(h), ps[:, 5, 0:P], ALU.mult).then_inc(s("rs_ready"), 1)
                if c == 1:
                    dve.tensor_tensor(qd[:], mT[:, 2 * h:2 * h + 2, tok],
                                      qdec(h).unsqueeze(1).to_broadcast([P, 2, P]), ALU.mult).then_inc(s("qd_ready"), 1)
                if n:
                    gated(n - 1)
                update(n, 0)
                update(n, 1)
                if n:
                    low(n - 1)
                update(n, 2)
                update(n, 3)
                if c == 1:
                    for dt in range(2):
                        dve.wait_ge(s("S_ps"), 2 * n + dt + 1)
                        if h and dt == 0:
                            dve.wait_ge(s("S2_stored"), 16 * h)
                        dve.scalar_tensor_tensor(out=S2[:, dt, :], in0=S1[:, dt, :], scalar=gL(h, CHUNK),
                                                 in1=ps[:, dt, :], op0=ALU.mult, op1=ALU.add).then_inc(s("S2_ready"), 1)
                dve.wait_ge(s("ro_ps"), n + 1)
                moments(dve, n, ps[:, 6, :])
                update(n, 4)
                update(n, 5)
                scaled_rows(dve, n, ps[:, 6, :])
                update(n, 6)
                update(n, 7)
            gated(7)
            low(7)
            moments(dve, 8, ps[:, BN, :])
            scaled_rows(dve, 8, ps[:, BN, :])
            dve.wait_ge(s("rT_ps"), 9)
            dve.wait_ge(s("rg_lo"), 8)
            dve.tensor_tensor(rg[:].rearrange("p e (h i) -> p e h i", h=RH), sample_gates(gS),
                              ps[:, 7, :].rearrange("p (e h i) -> p e h i", e=4, h=RH), ALU.mult).then_inc(s("rg_ready"), 1)
            for n, (dh, dl) in enumerate(((hh, hl), (h2h, h2l))):
                dve.wait_ge(s("rg_hi"), 9 + n)
                dve.tensor_tensor(sample_gates(dl), sample_rows(2 * n), sample_gates(dh).bitcast(F32),
                                  ALU.subtract).then_inc(s("rg_lo"), 1)

        def gL(h, n):
            return float(np.exp(np.float32(np.log1p(-np.exp2(np.float32(-5 - h)))) * np.float32(n)))

        def moments(dve, n, src):
            dve.bn_stats(small[:, 52:58], src).then_inc(s("ro_st"), 1)
            dve.wait_ge(s("ro_st"), n + 1)
            dve.bn_aggr(small[:, 10:12], small[:, 52:58]).then_inc(s("ro_mv"), 1)

        def scaled_rows(dve, n, src):
            dve.wait_ge(s("ro_root"), n + 1)
            dve.reciprocal(small[:, 13:14], small[:, 12:13]).then_inc(s("ro_inv"), 1)
            dve.wait_ge(s("ro_inv"), n + 1)
            if n:
                dve.wait_ge(s("rT_ps"), n)
            dve.tensor_scalar(rn[:], src, small[:, 10:11], small[:, 13:14], ALU.subtract,
                              ALU.mult).then_inc(s("rn_ready"), 1)

        def dve_attention(dve, l):
            def maxima(h):
                if h == XH:
                    dve.wait_ge(s("sS_mm"), 8 * l + 8)
                    src, mx, nm = ps[:, 5, 0:N_MEM], small[:, 48:49], small[:, 49:50]
                else:
                    dve.wait_ge(s("sc_ps"), 4 * l + h + 1)
                    src = ps[:, h, :].rearrange("p (t m) -> p t m", t=2)
                    mx, nm = small[:, 16 + 2 * h:18 + 2 * h], small[:, 24 + 2 * h:26 + 2 * h]
                dve.tensor_reduce(mx, src, AX.X, ALU.max).then_inc(s("mx_ready"), 1)
                dve.wait_ge(s("mx_ready"), 5 * l + h + 1)
                dve.tensor_scalar(nm, mx, -XD ** -0.5, None, ALU.mult).then_inc(s("nm_ready"), 1)

            def shares(h):
                sample = h == XH
                dve.wait_ge(s("exp_ready"), 9 * l + (9 if sample else 2 * h + 2))
                sm, rc = (small[:, 50:51], small[:, 51:52]) if sample else \
                    (small[:, 32 + 2 * h:34 + 2 * h], small[:, 40 + 2 * h:42 + 2 * h])
                dve.reciprocal(rc, sm).then_inc(s("rc_ready"), 1)
                dve.wait_ge(s("rc_ready"), 5 * l + h + 1)
                if sample:
                    dve.tensor_scalar(pS[:], pS[:], rc, None, ALU.mult).then_inc(s("p_ready"), 1)
                    return
                for n in (2 * h, 2 * h + 1):
                    dve.tensor_scalar(pr[:, n, :], pr[:, n, :], small[:, 40 + n:41 + n], None, ALU.mult).then_inc(s("p_ready"), 1)

            def heads_low(h):
                dve.wait_ge(s("oh_hi"), 5 * l + h + 1)
                dve.tensor_tensor(hl[:, 2 * h:2 * h + 2, 0:SEQ], ps[:, h, :].rearrange("p (d t) -> p d t", d=2),
                                  hh[:, 2 * h:2 * h + 2, 0:SEQ].bitcast(F32), ALU.subtract).then_inc(s("oh_lo"), 1)

            dve.wait_ge(s("q_ready"), CREDIT + 8 * l + 8)
            dve.wait_ge(s("own_zero"), 2 * l + 1)
            dve.tensor_copy(qB[:].rearrange("p k (b x) -> p k b x", b=DEC_B)[:, :, :, 0:DEC_T],
                            mT[:, :, SEQ:T].rearrange("p k (b t) -> p k b t", t=DEC_T)).then_inc(s("own_dve"), 1)
            for b in range(DEC_B):
                take_keys(dve, l, b, False)
                if b < 4:
                    maxima(b)
                if 1 <= b <= 4:
                    shares(b - 1)
                if b == 7:
                    heads_low(0)
            maxima(XH)
            heads_low(1)
            shares(XH)
            heads_low(2)
            dve.wait_ge(s("pB_act"), l + 1)
            dve.tensor_copy(own_tokens(pB[:, 1, :], P), ps[:, 7, P:2 * P].rearrange("p (h b t) -> p b h t", h=XH, t=DEC_T)) \
                .then_inc(s("own_dve"), 1)
            heads_low(3)
            dve.wait_ge(s("oh_hi"), 5 * l + 5)
            dve.tensor_tensor(sample_heads(hl), ps[:, 7, 0:XD].rearrange("p (d h i) -> p h d i", d=2, h=XH),
                              sample_heads(hh).bitcast(F32), ALU.subtract).then_inc(s("oh_lo"), 1)

        def pe_even(pe, l):
            g = G["in", l]
            products(pe, g, normed, s("in_even"), CREDIT, i1=4)
            pe.wait_ge(s("in_even"), CREDIT + 16)
            products(pe, g, normed, s("in_even"), CREDIT, i0=4, i1=5, drained=True)
            pe.wait_ge(s("vn_ready"), 1)
            pe.wait_ge(root_ready, 1)
            pe.matmul(ps[:, BN, 0:T], ones[:], acc[:, 0, :], start=True, stop=False)
            pe.matmul(ps[:, BN, 0:T], ones[:], acc[:, 1, :], start=False, stop=True).then_inc(s("v_ps"), 1)
            pe.wait_ge(s("sct_ready"), 2)
            pe.wait_ge(s("v_sq"), 5)
            transpose(pe, ps[0:8, BN, 0:P], sctP[:].rearrange("p t j -> p (t j)"))
            transpose(pe, ps[0:64, BN, P:2 * P], sctS[:].rearrange("p t r -> p (t r)")).then_inc(s("v_ps"), 1)
            pe.wait_ge(s("gT_ready"), 5)
            pe.wait_ge(s("vn_ready"), 6)
            for c in range(3):
                n = P if c < 2 else NS
                for t in range(4):
                    tr = transpose(pe, ps[0:n, 5 + c, t * P:(t + 1) * P], v[:, t, c * P:c * P + n])
                tr.then_inc(s("v_ps"), 1)
            pe.wait_ge(s("vnat_ready"), 3)
            pe.wait_ge(s("zz_main"), 4)
            for t in range(4):
                cut = slice(t * P, (t + 1) * P)
                for c in range(2):
                    pe.matmul(ps[:, t, c * CHUNK:(c + 1) * CHUNK], vnat[:, c, cut], sgT[:, t, :], start=True, stop=True)
                pe.matmul(ps[:, t, SEQ:T], vnat[0:NS, 2, cut], bdT[0:NS, t, :], start=True, stop=True).then_inc(s("mix_ps"), 1)
            pe.wait_ge(s("even_lo"), 8)

        def pe_odd(pe, l):
            g = G["in", l]
            products(pe, g, normed, s("z_ready"), CREDIT, i0=0, i1=4)

            def naturals(i, idx):
                if idx or i == 4:
                    return
                for t in range(4):
                    e = 4 * (i - 5) + t
                    pe.wait_ge(s("v4T_ready"), e + 1)
                    if e >= 2:
                        pe.wait_ge(s("vR_ready"), e - 1)
                    bank = 5 + e % 2
                    for c in range(2):
                        transpose(pe, ps[:, bank, c * P:(c + 1) * P], vt[:, t, c * P:(c + 1) * P])
                    transpose(pe, ps[:, bank, 2 * P:3 * P], v4T[:, t, :, :].rearrange("p r i -> p (r i)")).then_inc(s("vR_ps"), 1)
                pe.wait_ge(s("vR_ps"), 4 * (i - 5) + 4)
                pe.sem_inc(s("vt_used"), 4)
            for i in range(4, 9):
                products(pe, g, normed, s("z_ready"), CREDIT, i0=i, i1=i + 1, hook=naturals)
            pe.wait_ge(s("kdup"), 1)
            for h in range(RH):
                for dt in range(2):
                    mm = pe.matmul(ps[0:64, 7, h * NS:(h + 1) * NS], k4T[:, 2 * h + dt, 0:2, :].rearrange("p r i -> p (r i)"),
                                   mT[:, 2 * h + dt, SEQ:T], start=dt == 0, stop=dt == 1)
            mm.then_inc(s("scS_ps"), 1)
            products(pe, g, normed, s("z_ready"), CREDIT, i0=9, i1=10)
            products(pe, g, normed, s("z_ready"), CREDIT, i0=10, i1=11)
            pe.wait_ge(s("k4T_full"), 1)
            pe.wait_ge(s("vR_ready"), 16)
            for r in range(2):
                for k in range(4):
                    tr = transpose(pe, ps[:, 5 + r, k * P:(k + 1) * P], k4T[:, 4 * r + k, :, :].rearrange("p r i -> p (r i)"))
                tr.then_inc(s("k4_ps"), 1)
            products(pe, g, normed, s("z_ready"), CREDIT, i0=11, i1=12)
            pe.wait_ge(s("K4_ready"), 2)
            for n in range(4):
                c, hf = divmod(n, 2)
                if n >= 2:
                    pe.wait_ge(s("kR_ready"), n - 1)
                for k in range(4):
                    t = 4 * hf + k
                    tr = transpose(pe, ps[:, 5 + n % 2, k * P:(k + 1) * P], sq[:, t, c * P:(c + 1) * P])
                tr.then_inc(s("kR_ps"), 1)
            pe.wait_ge(s("scS_ready"), 1)
            for h in range(RH):
                pe.matmul(ps[h * NS:(h + 1) * NS, BN, :], scS[0:64, h, :], V4[0:64, h * RDV:(h + 1) * RDV].bitcast(F32),
                          start=True, stop=False, skip_group_check=True, tile_position=(0, h * NS))

            def sample_states(b, tiles):
                for k in tiles:
                    h = k // 2
                    n = 8 * b + k
                    pe.wait_ge(s(f"SR_in{h}"), 16 * b + 16)
                    pe.matmul(ps[h * NS:(h + 1) * NS, BN, :], QM[:, k, b * NS:(b + 1) * NS], state(h)[:, k % 2, :], start=False,
                              stop=b == DEC_B - 1 and k % 2 == 1, skip_group_check=True, tile_position=(0, h * NS))
                    if k == 0:
                        pe.wait_ge(s("K4m_ready"), b + 1)
                    if n >= 2:
                        pe.wait_ge(s("SR_new"), n - 1)
                    pe.matmul(ps[:, 2 + k % 2, :], K4m[:, b % 2, k * P:(k + 1) * P], V4[:, h * RDV:(h + 1) * RDV],
                              start=True, stop=True).then_inc(s("SU_ps"), 1)

            pe.wait_ge(s("z_ready"), CREDIT + 48)
            pe.wait_ge(s("kR_ready"), 4)
            pe.wait_ge(s("QM_step"), 3)
            for n, (h, c) in enumerate(UNITS):
                tok = slice(c * CHUNK, (c + 1) * CHUNK)
                if n:
                    pe.wait_ge(s("rs_ready"), n)
                for dt in range(2):
                    mm = pe.matmul(ps[:, 5, 0:P], sq[:, 2 * h + dt, tok], mT[:, 2 * h + dt, tok], start=dt == 0, stop=dt == 1)
                mm.then_inc(s("rs_ps"), 1)
                sample_states(n, (0, 1))
                if n:
                    if c == 1:
                        pe.wait_ge(s("S1_ready"), h + 1)
                    else:
                        pe.wait_ge(s("S2_ready"), 2 * h)
                for dt in range(2):
                    pe.matmul(ps[:, dt, :], kR[:, c, h * RDK + dt * P:h * RDK + dt * P + P], vR[:, c, h * RDV:(h + 1) * RDV],
                              start=True, stop=True).then_inc(s("S_ps"), 1)
                sample_states(n, (2, 3))
                pe.wait_ge(s("rs_ready"), n + 1)
                if n:
                    pe.wait_ge(s("rn_ready"), n)
                mm = pe.matmul(ps[:, 6, :], scr[:, n % 2, :], vR[:, c, h * RDV:(h + 1) * RDV], start=True, stop=c == 0)
                if c == 1:
                    pe.wait_ge(s("qd_ready"), h + 1)
                    pe.wait_ge(s("S1_ready"), h + 1)
                    for dt in range(2):
                        mm = pe.matmul(ps[:, 6, :], qd[:, dt, :], S1[:, dt, :], start=False, stop=dt == 1)
                mm.then_inc(s("ro_ps"), 1)
                sample_states(n, (4, 5, 6, 7))
                pe.wait_ge(s("rn_ready"), n + 1)
                if n:
                    pe.wait_ge(s("rg_ready"), n)
                for k in range(4):
                    tr = transpose(pe, ps[:, 7, k * P:(k + 1) * P], rn[:, k * P:(k + 1) * P])
                tr.then_inc(s("rT_ps"), 1)
            pe.wait_ge(s("rn_ready"), 9)
            pe.wait_ge(s("rg_ready"), 8)
            for k in range(4):
                tr = transpose(pe, ps[:, 7, k * P:(k + 1) * P], rn[:, k * P:(k + 1) * P])
            tr.then_inc(s("rT_ps"), 1)
            pe.wait_ge(s("rg_lo"), 10)

        def pe_attention(pe, l):
            def keys(b):
                pe.wait_ge(s(f"cache{b % 4}"), 64 * l + 16 * (b // 4) + 16)
                for r in range(4):
                    n = 4 * b + r
                    if n >= 3:
                        pe.wait_ge(s("kTb_dve" if (n - 3) % 2 else "kTb_act"), 16 * l + (n - 3) // 2 + 1)
                    for t in (2 * r, 2 * r + 1):
                        for m in range(2):
                            c = (t % 2) * N_MEM + m * P
                            tr = transpose(pe, ps[:, KBANKS[n % 3], c:c + P], ring[:, b % 4, m, t * P:(t + 1) * P])
                    tr.then_inc(s("kTb_ps"), 1)

            def sample_scores(b):
                pe.wait_ge(s("kTb_act"), 16 * l + 2 * b + 2)
                pe.wait_ge(s("kTb_dve"), 16 * l + 2 * b + 2)
                if b == 0:
                    pe.wait_ge(s("own_dve"), 2 * l + 1)
                for t in range(DT):
                    h = t // 2
                    mm = pe.matmul(ps[h * NS:(h + 1) * NS, 5, 0:N_MEM], qB[:, t, b * NS:(b + 1) * NS], kTb[:, b % 2, t, :],
                                   start=b == 0 and t % 2 == 0, stop=b == DEC_B - 1 and t % 2 == 1,
                                   skip_group_check=True, tile_position=(0, h * NS))
                mm.then_inc(s("sS_mm"), 1)

            def turn_shares(h):
                pe.wait_ge(s("p_ready"), 9 * l + 2 * h + 2)
                for m in range(2):
                    for tt in range(2):
                        tr = transpose(pe, ps[:, h, m * SEQ + tt * P:m * SEQ + (tt + 1) * P], pr[:, 2 * h + tt, m * P:(m + 1) * P])
                tr.then_inc(s("pT_ps"), 1)

            def values(h):
                pe.wait_ge(s("pT_ready"), 4 * l + h + 1)
                for dt in range(2):
                    for m in range(2):
                        mm = pe.matmul(ps[:, h, dt * SEQ:(dt + 1) * SEQ], vN[:, m, (2 * h + dt) * P:(2 * h + dt + 1) * P],
                                       prT[:, h, m, :], start=m == 0, stop=m == 1)
                mm.then_inc(s("o_ps"), 1)

            pe.wait_ge(s("q_ready"), CREDIT + 8 * l + 8)
            pe.wait_ge(s("kT_ready"), 4 * l + 4)
            for h in range(XH):
                for tt in range(2):
                    for dt in range(2):
                        mm = pe.matmul(ps[:, h, tt * N_MEM:(tt + 1) * N_MEM], mT[:, 2 * h + dt, tt * P:(tt + 1) * P],
                                       kT[:, 2 * h + dt, :], start=dt == 0, stop=dt == 1)
                mm.then_inc(s("sc_ps"), 1)
            keys(0)
            for b in range(DEC_B):
                if b < DEC_B - 1:
                    keys(b + 1)
                if b >= 4:
                    turn_shares(b - 4)
                sample_scores(b)
                if b >= 5:
                    values(b - 5)
            values(3)
            pe.wait_ge(s("p_ready"), 9 * l + 9)
            for m in range(2):
                tr = transpose(pe, ps[:, 7, m * P:(m + 1) * P], pS[:, m * P:(m + 1) * P])
            tr.then_inc(s("pT_ps"), 1)
            pe.wait_ge(s("pB_act"), l + 1)
            pe.wait_ge(s("own_dve"), 2 * l + 2)
            for b in range(DEC_B):
                n = DEC_B + b
                pe.wait_ge(s(f"cache{n % 4}"), 64 * l + 16 * (n // 4) + 16)
                for h in range(XH):
                    for m in range(2):
                        mm = pe.matmul(ps[h * NS:(h + 1) * NS, 6, 0:XD], pB[:, m, b * P + h * NS:b * P + (h + 1) * NS],
                                       ring[:, n % 4, m, h * XD:(h + 1) * XD], start=b == 0 and m == 0,
                                       stop=b == DEC_B - 1 and m == 1, skip_group_check=True, tile_position=(0, h * NS))
                mm.then_inc(s("oS_mm"), 1)
            pe.wait_ge(s("oS_out"), l + 1)
            for d in range(2):
                tr = transpose(pe, ps[:, 7, d * P:(d + 1) * P], pS[:, d * P:(d + 1) * P])
            tr.then_inc(s("o_ps"), 1)

        block = ctx.enter_context(nc.Block())

        @block.sync
        def _(sp):
            sp.dma_start(ident[:], a["c_ident"]).then_inc(s("x_in"), 16)
            sp.dma_start(xn[:, 0:2, :], a["x_prompt"][0].rearrange("(r p) d -> p r d", p=P)).then_inc(s("x_in"), 16)
            sp.dma_start(xn[0:NS, 2, :], a["x_sample"].rearrange("b t d -> (b t) d")).then_inc(s("x_in"), 16)
            rows = 0
            for l in L:
                for name in ("norm_mix_pre", "norm_mix_post", "norm_x_pre", "norm_x_post",
                             "norm_ffn_pre", "norm_ffn_post", "norm_mem"):
                    sp.dma_start(rowsn[rows:rows + DT, :], a[name][l].rearrange("(t p) -> t p", p=P)).then_inc(s("gain_in"), 16)
                    rows += DT
            sp.dma_start(rowsn[rows:rows + 4, :], a["sgu_vnorm"][0].rearrange("(t p) -> t p", p=P)).then_inc(s("gain_in"), 16)
            for j in range(3):
                sp.dma_start(rowsn[rows + 4 + 4 * j:rows + 8 + 4 * j, :],
                             a["conv_short"][0, j].rearrange("(t p) -> t p", p=P)).then_inc(s("gain_in"), 16)
            sp.sem_inc(landed[0], 16)
            sp.sem_inc(landed[1], 16)
            for g in order:
                load_weights(sp, g)

        @block.gpsimd
        def _(pool):
            stores[0] = 0

            def store(dst, src):
                pool.dma_start(dst, src).then_inc(s("stored"), 16)
                stores[0] += 16

            cf = a["conv_ffn"].rearrange("l j (t p) -> (l j t) p", p=P)
            pool.dma_start(cwn[:, 0:2, :], cf[0:2 * P].rearrange("(r p) c -> p r c", p=P)).then_inc(s("taps_in"), 16)
            pool.dma_start(cwn[0:8, 2, :], cf[2 * P:2 * P + 8]).then_inc(s("taps_in"), 16)
            pool.dma_start(sgn[:], a["sgu_w"][0].rearrange("g t s -> t g s")).then_inc(s("sgu_in"), 16)
            pool.memset(bdn[0:NS], 0.0).then_inc(s("bd_zero"), 1)
            pool.wait_ge(s("bd_zero"), 1)
            for b in range(DEC_B):
                r = slice(DEC_T * b, DEC_T * b + DEC_T)
                pool.dma_start(bdn[r, :, r], a["sgu_w"][0, :, 0:DEC_T, 0:DEC_T]
                               .rearrange("g t s -> t g s")).then_inc(s("bd_in"), 16)
            bias = a["sgu_b"][0]
            for c in range(SEQ // CHUNK):
                pool.dma_start(sbias[:, :, c * CHUNK:(c + 1) * CHUNK],
                               bias.unsqueeze(0).to_broadcast([P, 4, CHUNK])).then_inc(s("bias_in"), 16)
            for b in range(DEC_B):
                c = SEQ + DEC_T * b
                pool.dma_start(sbias[:, :, c:c + DEC_T],
                               bias[:, 0:DEC_T].unsqueeze(0).to_broadcast([P, 4, DEC_T])).then_inc(s("bias_in"), 16)
            pool.dma_start(scn[0:64, :], a["state_shortconv"][0].rearrange("b j (t p) -> t (b j) p", p=P)).then_inc(s("taps_in"), 16)
            pool.wait_ge(s("sgu_in"), 16)
            pool.affine_select(out=sgn[:], in_=sgn[:], compare_op=ALU.is_ge, fill=0.0, base=0,
                               pattern=[[0, 4], [-1, P]], channel_multiplier=1).then_inc(s("sgu_masked"), 1)
            pool.wait_ge(s("bd_in"), 16 * DEC_B)
            pool.affine_select(out=bdn[0:NS], in_=bdn[0:NS], compare_op=ALU.is_ge, fill=0.0, base=0,
                               pattern=[[0, 4], [-1, NS]], channel_multiplier=1).then_inc(s("sgu_masked"), 1)

            pool.wait_ge(s("vnat_ready"), 3)
            store(sgu_v[0].rearrange("b t d -> (b t) d"), vnat[0:NS, 2, :])
            pool.wait_ge(s("sco_ready"), 1)
            store(sc_prompt[0, 0].rearrange("j (t p) -> t j p", p=P), sco[0:8, 0, :])
            store(sc_sample[0].rearrange("b j (t p) -> t (b j) p", p=P), sco[0:64, 1, :])

            for l in L:
                q = 3 * l + 1
                if l == 1:
                    pool_retention(pool, store)
                if l == 0:
                    pool.wait_ge(s("stored"), stores[0])
                    pool.wait_ge(s("even_lo"), 8)
                else:
                    pool.wait_ge(w_used, CREDIT + 2 * (G["out", l].first + G["out", l].chunks))
                pool.dma_start(memn[:], a["mem_prompt"][0].rearrange("(r p) d -> p r d", p=P)).then_inc(s("mem_in"), 16)

                def cache(n):
                    src = a["cache_mem_k" if n < DEC_B else "cache_mem_v"][l, n % DEC_B]
                    pool.dma_start(ring[:, n % 4], src.rearrange("(r p) h d -> p r (h d)", p=P)).then_inc(s(f"cache{n % 4}"), 16)
                for n in range(4):
                    cache(n)
                pool.memset(qB[:], 0.0).then_inc(s("own_zero"), 1)
                pool.wait_ge(s("k_nat"), CREDIT + 8 * l + 8)
                pool.dma_start(mem_k[l, 0].rearrange("(r p) h d -> p r (h d)", p=P), kN[:]).then_inc(s("kv_stored"), 16)
                pool.wait_ge(s("v_nat"), CREDIT + 8 * l + 8)
                pool.dma_start(mem_v[l, 0].rearrange("(r p) h d -> p r (h d)", p=P), vN[:]).then_inc(s("kv_stored"), 16)
                pool.wait_ge(s("sc_ps"), 4 * l + 4)
                pool.memset(pB[:], 0.0).then_inc(s("own_zero"), 1)
                for n in range(4, 2 * DEC_B):
                    if n - 4 < DEC_B:
                        pool.wait_ge(s("kTb_ps"), 32 * l + 4 * (n - 3))
                    else:
                        pool.wait_ge(s("oS_mm"), 8 * l + n - 4 - DEC_B + 1)
                    cache(n)

                pool.wait_ge(s("oh_lo"), 5 * l + 5)
                pool.wait_ge(s("oS_mm"), 8 * l + 8)
                pool.wait_ge(s("kv_stored"), 32 * l + 32)
                rows = a["state_ffn_conv"][l].rearrange("b j (t p) -> t (b j) p", p=P)
                for r in range(6):
                    n = min(8, 2 * FT - 8 * r)
                    pool.dma_start(stn[0:16 * n, r, :], rows[8 * r:8 * r + n]).then_inc(s("st_in"), 16)
                pool.wait_ge(s("stT_ready"), 2 * l + 2)

                def prefix(i):
                    for t in range(4):
                        pool.wait_ge(s("conv_done"), i * 4 + 44 * l + t + 1)
                        pool.tensor_copy(zb[:, t, PG:, 0:2],
                                         stT[:, bass.ds(i * 2 + FT * (t // 2) + t % 2, 1), :]
                                         .rearrange("p o (b j) -> p (o b) j", j=2)).then_inc(s("prefix"), 1)
                    for t in range(4):
                        pool.wait_ge(s("conv_in"), CREDIT + i * 4 + 44 * l + t + 1)
                        col = i * 2 + FT * (t // 2) + t % 2
                        pool.tensor_copy(tlS[:, bass.ds(col, 1), :].rearrange("p o (b j) -> p (o b) j", j=2),
                                         zb[:, t, PG:, 4:6])
                        pool.tensor_copy(tlP[:, bass.ds(col, 1), :], zb[:, t, PG - 1:PG, 4:6]).then_inc(s("tails"), 1)
                with pool.Fori(0, G["up", l].steps) as i:
                    prefix(i)
                pool.wait_ge(s("tlo_ready"), 2 * l + 2)
                rows = fc_sample[l].rearrange("b j (t p) -> t (b j) p", p=P)
                for r in range(6):
                    n = min(8, 2 * FT - 8 * r)
                    store(rows[8 * r:8 * r + n], tlo[0:16 * n, r, :])
                store(fc_prompt[l, 0].rearrange("j (t p) -> t j p", p=P), tlo[0:4 * FT, 6, :])
                pool.wait_ge(s("stored"), stores[0])

            pool.wait_ge(s("y_out"), 6)
            store(y_prompt[0].rearrange("(r p) d -> p r d", p=P), yn[:, 0:2, :])
            store(y_sample.rearrange("b t d -> (b t) d"), yn[0:NS, 2, :])
            pool.wait_ge(s("stored"), stores[0])

        @block.scalar
        def _(act):
            for t in range(DT):
                act.wait_ge(s("xt_ps"), t + 1)
                act.activation(xT[:, t, :], ps[:, t % 4, 0:T], ACT.Copy).then_inc(x_ready, 1)
            act.wait_ge(s("const_ps"), 1)
            act.activation(gT[:], ps[:, 5, 0:P], ACT.Copy).then_inc(s("gT_ready"), 1)
            act.wait_ge(s("const_ps"), 2)
            act.activation(cwT[:, 0:2 * P + 8], ps[:, 6, 0:2 * P + 8], ACT.Copy).then_inc(s("gT_ready"), 1)
            act.wait_ge(s("const_ps"), 3)
            act.activation(sgT[:], ps[:, 7, :].rearrange("p (g t) -> p g t", g=4), ACT.Copy).then_inc(s("gT_ready"), 1)
            act.wait_ge(s("const_ps"), 4)
            act.activation(bdT[0:NS], ps[0:NS, 5, 128:256].rearrange("p (g t) -> p g t", g=4), ACT.Copy).then_inc(s("gT_ready"), 1)
            act.activation(scT[:], ps[:, 5, 256:320], ACT.Copy).then_inc(s("gT_ready"), 1)
            act.wait_ge(s("set_up"), 2)
            for c in range(2):
                split(act, order[0], 0, c, True)

            for l in L:
                q = 3 * l
                if l == 0:
                    act.wait_ge(s("gT_ready"), 1)
                pre_act(act, q)
                (act_even if l % 2 == 0 else act_odd)(act, l)
                branch_out_act(act, G["out", l], q)
                post_act(act, q)

                act.wait_ge(s("mem_in"), 16 * l + 16)
                for r in range(2):
                    act.activation(kN[:, r, :], memn[:, r, :], ACT.Square,
                                   accum_out=small[:, 1 + r:2 + r]).then_inc(s("mem_sq"), 1)
                act.wait_ge(s("mem_sq"), 2 * l + 2)
                act.activation(small[:, 3:5], small[:, 1:3], ACT.Sqrt, bias=eps_col, scale=1.0 / D).then_inc(s("mem_root"), 1)
                for t in range(DT):
                    act.wait_ge(s("memT_ps"), 4 * l + t // 2 + 1)
                    act.activation(mh[:, t, :], ps[:, 5 + t // 2 % 3, (t % 2) * N_MEM:(t % 2 + 1) * N_MEM],
                                   ACT.Copy, scale=memgain(l, t)).then_inc(s("mem_hi"), 1)
                for name, dst in (("k", kN), ("v", vN)):
                    def evac(i, half, g=G[name, l], dst=dst, name=name):
                        for j in range(2):
                            tiles_ready(act, g, i, half, j)
                            act.activation(dst[:, j, bass.ds(i * 2 * CW + half * CW, CW)],
                                           ps[:, 2 * half + j, 0:CW], ACT.Copy).then_inc(s(f"{name}_nat"), 1)
                    run(act, G[name, l], True, evac)
                    if name == "k":
                        pre_act(act, q + 1)
                for r in range(4):
                    act.wait_ge(s("kT_ps"), 4 * l + r + 1)
                    act.activation(kT[:, 2 * r:2 * r + 2, :],
                                   ps[:, 5 + r % 3, :].rearrange("p (t m) -> p t m", t=2), ACT.Copy).then_inc(s("kT_ready"), 1)

                def evac(i, half, g=G["q", l]):
                    if not isinstance(i, int) or i == 0:
                        act.wait_ge(h_lo, DT * (q + 2))
                    for j in range(2):
                        tiles_ready(act, g, i, half, j)
                        act.activation(mT[:, i * 4 + (2 * half + j), :], ps[:, 2 * half + j, 0:T],
                                       ACT.Copy).then_inc(s("q_ready"), 1)
                run(act, G["q", l], True, evac)
                act_attention(act, l)
                branch_out_act(act, G["o", l], q + 1)
                post_act(act, q + 1)

                act.wait_ge(s("kv_stored"), 32 * l + 32)
                pre_act(act, q + 2)
                for r in range(2):
                    act.wait_ge(s("stT_ps"), 2 * l + r + 1)
                    n = (32, 12)[r]
                    act.activation(stT[:, 32 * r:32 * r + n, :],
                                   ps[:, 5 + r, 0:16 * n].rearrange("p (t r) -> p t r", r=16), ACT.Copy).then_inc(s("stT_ready"), 1)

                def evac(i, half, g=G["up", l]):
                    for j in range(2):
                        t = 2 * half + j
                        tiles_ready(act, g, i, half, j)
                        act.wait_ge(s("conv_done"), i * 4 + 44 * l + t + 1)
                        act.wait_ge(s("tails"), i * 4 + 44 * l + t + 1)
                        act.wait_ge(s("prod"), i * 2 + 22 * l + 2)
                        src = groups(ps[:, t, 0:T])
                        act.activation(zb[:, t, :, 2:PAD], src, ACT.Copy)
                        act.activation(zb[:, t, 1:PG, 0:2], src[:, 0:PG - 1, 2:4], ACT.Copy)
                        act.activation(cb[:, t, :], ps[:, t, 0:T], ACT.Copy,
                                       scale=ftap(l, 2, i * 2 + FT * half + j)).then_inc(s("conv_in"), 1)
                    if half == 0:
                        return
                    for j in range(2):
                        act.wait_ge(s("conv_done"), CREDIT + i * 4 + 44 * l + j + 1)
                        act.activation(ge[:, j, :], cb[:, j, :], ACT.Gelu_apprx_tanh).then_inc(s("gelu"), 1)
                    for j in range(2):
                        act.wait_ge(s("prod"), i * 2 + 22 * l + j + 3)
                        act.activation(aH[:, i * 2 + j, :], pd[:, j, :], ACT.Copy).then_inc(s("a_hi"), 1)
                run(act, G["up", l], True, evac)
                for r in range(3):
                    act.wait_ge(s("tlo_ps"), 2 * l + min(r, 1) + 1)
                    if r == 0:
                        act.activation(tlo[:, 0:4, :], ps[:, 5, :].rearrange("p (r c) -> p r c", c=P), ACT.Copy)
                    elif r == 1:
                        act.activation(tlo[:, 4, :], ps[:, 6, 0:P], ACT.Copy)
                        act.activation(tlo[0:64, 5, :], ps[0:64, 6, P:2 * P], ACT.Copy).then_inc(s("tlo_ready"), 1)
                    else:
                        act.activation(tlo[0:4 * FT, 6, :], ps[0:4 * FT, 6, 2 * P:3 * P], ACT.Copy).then_inc(s("tlo_ready"), 1)
                branch_out_act(act, G["down", l], q + 2)
                post_act(act, q + 2)

            for r in range(3):
                n = P if r < 2 else NS
                for half in range(2):
                    act.wait_ge(s("y_ps"), 2 * r + half + 1)
                    ins = act.activation(yn[0:n, r, 512 * half:512 * half + 512], ps[0:n, 2 * (r % 2) + half, :], ACT.Copy)
                    ins.then_inc(s("y_out"), 1)

        @block.vector
        def _(dve):
            dve.memset(ones[:], 1.0).then_inc(s("set_up"), 1)
            dve.memset(small[:, 0:1], EPS).then_inc(s("set_up"), 1)
            dve.memset(zz[:, :, 0, 0:2], 0.0).then_inc(s("set_up"), 1)
            dve.sem_inc(lo_ready, CREDIT)
            for c in range(2):
                split(dve, order[0], 0, c, False)
            for l in L:
                q = 3 * l
                if l == 0:
                    dve.wait_ge(s("gT_ready"), 5)
                pre_dve(dve, q)
                (dve_even if l % 2 == 0 else dve_odd)(dve, l)
                run(dve, G["out", l], False, nothing)
                post_dve(dve, q)

                dve.wait_ge(s("mem_root"), l + 1)
                dve.reciprocal(small[:, 5:7], small[:, 3:5]).then_inc(s("mem_inv"), 1)
                dve.wait_ge(s("mem_inv"), l + 1)
                for r in range(2):
                    dve.tensor_scalar(memn[:, r, :], memn[:, r, :], small[:, 5 + r:6 + r], None,
                                      ALU.mult).then_inc(s("mem_scaled"), 1)
                for t in range(DT):
                    dve.wait_ge(s("mem_hi"), 8 * l + 2 * (t // 2) + 2)
                    dve.scalar_tensor_tensor(out=ml[:, t, :], in0=ps[:, 5 + t // 2 % 3, (t % 2) * N_MEM:(t % 2 + 1) * N_MEM],
                                             scalar=memgain(l, t), in1=mh[:, t, :].bitcast(F32), op0=ALU.mult,
                                             op1=ALU.subtract).then_inc(s("mem_lo"), 1)
                run(dve, G["k", l], False, nothing)
                pre_dve(dve, q + 1)
                run(dve, G["v", l], False, nothing)
                run(dve, G["q", l], False, nothing)
                dve_attention(dve, l)
                run(dve, G["o", l], False, nothing)
                post_dve(dve, q + 1)

                pre_dve(dve, q + 2)
                dve.memset(zb[:, :, 0, 0:2], 0.0).then_inc(s("zb_zero"), 1)

                def evac(i, half):
                    for j in range(2):
                        t = 2 * half + j
                        tile = i * 2 + FT * half + j
                        if half == 0 and j == 0:
                            dve.wait_ge(s("zb_zero"), l + 1)
                        dve.wait_ge(s("conv_in"), CREDIT + i * 4 + 44 * l + t + 1)
                        dve.wait_ge(s("prefix"), i * 4 + 44 * l + t + 1)
                        dve.scalar_tensor_tensor(out=groups(cb[:, t, :]), in0=zb[:, t, :, 1:5], scalar=ftap(l, 1, tile),
                                                 in1=groups(cb[:, t, :]), op0=ALU.mult, op1=ALU.add).then_inc(s("conv_mid"), 1)
                    for j in range(2):
                        t = 2 * half + j
                        tile = i * 2 + FT * half + j
                        dve.wait_ge(s("conv_mid"), i * 4 + 44 * l + t + 1)
                        dve.scalar_tensor_tensor(out=groups(cb[:, t, :]), in0=zb[:, t, :, 0:4], scalar=ftap(l, 0, tile),
                                                 in1=groups(cb[:, t, :]), op0=ALU.mult, op1=ALU.add).then_inc(s("conv_done"), 1)
                    if half == 0:
                        return
                    for j in range(2):
                        dve.wait_ge(s("gelu"), i * 2 + 22 * l + j + 1)
                        dve.wait_ge(s("conv_done"), CREDIT + i * 4 + 44 * l + 3 + j)
                        dve.wait_ge(s("a_lo"), i * 2 + 22 * l + j + 1)
                        dve.tensor_tensor(pd[:, j, :], ge[:, j, :], cb[:, 2 + j, :], ALU.mult).then_inc(s("prod"), 1)
                    for j in range(2):
                        dve.wait_ge(s("a_hi"), i * 2 + 22 * l + j + 1)
                        dve.tensor_tensor(aL[:, i * 2 + j, :], pd[:, j, :], aH[:, i * 2 + j, :].bitcast(F32),
                                          ALU.subtract).then_inc(s("a_lo"), 1)
                run(dve, G["up", l], False, evac)
                run(dve, G["down", l], False, nothing)
                post_dve(dve, q + 2)

        @block.tensor
        def _(pe):
            for name in ("in_even", "q_ready", "k_nat", "v_nat", "z_ready"):
                pe.sem_inc(s(name), CREDIT)
            for name in ("conv_in", "conv_done", "tails", "vt_used", "turned"):
                pe.sem_inc(s(name), CREDIT)
            for name in ("prod", "a_lo"):
                pe.sem_inc(s(name), 2)
            pe.sem_inc(sq_ready, CREDIT)
            pe.sem_inc(w_used, CREDIT)
            pe.wait_ge(s("x_in"), 48)
            for t in range(DT):
                if t >= 4:
                    pe.wait_ge(x_ready, t - 3)
                for r in range(3):
                    n = P if r < 2 else NS
                    tr = transpose(pe, ps[:, t % 4, r * P:r * P + n], xn[0:n, r, t * P:(t + 1) * P], n)
                tr.then_inc(s("xt_ps"), 1)
            pe.wait_ge(s("gain_in"), 16 * 18)
            transpose(pe, ps[:, 5, 0:P], rowsn[:]).then_inc(s("const_ps"), 1)
            pe.wait_ge(s("taps_in"), 48)
            for r in range(3):
                n = P if r < 2 else 8
                tr = transpose(pe, ps[:, 6, r * P:r * P + n], cwn[0:n, r, :], n)
            tr.then_inc(s("const_ps"), 1)
            pe.wait_ge(s("sgu_masked"), 2)
            for g in range(4):
                tr = transpose(pe, ps[:, 7, g * P:(g + 1) * P], sgn[:, g, :])
            tr.then_inc(s("const_ps"), 1)
            pe.wait_ge(s("gT_ready"), 1)
            for g in range(4):
                transpose(pe, ps[0:NS, 5, P + g * NS:P + (g + 1) * NS], bdn[0:NS, g, :], NS)
            transpose(pe, ps[:, 5, 2 * P:2 * P + 64], scn[0:64, :], 64).then_inc(s("const_ps"), 1)
            pe.wait_ge(s("set_up"), 1)

            for l in L:
                q = 3 * l
                pre_pe(pe, q)
                pe.wait_ge(h_lo, DT * (q + 1))
                if l == 0:
                    pe.wait_ge(x_ready, 8)
                (pe_even if l % 2 == 0 else pe_odd)(pe, l)
                if l % 2 == 0:
                    products(pe, G["out", l], normed, sq_ready, CREDIT + 8 * (2 * q + 1))
                else:
                    products(pe, G["out", l], lambda k: (hh[:, k, :], hl[:, k, :]) if k < 8 else
                             (h2h[:, k - 8, :], h2l[:, k - 8, :]), sq_ready, CREDIT + 8 * (2 * q + 1))
                ssq(pe, 2 * q + 1)

                pe.wait_ge(s("mem_scaled"), 2 * l + 2)
                for r in range(4):
                    if r == 3:
                        pe.wait_ge(s("mem_lo"), 8 * l + 2)
                    for t in (2 * r, 2 * r + 1):
                        for m in range(2):
                            c = (t % 2) * N_MEM + m * P
                            tr = transpose(pe, ps[:, 5 + r % 3, c:c + P], memn[:, m, t * P:(t + 1) * P])
                    tr.then_inc(s("memT_ps"), 1)
                pe.wait_ge(s("mem_lo"), 8 * l + 8)
                pe.wait_ge(sq_ready, CREDIT + 8 * (2 * q + 2))
                mem = lambda k: (mh[:, k, :], ml[:, k, :])
                products(pe, G["k", l], mem, s("k_nat"), CREDIT + 8 * l, natural=True)
                pre_pe(pe, q + 1)
                pe.wait_ge(s("k_nat"), CREDIT + 8 * l + 8)
                products(pe, G["v", l], mem, s("v_nat"), CREDIT + 8 * l, natural=True)
                for r in range(4):
                    if r == 3:
                        pe.wait_ge(s("kT_ready"), 4 * l + 1)
                    for t in (2 * r, 2 * r + 1):
                        for m in range(2):
                            c = (t % 2) * N_MEM + m * P
                            tr = transpose(pe, ps[:, 5 + r % 3, c:c + P], kN[:, m, t * P:(t + 1) * P])
                    tr.then_inc(s("kT_ps"), 1)

                pe.wait_ge(h_lo, DT * (q + 2))
                pe.wait_ge(s("v_nat"), CREDIT + 8 * l + 8)
                products(pe, G["q", l], normed, s("q_ready"), CREDIT + 8 * l)
                pe_attention(pe, l)
                pe.wait_ge(s("oh_lo"), 5 * l + 5)
                products(pe, G["o", l], normed, sq_ready, CREDIT + 8 * (2 * q + 3))
                ssq(pe, 2 * q + 3)

                for r in range(6):
                    n = min(8, 2 * FT - 8 * r) * 16
                    if r == 0:
                        pe.wait_ge(s("st_in"), 96 * l + 96)
                    tr = transpose(pe, ps[:, 5 + r // 4, (r % 4) * P:(r % 4) * P + n], stn[0:n, r, :], n)
                    if r in (3, 5):
                        tr.then_inc(s("stT_ps"), 1)
                pre_pe(pe, q + 2)
                pe.wait_ge(h_lo, DT * (q + 3))
                pe.wait_ge(sq_ready, CREDIT + 8 * (2 * q + 5))
                products(pe, G["up", l], normed, s("conv_in"), CREDIT + 44 * l)
                pe.wait_ge(s("a_lo"), 22 * l + 24)
                pe.wait_ge(s("tails"), CREDIT + 44 * l + 44)
                for r in range(7):
                    if r < 6:
                        n = min(8, 2 * FT - 8 * r) * 16
                        src = tlS[:, 8 * r:8 * r + n // 16, :].rearrange("p t r -> p (t r)")
                    else:
                        n = 4 * FT
                        src = tlP[:].rearrange("p t j -> p (t j)")
                    c = (r % 4) * P
                    tr = transpose(pe, ps[0:n, 5 + r // 4, c:c + P], src)
                    if r in (3, 6):
                        tr.then_inc(s("tlo_ps"), 1)
                pe.wait_ge(s("conv_in"), CREDIT + 44 * l + 44)
                products(pe, G["down", l], lambda k: (aH[:, k, :], aL[:, k, :]), sq_ready, CREDIT + 8 * (2 * q + 5))
                pe.wait_ge(w_used, CREDIT + 2 * (G["down", l].first + G["down", l].chunks))
                pe.sem_inc(s("a_free"), 1)
                ssq(pe, 2 * q + 5)

            pe.wait_ge(x_ready, 8 * 7)
            for r in range(3):
                n = P if r < 2 else NS
                for half in range(2):
                    if r == 2:
                        pe.wait_ge(s("y_out"), half + 1)
                    for t in range(4):
                        tr = transpose(pe, ps[0:n, 2 * (r % 2) + half, t * P:(t + 1) * P],
                                       xT[:, 4 * half + t, r * P:r * P + n])
                    tr.then_inc(s("y_ps"), 1)

def constants():
    f = np.float32
    half = RDK // 2
    pos = np.concatenate([np.arange(SEQ), np.tile(PAST + np.arange(DEC_T), DEC_B)]).astype(f)
    inv = f(10000.0) ** (-np.arange(half, dtype=f) / f(half))
    ang = inv[:, None] * pos[None, :]
    rope = np.stack([np.cos(ang), np.sin(ang)], axis=1).astype(f)
    lg = np.log1p(-np.exp2(f(-5) - np.arange(RH, dtype=f))).astype(f)
    sc = f(RDK ** -0.5)

    def decay(n, h):
        d = np.arange(n, dtype=f)[None, :] - np.arange(n, dtype=f)[:, None]
        return np.where(d >= 0, np.exp(lg[h] * np.maximum(d, 0)), 0).astype(f) * sc

    ret = np.zeros((P, 8 * P + 4), f)
    retS = np.zeros((P, 12 * NS + 8), f)
    tok = np.arange(NS)
    same = (tok[:, None] // DEC_T == tok[None, :] // DEC_T)
    for h in range(RH):
        ret[:, h * P:(h + 1) * P] = decay(CHUNK, h)
        ret[:, (4 + h) * P:(5 + h) * P] = np.exp(lg[h] * (np.arange(CHUNK, dtype=f) + 1)) * sc
        ret[:, 8 * P + h] = np.exp(lg[h] * (CHUNK - 1 - np.arange(CHUNK, dtype=f)))
        small = np.tile(decay(DEC_T, h), (DEC_B, DEC_B)) * same
        retS[0:2 * NS, h * NS:(h + 1) * NS] = np.tile(small, (2, 1))
        retS[:, (4 + h) * NS:(5 + h) * NS] = np.exp(lg[h] * (tok % DEC_T + 1).astype(f)) * sc
        retS[:, (8 + h) * NS:(9 + h) * NS] = np.exp(lg[h] * (DEC_T - 1 - tok % DEC_T).astype(f))
    for b in range(DEC_B):
        retS[:, 12 * NS + b] = (np.arange(P) % NS) // DEC_T == b
    return {"c_ident": np.eye(P, dtype=f), "c_rope": rope, "c_ret": ret, "c_retS": retS}


OUTS = [(1, SEQ, D), (DEC_B, DEC_T, D), (DEPTH, 1, N_MEM, XH, XD), (DEPTH, 1, N_MEM, XH, XD),
        (1, 1, 2, 512), (1, DEC_B, 2, 512), (1, DEC_B, DEC_T, 512), (1, 1, RH, RDK, RDV),
        (1, DEC_B, RH, RDK, RDV), (DEPTH, 1, 2, 2 * DFF), (DEPTH, DEC_B, 2, 2 * DFF)]


def kernel(**inputs):
    import concourse.bacc as bacc
    from concourse.bass_utils import run_bass_kernel_spmd

    nc = bacc.Bacc("TRN2", target_bir_lowering=False, num_devices=1)
    arrays = {k: np.ascontiguousarray(v) for k, v in inputs.items()}
    arrays.update(constants())
    a = {k: nc.dram_tensor(k, v.shape, F32, kind="ExternalInput").ap() for k, v in arrays.items()}
    outs = [nc.dram_tensor(f"out_{i}", shape, F32, kind="ExternalOutput").ap() for i, shape in enumerate(OUTS)]
    build(nc, a, outs)
    r = run_bass_kernel_spmd(nc, [arrays], core_ids=[0]).results[0]
    return tuple(r[f"out_{i}"] for i in range(len(OUTS)))
```

```python
from contextlib import ExitStack

import numpy as np
import concourse.bass as bass
from concourse import mybir

F32 = mybir.dt.float32
F32R = mybir.dt.float32r
ACT = mybir.ActivationFunctionType
ALU = mybir.AluOpType
AX = mybir.AxisListType

P = 128
D = 1024
DT = D // P
SEQ, DEC_B, DEC_T = 256, 8, 4
NS = DEC_B * DEC_T
T = SEQ + NS
GRP = T // DEC_T
PG = SEQ // DEC_T
PAD = DEC_T + 2
CHUNK = 128
EPS = 1e-6
DEPTH = 2
N_MEM, XH, XD = 256, 4, 256
DFF = 2816
FT = DFF // P
RH, RDK, RDV = 4, 256, 512
PAST = 2048
CREDIT = 4
CW = 256


class Gemm:

    def __init__(self, name, w, ks, first, cols=None):
        self.name, self.w, self.ks, self.first = name, w, ks, first
        self.nk = len(ks)
        self.per = 2 * self.nk
        self.ncols = w.shape[1]
        self.steps = self.ncols // (2 * CW)
        self.chunks = self.steps * self.per
        self.cols = cols or (lambda i, half: 2 * CW * i + CW * half)
        self.next = None

    def rows(self, idx):
        kc = idx % self.nk
        return sum(self.ks[:kc]), self.ks[kc]


def build(nc, a, outs):
    (y_prompt, y_sample, mem_k, mem_v, sc_prompt, sc_sample, sgu_v, ret_prompt, ret_sample,
     fc_prompt, fc_sample) = outs

    order = []

    def gemm(name, w, ks=(8,), cols=None):
        g = Gemm(name, w, list(ks), sum(x.chunks for x in order), cols)
        if order:
            order[-1].next = g
        order.append(g)
        return g

    G = {}
    for l in range(DEPTH):
        if l % 2 == 0:
            G["in", l] = gemm("in_even", a["w_in_even"][l // 2], (8,),
                              lambda i, half: (i * 3 + 3) % 5 * (2 * CW) + CW * half)
            G["out", l] = gemm("out_even", a["w_out_even"][l // 2])
        else:
            G["in", l] = gemm("in_odd", a["w_in_odd"][l // 2])
            G["out", l] = gemm("out_odd", a["w_out_odd"][l // 2], (8, 8))
        G["k", l] = gemm("xk", a["w_xk"][l])
        G["v", l] = gemm("xv", a["w_xv"][l])
        G["q", l] = gemm("xq", a["w_xq"][l])
        G["o", l] = gemm("xo", a["w_xo"][l])
        G["up", l] = gemm("up", a["w_ffn_up"][l], (8,), lambda i, half: CW * i + DFF * half)
        G["down", l] = gemm("down", a["w_ffn_down"][l], (6, 6, 5, 5))

    ctx = ExitStack()
    with ctx:
        def sb(name, shape, dt=F32, scope=ctx):
            return scope.enter_context(nc.sbuf_tensor(name, [P] + shape, dt))

        def sem(name):
            return ctx.enter_context(nc.semaphore(name))

        raw = sb("raw", [4, 8, CW])
        wh = sb("wh", [2, 8, CW], F32R)
        wl = sb("wl", [2, 8, CW], F32R)
        xT = sb("xT", [DT, T])
        hh = sb("hh", [DT, T], F32R)
        hl = sb("hl", [DT, T], F32R)
        mT = sb("mT", [DT, T])
        sq = sb("sq", [DT, T])
        acc = sb("acc", [2, T])
        root = sb("root", [T])
        rstd = sb("rstd", [T])
        ident = sb("ident", [P])
        ones = sb("ones", [P])
        rowsn = sb("rowsn", [P])
        gT = sb("gT", [P])
        cwT = sb("cwT", [3 * P])
        small = sb("small", [64])

        ev = ExitStack()
        bh = sb("bh", [4, T], F32R, ev)
        bl = sb("bl", [4, T], F32R, ev)
        u = sb("u", [4, T], F32, ev)
        v = sb("v", [4, T], F32, ev)
        bg = sb("bg", [4, T], F32, ev)
        cg = sb("cg", [4, T], F32, ev)
        zz = sb("zz", [4, GRP, PAD], F32, ev)
        cv = sb("cv", [4, T], F32, ev)
        av = sb("av", [4, T], F32, ev)
        vnat = sb("vnat", [3, 4 * P], F32, ev)
        sgT = sb("sgT", [4, P], F32, ev)
        bdT = sb("bdT", [4, NS], F32, ev)
        sbias = sb("sbias", [4, T], F32, ev)
        scT = sb("scT", [64], F32, ev)
        sctP = sb("sctP", [4, 2], F32, ev)
        sctS = sb("sctS", [4, 16], F32, ev)
        sco = sb("sco", [2, P], F32, ev)
        xn = sb("xn", [3, D], F32, ev)
        cwn = sb("cwn", [3, P], F32, ev)
        sgn = sb("sgn", [4, P], F32, ev)
        bdn = sb("bdn", [4, NS], F32, ev)
        scn = sb("scn", [P], F32, ev)
        ev.close()

        at = ExitStack()
        kt = ExitStack()
        kT = sb("kT", [DT, N_MEM], F32, kt)
        kt.close()
        pB = sb("pB", [2, DEC_B * (P + DEC_T)], F32, at)
        vN = sb("vN", [2, D], F32, at)
        ring = sb("ring", [4, 2, D], F32, at)
        qB = sb("qB", [DT, DEC_B * (NS + DEC_T)], F32, at)
        pS = sb("pS", [N_MEM], F32, at)
        kv = ExitStack()
        memn = sb("memn", [2, D], F32, kv)
        kN = sb("kN", [2, D], F32, kv)
        mh = sb("mh", [DT, N_MEM], F32R, kv)
        ml = sb("ml", [DT, N_MEM], F32R, kv)
        kv.close()
        pr = sb("pr", [8, N_MEM], F32, at)
        prT = sb("prT", [4, 2, SEQ], F32, at)
        kTb = sb("kTb", [2, DT, N_MEM], F32, at)
        at.close()

        ff = ExitStack()
        aH = sb("aH", [FT, T], F32R, ff)
        aL = sb("aL", [FT, T], F32R, ff)
        zb = sb("zb", [4, GRP, PAD], F32, ff)
        cb = sb("cb", [4, T], F32, ff)
        ge = sb("ge", [2, T], F32, ff)
        pd = sb("pd", [2, T], F32, ff)
        stn = sb("stn", [6, P], F32, ff)
        stT = sb("stT", [2 * FT, 16], F32, ff)
        tlS = sb("tlS", [48, 16], F32, ff)
        tlP = sb("tlP", [2 * FT, 2], F32, ff)
        tlo = sb("tlo", [7, P], F32, ff)
        ff.close()

        od = ExitStack()
        gs = ExitStack()
        gS = sb("gS", [16, T], F32, gs)
        gs.close()
        h2l = sb("h2l", [8, T], F32R, od)
        h2h = sb("h2h", [8, T], F32R, od)
        V4 = sb("V4", [RH * RDV], F32R, od)
        vR = sb("vR", [2, RH * RDV], F32, od)
        kR = sb("kR", [2, RH * RDK], F32, od)
        cR = sb("cR", [8 * P + 4], F32, od)
        cS = sb("cS", [12 * NS + 8], F32, od)
        QM = sb("QM", [8, DEC_B * (NS + DEC_T)], F32, od)
        K4 = sb("K4", [RH * RDK], F32, od)
        gp = ExitStack()
        cs = sb("cs", [2, T], F32, gp)
        cr = sb("cr", [2, T], F32, gp)
        rA = sb("rA", [2, T], F32, gp)
        rB = sb("rB", [2, T], F32, gp)
        vt = sb("vt", [4, T], F32, gp)
        vhS = sb("vhS", [4, NS], F32R, gp)
        v4T = sb("v4T", [4, 4, NS], F32, gp)
        gp.close()
        K4m = sb("K4m", [2, RH * RDK], F32R, od)
        ks = ExitStack()
        k4T = sb("k4T", [8, 4, NS], F32, ks)
        kd = sb("kd", [8, NS], F32, ks)
        kdh = sb("kdh", [8, NS], F32R, ks)
        ks.close()
        S1 = sb("S1", [2, RDV], F32, od)
        S2 = sb("S2", [2, RDV], F32, od)
        scr = sb("scr", [2, P], F32, od)
        qd = sb("qd", [2, P], F32, od)
        rn = sb("rn", [RDV], F32, od)
        rg = sb("rg", [4, P], F32, od)
        od.close()
        scS = rowsn[:].rearrange("p (h i) -> p h i", h=RH)

        def state_slot(b, hp):
            return (G["out", 1].first + 2 + 2 * (b % 2) + hp) % 4

        def state(b, h):
            return raw[:, state_slot(b, h // 2), 4 * (h % 2):4 * (h % 2) + 4, :].rearrange("p (d x) n -> p d (x n)", d=2)

        def states_dram(x, b, hp):
            return x[0, b, 2 * hp:2 * hp + 2].rearrange("h (d p) e -> p (h d) e", p=P)

        def states(b, hp):
            return raw[:, state_slot(b, hp)].rearrange("p (k x) n -> p k (x n)", k=4)

        fin = ExitStack()
        yn = sb("yn", [3, D], F32, fin)
        fin.close()

        ps = ctx.enter_context(nc.psum_tensor("ps", [P, 8, 512], F32))
        BN = 4

        landed = [sem("landed_even"), sem("landed_odd")]
        hi_ready, lo_ready, w_used = sem("hi_ready"), sem("lo_ready"), sem("w_used")
        sq_ready, sum_step, ssq_ready = sem("sq_ready"), sem("sum_step"), sem("ssq_ready")
        root_ready, rstd_ready = sem("root_ready"), sem("rstd_ready")
        m_ready, scaled, x_ready = sem("m_ready"), sem("scaled"), sem("x_ready")
        h_hi, h_lo = sem("h_hi"), sem("h_lo")
        S = {}

        def s(name):
            if name not in S:
                S[name] = sem(name)
            return S[name]

        def load_weights(e, g):
            w = g.w

            def step(i):
                cols = [g.cols(i, half) for half in range(2)]
                even = ((i + g.first // 2) % 2) * 2
                if not isinstance(i, int):
                    cols, even = [e.snap(x) for x in cols], e.snap(even)
                for idx in range(g.per):
                    c = g.first + idx
                    r0, kn = g.rows(idx)
                    src = w[r0 * P:(r0 + kn) * P, bass.ds(cols[idx // g.nk], CW)] \
                        .rearrange("(t p) n -> p t n", p=P)
                    if g is G["out", 1] and (i, idx) in ((0, 2), (1, 0)):
                        if i == 0:
                            load_states(e)
                        for slot in (2 * i, 2 * i + 1):
                            e.wait_ge(s(f"SR_out{slot}"), 16 * (DEC_B // 2))
                    e.wait_ge(lo_ready, i * g.per + c - 4 + CREDIT + 1)
                    e.wait_ge(landed[c % 2], i * (8 * g.per) + 16 * (c // 2) + 16)
                    slot = even + c % 2 if g.per % 4 else c % 4
                    e.dma_start(raw[:, slot, 0:kn, :], src).then_inc(landed[c % 2], 16)
            if g.steps > 2:
                with e.Fori(0, g.steps) as i:
                    step(i)
            else:
                for i in range(g.steps):
                    step(i)

        def load_states(e):
            for b in range(DEC_B):
                for hp in range(2):
                    if b < 2:
                        e.wait_ge(lo_ready, CREDIT + G["out", 1].first - 2 + 2 * b + hp + 1)
                    else:
                        e.wait_ge(s(f"SR_out{b % 2 * 2 + hp}"), 16 * (b // 2))
                    e.dma_start(states(b, hp), states_dram(a["state_retention"], b, hp)).then_inc(s(f"SR_in{b % 2 * 2 + hp}"), 16)

        def target(g, i, idx, last):
            idx += 2
            if idx < g.per:
                return g, i, idx
            if not last:
                return g, i + 1, idx - g.per
            return (g.next, 0, idx - g.per) if g.next else (None, 0, 0)

        def split(e, g, i, idx, high):
            if g is None:
                return
            c, kn = g.first + idx, g.rows(idx)[1]
            slot = (((i + c // 2) % 2) * 2 + c % 2) if g.per % 4 else c % 4
            src = raw[:, slot, 0:kn, :]
            if high:
                e.wait_ge(landed[c % 2], i * (8 * g.per) + 16 * (c // 2) + 32)
                e.wait_ge(w_used, i * (2 * g.per) + 2 * c - 2 + CREDIT)
                e.activation(wh[:, c % 2, 0:kn, :], src, ACT.Copy).then_inc(hi_ready, 1)
            else:
                e.wait_ge(hi_ready, i * g.per + c + 1)
                e.tensor_tensor(wl[:, c % 2, 0:kn, :], src, wh[:, c % 2, 0:kn, :].bitcast(F32),
                                ALU.subtract).then_inc(lo_ready, 1)

        def tiles_ready(e, g, i, half, j):
            c = g.first + half * g.nk + g.nk - 1
            e.wait_ge(w_used, i * (2 * g.per) + 2 * c + j + 1 + CREDIT)

        def run(e, g, high, evac, i0=0, i1=None, hold=False):
            i1 = g.steps if i1 is None else i1

            def step(i, last):
                for idx in range(g.per):
                    if idx % g.nk == g.nk - 1:
                        evac(i, idx // g.nk)
                    if not (hold and last and idx == g.per - 1):
                        split(e, *target(g, i, idx, last), high)
            end = i1 == g.steps
            n = i1 - end
            if n - i0 > 1:
                with e.Fori(i0, n) as i:
                    step(i, False)
            elif n - i0 == 1:
                step(i0, False)
            if end:
                step(g.steps - 1, True)

        def held(e, g, high):
            split(e, *target(g, g.steps - 1, g.per - 1, True), high)

        def products(pe, g, pairs, freed, base, natural=False, i0=0, i1=None, turn=0,
                     hook=None, need=None):
            i1 = g.steps if i1 is None else i1

            def step(i):
                for idx in range(g.per):
                    half, kc = divmod(idx, g.nk)
                    r0, kn = g.rows(idx)
                    c = g.first + idx
                    pe.wait_ge(lo_ready, i * g.per + c + 1 + CREDIT)
                    for j in range(2):
                        t = 2 * half + j
                        if kc == 0:
                            pe.wait_ge(freed, i * 4 + base + t - 3)
                        for n_k in range(kn):
                            k = (n_k + turn) % kn
                            if need and t == 0:
                                need(r0 + k)
                            xh, xl = pairs(r0 + k)
                            if natural:
                                w_h, w_l = wh[:, c % 2, k, :], wl[:, c % 2, k, :]
                                cut = slice(j * P, (j + 1) * P)
                                trio = ((xh[:, cut], w_h), (xl[:, cut], w_h), (xh[:, cut], w_l))
                                out = ps[:, t, 0:CW]
                            else:
                                w_h = wh[:, c % 2, k, j * P:(j + 1) * P]
                                w_l = wl[:, c % 2, k, j * P:(j + 1) * P]
                                trio = ((w_h, xh), (w_h, xl), (w_l, xh))
                                out = ps[:, t, 0:T]
                            for n, (lhsT, rhs) in enumerate(trio):
                                mm = pe.matmul(out, lhsT, rhs, start=(kc == 0 and n_k == 0 and n == 0),
                                               stop=(kc == g.nk - 1 and n_k == kn - 1 and n == 2))
                        mm.then_inc(w_used, 1)
                    if hook:
                        hook(i, idx)
            if i1 - i0 > 1:
                with pe.Fori(i0, i1) as i:
                    step(i)
            else:
                step(i0)

        def sums(dve, n, part):
            if part == 0:
                if n:
                    dve.wait_ge(ssq_ready, n)
                dve.wait_ge(sq_ready, CREDIT + 8 * n + 4)
                dve.tensor_tensor(acc[:], sq[:, 0:2, :], sq[:, 2:4, :], ALU.add).then_inc(sum_step, 1)
            else:
                dve.wait_ge(sq_ready, CREDIT + 8 * n + 6)
                dve.wait_ge(sum_step, 2 * n + 1)
                dve.tensor_tensor(acc[:], acc[:], sq[:, 4:6, :], ALU.add).then_inc(sum_step, 1)

        def ssq(pe, n):
            pe.wait_ge(sum_step, 2 * n + 2)
            if n:
                pe.wait_ge(root_ready, n)
            pe.matmul(ps[:, BN, 0:T], ones[:], acc[:, 0, :], start=True, stop=False)
            pe.matmul(ps[:, BN, 0:T], ones[:], acc[:, 1, :], start=False, stop=False)
            pe.wait_ge(sq_ready, CREDIT + 8 * n + 8)
            pe.matmul(ps[:, BN, 0:T], ones[:], sq[:, 6, :], start=False, stop=False)
            pe.matmul(ps[:, BN, 0:T], ones[:], sq[:, 7, :], start=False, stop=True).then_inc(ssq_ready, 1)

        def take_root(act, n):
            act.wait_ge(ssq_ready, n + 1)
            act.activation(root[:], ps[:, BN, 0:T], ACT.Sqrt, bias=eps_col, scale=1.0 / D).then_inc(root_ready, 1)

        def invert(dve, n):
            dve.wait_ge(root_ready, n + 1)
            dve.reciprocal(rstd[:], root[:]).then_inc(rstd_ready, 1)
            dve.wait_ge(rstd_ready, n + 1)

        def gained_high(act, q, squares=True):
            gain = gcol("pre", q)
            if q:
                act.wait_ge(ssq_ready, 2 * q)
            for t in range(DT):
                act.wait_ge(x_ready, DT * q + t + 1)
                act.activation(hh[:, t, :], xT[:, t, :], ACT.Copy, scale=gain(t)).then_inc(h_hi, 1)
                if squares:
                    act.activation(sq[:, t, :], xT[:, t, :], ACT.Square).then_inc(sq_ready, 1)

        def gained_low(dve, q, t):
            dve.wait_ge(h_hi, DT * q + t + 1)
            dve.scalar_tensor_tensor(out=hl[:, t, :], in0=xT[:, t, :], scalar=gcol("pre", q)(t),
                                     in1=hh[:, t, :].bitcast(F32), op0=ALU.mult, op1=ALU.subtract).then_inc(h_lo, 1)

        def scale_branch(pool, q):
            pool.wait_ge(rstd_ready, 2 * q + 2)
            for t in range(1, DT):
                pool.wait_ge(m_ready, DT * q + t + 1)
                pool.tensor_tensor(mT[:, t, :], mT[:, t, :], rstd[:], ALU.mult).then_inc(scaled, 1)

        def add_branch(dve, q, splits, late=True):
            invert(dve, 2 * q + 1)
            gain = gcol("post", q)
            dve.wait_ge(m_ready, DT * q + 1)
            dve.tensor_tensor(mT[:, 0, :], mT[:, 0, :], rstd[:], ALU.mult).then_inc(s("scaled_first"), 1)
            for t in range(DT + 2):
                if t < DT:
                    if t == 0:
                        dve.wait_ge(s("scaled_first"), q + 1)
                    else:
                        dve.wait_ge(scaled, (DT - 1) * q + t)
                    dve.scalar_tensor_tensor(out=xT[:, t, :], in0=mT[:, t, :], scalar=gain(t),
                                             in1=xT[:, t, :], op0=ALU.mult,
                                             op1=ALU.add).then_inc(x_ready, 1)
                if t >= 2 and q < 3 * DEPTH - 1:
                    dve.wait_ge(x_ready, DT * (q + 1) + t - 1)
                    gained_low(dve, q + 1, t - 2)
                if t == 3 and not late:
                    splits()
            if late:
                splits()
            if q < 3 * DEPTH - 1:
                sums(dve, 2 * q + 2, 0)
                sums(dve, 2 * q + 2, 1)

        GAINS = ("norm_mix_pre", "norm_mix_post", "norm_x_pre", "norm_x_post", "norm_ffn_pre", "norm_ffn_post", "norm_mem")

        def gcol(kind, q):
            l, br = divmod(q, 3)
            c = 2 * DT * (2 * br + (kind == "post")) + DT * l
            return lambda t: gT[:, c + t:c + t + 1]

        def memgain(l, t):
            c = 2 * DT * 6 + DT * l
            return gT[:, c + t:c + t + 1]

        def vgain(t):
            return gT[:, 112 + t:113 + t]

        def sctap(j, t):
            return gT[:, 116 + 4 * j + t:117 + 4 * j + t]

        def ftap(l, j, t):
            c = (3 * l + j) * 2 * FT
            return cwT[:, bass.ds(t + c, 1)]

        eps_col = small[:, 0:1]

        def first_step(pe, g, q, pairs, freed, base):
            products(pe, g, pairs, freed, base, i0=0, i1=1, need=lambda k: pe.wait_ge(h_lo, DT * q + k + 1),
                     hook=lambda i, idx: ssq(pe, 2 * q) if idx == 0 else None)

        def nothing(*_):
            pass

        def branch_out_act(act, g, q, between=nothing, half_way=nothing):
            def evac(i, half):
                if (i, half) == (0, 0):
                    act.wait_ge(ssq_ready, 2 * q + 1)
                for j in range(2):
                    t = i * 4 + 2 * half + j
                    tiles_ready(act, g, i, half, j)
                    src = ps[:, 2 * half + j, 0:T]
                    act.activation(sq[:, t, :], src, ACT.Square).then_inc(sq_ready, 1)
                    act.activation(mT[:, t, :], src, ACT.Copy).then_inc(m_ready, 1)
                if (i, half) == (1, 0):
                    half_way()
            run(act, g, True, evac, 0, 1)
            between()
            run(act, g, True, evac, 1, 2, hold=True)

        def branch_out_dve(dve, g, q, between=nothing, half_way=nothing):
            def evac(i, half):
                if i == 1:
                    sums(dve, 2 * q + 1, half)
                    if half == 0:
                        half_way()
            run(dve, g, False, evac, 0, 1)
            between()
            run(dve, g, False, evac, 1, 2, hold=True)

        def out_pe(pe, g, q, pairs):
            products(pe, g, pairs, sq_ready, CREDIT + 8 * (2 * q + 1))
            ssq(pe, 2 * q + 1)

        def normed(k):
            return hh[:, k, :], hl[:, k, :]

        def groups(x):
            return x.rearrange("p (g t) -> p g t", t=DEC_T)

        def transpose(pe, out, x, rows=P):
            return pe.transpose(out, x, ident[0:rows, 0:rows])

        MIX_BANKS = (5, 6, 7, BN)
        KR_BANKS = (5, 6, 7, 6)
        v_root, v_inv = sq[:, 4, :], sq[:, 5, :]
        L = range(DEPTH)
        stores = [0]
        dmat = lambda h: cR[:, h * P:(h + 1) * P]
        qdec = lambda h: cR[:, (4 + h) * P:(5 + h) * P]
        kdec = lambda h: cR[:, 8 * P + h:8 * P + h + 1]
        dmatS = cS[:, 0:4 * NS].rearrange("p (h i) -> p h i", h=RH)
        qdecS = cS[:, 4 * NS:8 * NS].rearrange("p (h o i) -> p h o i", h=RH, o=1)
        kdecS = cS[:, 8 * NS:12 * NS].rearrange("p (h o i) -> p h o i", h=RH, o=1)
        maskS = lambda b: cS[:, 12 * NS + b:12 * NS + b + 1]
        gam = [float(np.float32(1) - np.float32(2.0) ** np.float32(-5 - h)) for h in range(RH)]
        UNITS = [(h, c) for h in range(RH) for c in range(2)]

        def pool_retention(pool, store):
            pool.wait_ge(s("a_free"), 1)
            pool.dma_start(cs[:], a["c_rope"]).then_inc(s("ret_in"), 16)
            pool.dma_start(cR[:], a["c_ret"]).then_inc(s("ret_in"), 16)
            pool.dma_start(cS[:], a["c_retS"]).then_inc(s("ret_in"), 16)
            for n, (hp, c) in enumerate(UNITS):
                for half in range(2):
                    pool.wait_ge(s("SR_new"), 8 * n + 4 * half + 4)
                    pool.dma_start(states_dram(ret_sample, n, half), states(n, half)).then_inc(s(f"SR_out{n % 2 * 2 + half}"), 16)
                    if c == 1 and half == 0:
                        pool.wait_ge(s("S2_ready"), 2 * hp + 2)
                        pool.dma_start(ret_prompt[0, 0, hp].rearrange("(t p) e -> p t e", p=P), S2[:]).then_inc(s("S2_stored"), 16)
            pool.wait_ge(s("S2_stored"), 16 * RH)

        def act_even(act, l):
            g = G["in", l]

            def gate(i, half):
                for j in range(2):
                    t = 2 * half + j
                    act.wait_ge(s("in_even"), CREDIT + 4 * i + t + 1)
                    act.activation(v[:, t, :], v[:, t, :], ACT.Gelu_apprx_tanh).then_inc(s("v_sq"), 1)
                    act.wait_ge(s("v_sq"), 2 * t + 1)
                    act.activation(sq[:, t, :], v[:, t, :], ACT.Square).then_inc(s("v_sq"), 1)
            run(act, g, True, nothing, 0, 1)
            run(act, g, True, gate, 1, 2)
            act.wait_ge(s("const_ps"), 3)
            act.activation(sgT[:], ps[:, 7, :].rearrange("p (g t) -> p g t", g=4), ACT.Copy).then_inc(s("gT_ready"), 1)
            act.wait_ge(s("const_ps"), 4)
            act.activation(bdT[0:NS], ps[0:NS, 5, 128:256].rearrange("p (g t) -> p g t", g=4), ACT.Copy).then_inc(s("gT_ready"), 1)
            act.activation(scT[:], ps[:, 5, 256:320], ACT.Copy).then_inc(s("gT_ready"), 1)
            run(act, g, True, nothing, 2, 3)
            act.wait_ge(s("v_ps"), 1)
            act.activation(v_root[:], ps[:, BN, 0:T], ACT.Sqrt, bias=eps_col, scale=1.0 / (4 * P)).then_inc(s("v_sq"), 1)
            run(act, g, True, nothing, 3, 4)
            for c in range(3):
                n = P if c < 2 else NS
                act.wait_ge(s("v_ps"), c + 2)
                act.activation(vnat[0:n, c, :], ps[0:n, 5 + c, :], ACT.Copy).then_inc(s("vnat_ready"), 1)
            act.wait_ge(s("v_ps"), 5)
            act.activation(sco[0:8, 0, :], ps[0:8, BN, 0:P], ACT.Copy)
            act.activation(sco[0:64, 1, :], ps[0:64, BN, P:2 * P], ACT.Copy).then_inc(s("sco_ready"), 1)
            for t in range(4):
                act.wait_ge(s("b_ready"), t + 1)
                act.activation(bh[:, t, :], cv[:, t, :], ACT.Copy).then_inc(s("even_hi"), 1)

            def outer(i, half):
                for t in (2 * half, 2 * half + 1):
                    act.wait_ge(s("in_even"), CREDIT + 16 + t + 1)
                    act.activation(u[:, t, :], u[:, t, :], ACT.Gelu_apprx_tanh).then_inc(s("v_sq"), 1)
            run(act, g, True, outer, 4, 5, hold=True)
            for t in range(4):
                act.wait_ge(s("av_ready"), t + 1)
                act.activation(hh[:, t, :], av[:, t, :], ACT.Copy).then_inc(s("even_hi"), 1)
            held(act, g, True)

        def act_odd(act, l):
            g = G["in", l]
            act.wait_ge(s("ret_in"), 48)

            def gates(i, half):
                for j in range(2):
                    t = 2 * half + j
                    act.wait_ge(s("z_ready"), CREDIT + i * 4 + t + 1)
                    e = i * 4 + (t - 32)
                    act.activation(gS[:, e, :], gS[:, e, :], ACT.Silu).then_inc(s("silu"), 1)
            run(act, g, True, nothing, 0, 4)
            def naturals(i):
                for t in range(4):
                    e = 4 * (i - 4) + t
                    act.wait_ge(s("vR_ps"), e + 1)
                    act.activation(vR[:, :, e * P:(e + 1) * P],
                                   ps[:, 5 + e % 2, 0:2 * P].rearrange("p (c e) -> p c e", c=2), ACT.Copy)
                    act.activation(V4[:, e * P:(e + 1) * P], ps[:, 5 + e % 2, 2 * P:3 * P], ACT.Copy).then_inc(s("vR_ready"), 1)
            for i in range(4, 9):
                for idx in range(2):
                    if idx == 0 and i > 4:
                        naturals(i - 1)
                    if i == 8:
                        gates(i, idx)
                    split(act, *target(g, i, idx, False), True)
            run(act, g, True, gates, 9, 10)
            run(act, g, True, gates, 10, 11)
            for r in range(2):
                act.wait_ge(s("k4_ps"), r + 1)
                act.activation(K4[:, 512 * r:512 * r + 512], ps[:, 5 + r, :], ACT.Copy).then_inc(s("K4_ready"), 1)

            def own_keys(b):
                if b >= 2:
                    act.wait_ge(s("SU_ps"), 8 * (b - 1))
                act.activation(K4m[:, b % 2, :], K4[:], ACT.Copy, scale=maskS(b)).then_inc(s("K4m_ready"), 1)

            def natural_keys(n):
                c, hf = divmod(n, 2)
                act.wait_ge(s("kR_ps"), n + 1)
                for h in (2 * hf, 2 * hf + 1):
                    ins = act.activation(kR[:, c, h * RDK:(h + 1) * RDK], ps[:, KR_BANKS[n], h % 2 * RDK:(h % 2 + 1) * RDK],
                                         ACT.Copy, scale=kdec(h))
                ins.then_inc(s("kR_ready"), 1)

            def last_gates(i, half):
                if half == 1:
                    for n in range(3):
                        natural_keys(n)
                    act.wait_ge(s("K4_ready"), 2)
                    own_keys(0)
                gates(i, half)
            run(act, g, True, last_gates, 11, 12)
            natural_keys(3)

            def high(n):
                h, c = UNITS[n]
                act.wait_ge(s("rg_ready"), n + 1)
                (dh, o) = (hh, 4 * h) if h < 2 else (h2h, 4 * h - 8)
                act.activation(dh[:, o:o + 4, c * CHUNK:(c + 1) * CHUNK], rg[:], ACT.Copy).then_inc(s("rg_hi"), 1)

            for n, (h, c) in enumerate(UNITS):
                if n:
                    high(n - 1)
                if c == 0:
                    act.wait_ge(s("S_ps"), 2 * n + 2)
                    if h:
                        act.wait_ge(s("S2_ready"), 2 * h)
                    act.activation(S1[:], ps[:, 0:2, :], ACT.Copy).then_inc(s("S1_ready"), 1)
                if n < DEC_B - 1:
                    own_keys(n + 1)
                act.wait_ge(s("ro_mv"), n + 1)
                act.activation(small[:, 12:13], small[:, 11:12], ACT.Sqrt, bias=eps_col).then_inc(s("ro_root"), 1)
            act.wait_ge(s("ro_mv"), 9)
            act.activation(small[:, 12:13], small[:, 11:12], ACT.Sqrt, bias=eps_col).then_inc(s("ro_root"), 1)
            high(7)
            act.wait_ge(s("rg_ready"), 9)
            for dh, h in ((hh, 0), (h2h, 2)):
                act.activation(sample_gates(dh), sample_rows(h), ACT.Copy).then_inc(s("rg_hi"), 1)

        def sample_gates(x):
            return x[:, :, SEQ:T].rearrange("p (h e) i -> p e h i", e=4)

        def sample_rows(h):
            return rg[:].rearrange("p e (h i) -> p e h i", h=RH)[:, :, h:h + 2]

        KBANKS = (4, 6, 7)

        def own_tokens(row, width):
            return row.rearrange("p (b x) -> p b x", b=DEC_B)[:, :, 0:width].rearrange("p b (h i) -> p b h i", i=NS)[:, :, :, 0:DEC_T]

        def sample_heads(x):
            return x[:, :, SEQ:T].rearrange("p (h d) i -> p h d i", d=2)

        def take_keys(e, l, b, act):
            for r in (0, 2) if act else (1, 3):
                n = 4 * b + r
                e.wait_ge(s("kTb_ps"), 32 * l + n + 1)
                if b >= 2:
                    e.wait_ge(s("sS_mm"), 8 * l + b - 1)
                src = ps[:, KBANKS[n % 3], :].rearrange("p (t m) -> p t m", t=2)
                if act:
                    e.activation(kTb[:, b % 2, 2 * r:2 * r + 2, :], src, ACT.Copy).then_inc(s("kTb_act"), 1)
                else:
                    e.tensor_copy(kTb[:, b % 2, 2 * r:2 * r + 2, :], src).then_inc(s("kTb_dve"), 1)

        def act_attention(act, l):
            def exps(h):
                act.wait_ge(s("nm_ready"), 5 * l + h + 1)
                for n in (2 * h, 2 * h + 1):
                    act.activation(pr[:, n, :], ps[:, h, (n % 2) * N_MEM:(n % 2 + 1) * N_MEM], ACT.Exp, scale=XD ** -0.5,
                                   bias=small[:, 24 + n:25 + n], accum_out=small[:, 32 + n:33 + n]).then_inc(s("exp_ready"), 1)

            def turned(h):
                act.wait_ge(s("pT_ps"), 5 * l + h + 1)
                act.activation(prT[:, h, :, :], ps[:, h, :].rearrange("p (m t) -> p m t", m=2), ACT.Copy).then_inc(s("pT_ready"), 1)

            def heads_high(h):
                act.wait_ge(s("o_ps"), 5 * l + h + 1)
                act.activation(hh[:, 2 * h:2 * h + 2, 0:SEQ], ps[:, h, :].rearrange("p (d t) -> p d t", d=2), ACT.Copy).then_inc(s("oh_hi"), 1)

            for b in range(DEC_B):
                take_keys(act, l, b, True)
                if b < 4:
                    exps(b)
                if b == 5:
                    act.wait_ge(s("kv_stored"), 32 * l + 32)
                if b >= 5:
                    turned(b - 5)
                if b >= 6:
                    heads_high(b - 6)
            turned(3)
            act.wait_ge(s("nm_ready"), 5 * l + 5)
            act.activation(pS[:], ps[:, 5, 0:N_MEM], ACT.Exp, scale=XD ** -0.5, bias=small[:, 49:50],
                           accum_out=small[:, 50:51]).then_inc(s("exp_ready"), 1)
            heads_high(2)
            act.wait_ge(s("pT_ps"), 5 * l + 5)
            act.wait_ge(s("own_zero"), 2 * l + 2)
            act.activation(own_tokens(pB[:, 0, :], P), ps[:, 7, 0:P].rearrange("p (h b t) -> p b h t", h=XH, t=DEC_T),
                           ACT.Copy).then_inc(s("pB_act"), 1)
            heads_high(3)
            act.wait_ge(s("oS_mm"), 8 * l + 8)
            act.activation(pS[:], ps[:, 6, 0:XD], ACT.Copy).then_inc(s("oS_out"), 1)
            act.wait_ge(s("o_ps"), 5 * l + 5)
            act.activation(sample_heads(hh), ps[:, 7, 0:XD].rearrange("p (d h i) -> p h d i", d=2, h=XH),
                           ACT.Copy).then_inc(s("oh_hi"), 1)

        def dve_even(dve, l):
            g = G["in", l]

            def evac(i, half):
                for j in range(2):
                    t = 2 * half + j
                    tiles_ready(dve, g, i, half, j)
                    if i == 2:
                        dve.wait_ge(s("cg_ready"), t + 1)
                        dve.tensor_tensor(zz[:, t, :, 2:PAD], groups(cg[:, t, :]), groups(ps[:, t, 0:T]),
                                          ALU.mult).then_inc(s("in_even"), 1)
                    else:
                        dve.tensor_tensor((cg, v, None, bg, u)[i][:, t, :], ps[:, t, 0:T], rstd[:], ALU.mult).then_inc(s("in_even"), 1)
            run(dve, g, False, evac, 0, 1)
            for t in range(4):
                dve.wait_ge(s("in_even"), CREDIT + t + 1)
                dve.tensor_tensor(cg[:, t, :], cg[:, t, :], rstd[:], ALU.mult).then_inc(s("cg_ready"), 1)
            run(dve, g, False, evac, 1, 2)
            dve.wait_ge(s("v_sq"), 8)
            dve.wait_ge(ssq_ready, 1)
            dve.tensor_tensor(acc[:], sq[:, 0:2, :], sq[:, 2:4, :], ALU.add).then_inc(s("vn_ready"), 1)
            run(dve, g, False, evac, 2, 3)
            dve.wait_ge(s("in_even"), CREDIT + 12)
            dve.wait_ge(s("gT_ready"), 5)
            dve.tensor_copy(zz[:, :, 1:PG, 0:2], zz[:, :, 0:PG - 1, 4:6]).then_inc(s("zz_pre"), 1)
            dve.tensor_copy(zz[:, :, PG:, 0:2], scT[:].rearrange("p (t b j) -> p t b j", t=4, j=2)).then_inc(s("zz_pre"), 1)
            dve.tensor_copy(sctP[:], zz[:, :, PG - 1, 4:6]).then_inc(s("sct_ready"), 1)
            dve.tensor_copy(sctS[:].rearrange("p t (b j) -> p t b j", j=2), zz[:, :, PG:, 4:6]).then_inc(s("sct_ready"), 1)
            dve.wait_ge(s("v_sq"), 9)
            dve.reciprocal(v_inv[:], v_root[:]).then_inc(s("vn_ready"), 1)
            dve.wait_ge(s("vn_ready"), 2)
            for t in range(4):
                dve.scalar_tensor_tensor(out=v[:, t, :], in0=v[:, t, :], scalar=vgain(t), in1=v_inv[:],
                                         op0=ALU.mult, op1=ALU.mult).then_inc(s("vn_ready"), 1)
            run(dve, g, False, evac, 3, 4)
            dve.wait_ge(s("zz_pre"), 2)
            for t in range(4):
                dve.tensor_scalar(groups(cv[:, t, :]), zz[:, t, :, 2:PAD], sctap(2, t), None, ALU.mult).then_inc(s("cv"), 1)
            for j in (1, 0):
                for t in range(4):
                    dve.wait_ge(s("cv"), 4 * (1 - j) + t + 1)
                    dve.scalar_tensor_tensor(out=groups(cv[:, t, :]), in0=zz[:, t, :, j:j + 4], scalar=sctap(j, t),
                                             in1=groups(cv[:, t, :]), op0=ALU.mult, op1=ALU.add).then_inc(s("cv"), 1)
            for t in range(4):
                dve.wait_ge(s("cv"), 8 + t + 1)
                dve.wait_ge(s("in_even"), CREDIT + 12 + t + 1)
                dve.tensor_tensor(cv[:, t, :], cv[:, t, :], bg[:, t, :], ALU.mult).then_inc(s("b_ready"), 1)

            def outer(i, half):
                evac(i, half)
                if half == 0:
                    for t in range(4):
                        dve.wait_ge(s("even_hi"), t + 1)
                        dve.tensor_tensor(bl[:, t, :], cv[:, t, :], bh[:, t, :].bitcast(F32), ALU.subtract).then_inc(s("even_lo"), 1)
                    dve.wait_ge(s("bias_in"), 160)
                    for t in range(4):
                        dve.wait_ge(s("mix_ps"), t + 1)
                        dve.tensor_tensor(av[:, t, :], sbias[:, t, :], ps[:, MIX_BANKS[t], 0:T], ALU.add).then_inc(s("mixed"), 1)
            run(dve, g, False, outer, 4, 5, hold=True)
            tiles_ready(dve, g, 4, 1, 1)
            for t in range(4):
                dve.wait_ge(s("mixed"), t + 1)
                dve.wait_ge(s("v_sq"), 9 + t + 1)
                dve.tensor_tensor(av[:, t, :], av[:, t, :], u[:, t, :], ALU.mult).then_inc(s("av_ready"), 1)
            for t in range(4):
                dve.wait_ge(s("even_hi"), 4 + t + 1)
                dve.tensor_tensor(hl[:, t, :], av[:, t, :], hh[:, t, :].bitcast(F32), ALU.subtract).then_inc(s("even_lo"), 1)
            held(dve, g, False)

        def dve_odd(dve, l):
            g = G["in", l]

            dve.wait_ge(s("ret_in"), 48)
            dve.tensor_tensor(cr[:], cs[:], rstd[:].unsqueeze(1).to_broadcast([P, 2, T]), ALU.mult).then_inc(s("cr_ready"), 1)

            def turn(dst, i0):
                def evac(i, half):
                    pair = ps[:, 2 * half:2 * half + 2, 0:T]
                    tiles_ready(dve, g, i, half, 1)
                    dve.wait_ge(s("cr_ready"), 1)
                    dve.wait_ge(s("turned"), i * 4 + 2 * half + CREDIT)
                    dve.tensor_tensor(rA[:], pair, cr[:, 0, :].unsqueeze(1).to_broadcast([P, 2, T]), ALU.mult)
                    dve.tensor_tensor(rB[:], pair, cr[:, 1, :].unsqueeze(1).to_broadcast([P, 2, T]), ALU.mult).then_inc(s("z_ready"), 2)
                    dve.wait_ge(s("z_ready"), CREDIT + i * 4 + 2 * half + 2)
                    dve.tensor_tensor(dst[:, i * 4 + (2 * half - 4 * i0), :], rA[:, 0, :], rB[:, 1, :], ALU.subtract).then_inc(s("turned"), 1)
                    dve.tensor_tensor(dst[:, i * 4 + (2 * half + 1 - 4 * i0), :], rB[:, 0, :], rA[:, 1, :], ALU.add).then_inc(s("turned"), 1)
                return evac
            run(dve, g, False, turn(mT, 0), 0, 2)
            run(dve, g, False, turn(sq, 2), 2, 4)

            def keep(i, half):
                for j in range(2):
                    t = 2 * half + j
                    e = 4 * (i - 4) + t
                    tiles_ready(dve, g, i, half, j)
                    if e >= 4:
                        dve.wait_ge(s("vR_ps"), e - 3)
                    dve.tensor_tensor(vt[:, t, :], ps[:, t, 0:T], rstd[:], ALU.mult).then_inc(s("z_ready"), 1)
                for j in range(2):
                    t = 2 * half + j
                    e = 4 * (i - 4) + t
                    dve.wait_ge(s("z_ready"), CREDIT + 4 * i + t + 1)
                    dve.tensor_copy(vhS[:, t, :], vt[:, t, SEQ:T]).then_inc(s("vh"), 1)
                    dve.wait_ge(s("vh"), e + 1)
                    both = vhS[:, t, :].bitcast(F32).unsqueeze(1).to_broadcast([P, 2, NS])
                    dve.tensor_copy(v4T[:, t, 0:4:2, :], both)
                    dve.tensor_tensor(v4T[:, t, 1:4:2, :], vt[:, t, SEQ:T].unsqueeze(1).to_broadcast([P, 2, NS]),
                                      both, ALU.subtract).then_inc(s("v4T_ready"), 1)

            def gates(i, half):
                for j in range(2):
                    t = 2 * half + j
                    tiles_ready(dve, g, i, half, j)
                    dve.tensor_tensor(gS[:, i * 4 + (t - 32), :], ps[:, t, 0:T], rstd[:], ALU.mult).then_inc(s("z_ready"), 1)
            for i in range(4, 8):
                run(dve, g, False, keep, i, i + 1)
            run(dve, g, False, gates, 8, 9)
            kS = sq[:, :, SEQ:T]
            four = lambda x: x.rearrange("p (h d) i -> p h d i", d=2)
            dve.wait_ge(s("ret_in"), 48)
            dve.wait_ge(s("vR_ps"), 16)
            dve.wait_ge(s("turned"), CREDIT + 16)
            dve.tensor_copy(k4T[:, :, 0:2, :], kS.unsqueeze(2).to_broadcast([P, 8, 2, NS])).then_inc(s("kdup"), 1)
            dve.memset(QM[:], 0.0).then_inc(s("QM_step"), 1)
            dve.tensor_tensor(four(kd[:]), four(mT[:, :, SEQ:T]), qdecS.to_broadcast([P, RH, 2, NS]), ALU.mult).then_inc(s("QM_step"), 1)
            run(dve, g, False, gates, 9, 10)
            dve.wait_ge(s("QM_step"), 2)
            dve.tensor_copy(QM[:].rearrange("p k (b x) -> p k b x", b=DEC_B)[:, :, :, 0:DEC_T],
                            kd[:].rearrange("p k (b t) -> p k b t", t=DEC_T)).then_inc(s("QM_step"), 1)
            dve.wait_ge(s("scS_ps"), 1)
            dve.tensor_tensor(scS[0:64], dmatS[0:64], ps[0:64, 7, 0:4 * NS].rearrange("p (h i) -> p h i", h=RH),
                              ALU.mult).then_inc(s("scS_ready"), 1)
            dve.wait_ge(s("QM_step"), 3)
            dve.tensor_tensor(four(kd[:]), four(kS), kdecS.to_broadcast([P, RH, 2, NS]), ALU.mult).then_inc(s("kd"), 1)
            dve.wait_ge(s("kd"), 1)
            dve.tensor_copy(kdh[:], kd[:]).then_inc(s("kd"), 1)
            dve.wait_ge(s("kd"), 2)
            kh2 = kdh[:].bitcast(F32).unsqueeze(2).to_broadcast([P, 8, 2, NS])
            dve.tensor_copy(k4T[:, :, 0:2, :], kh2)
            dve.tensor_tensor(k4T[:, :, 2:4, :], kd[:].unsqueeze(2).to_broadcast([P, 8, 2, NS]), kh2,
                              ALU.subtract).then_inc(s("k4T_full"), 1)
            run(dve, g, False, gates, 10, 11)
            run(dve, g, False, gates, 11, 12)

            def update(b, k):
                dve.wait_ge(s("SU_ps"), 8 * b + k + 1)
                st = state(b, k // 2)[:, k % 2, :]
                dve.scalar_tensor_tensor(out=st, in0=st, scalar=gL(k // 2, DEC_T), in1=ps[:, 2 + k % 2, :],
                                         op0=ALU.mult, op1=ALU.add).then_inc(s("SR_new"), 1)

            def gated(n):
                h, c = UNITS[n]
                dve.wait_ge(s("rT_ps"), n + 1)
                dve.wait_ge(s("silu"), 16)
                if n:
                    dve.wait_ge(s("rg_lo"), n)
                dve.tensor_tensor(rg[:], gS[:, 4 * h:4 * h + 4, c * CHUNK:(c + 1) * CHUNK],
                                  ps[:, 7, :].rearrange("p (e i) -> p e i", e=4), ALU.mult).then_inc(s("rg_ready"), 1)

            def low(n):
                h, c = UNITS[n]
                tok = slice(c * CHUNK, (c + 1) * CHUNK)
                (dh, dl, o) = (hh, hl, 4 * h) if h < 2 else (h2h, h2l, 4 * h - 8)
                dve.wait_ge(s("rg_hi"), n + 1)
                dve.tensor_tensor(dl[:, o:o + 4, tok], rg[:], dh[:, o:o + 4, tok].bitcast(F32), ALU.subtract).then_inc(s("rg_lo"), 1)

            for n, (h, c) in enumerate(UNITS):
                tok = slice(c * CHUNK, (c + 1) * CHUNK)
                dve.wait_ge(s("rs_ps"), n + 1)
                dve.tensor_tensor(scr[:, n % 2, :], dmat(h), ps[:, 5, 0:P], ALU.mult).then_inc(s("rs_ready"), 1)
                if c == 1:
                    dve.tensor_tensor(qd[:], mT[:, 2 * h:2 * h + 2, tok],
                                      qdec(h).unsqueeze(1).to_broadcast([P, 2, P]), ALU.mult).then_inc(s("qd_ready"), 1)
                if n:
                    gated(n - 1)
                update(n, 0)
                update(n, 1)
                if n:
                    low(n - 1)
                update(n, 2)
                update(n, 3)
                if c == 1:
                    for dt in range(2):
                        dve.wait_ge(s("S_ps"), 2 * n + dt + 1)
                        if h and dt == 0:
                            dve.wait_ge(s("S2_stored"), 16 * h)
                        dve.scalar_tensor_tensor(out=S2[:, dt, :], in0=S1[:, dt, :], scalar=gL(h, CHUNK),
                                                 in1=ps[:, dt, :], op0=ALU.mult, op1=ALU.add).then_inc(s("S2_ready"), 1)
                dve.wait_ge(s("ro_ps"), n + 1)
                update(n, 4)
                moments(dve, n, ps[:, 6, :])
                update(n, 5)
                scaled_rows(dve, n, ps[:, 6, :])
                update(n, 6)
                update(n, 7)
            moments(dve, 8, ps[:, BN, :])
            gated(7)
            scaled_rows(dve, 8, ps[:, BN, :])
            low(7)
            dve.wait_ge(s("rT_ps"), 9)
            dve.wait_ge(s("rg_lo"), 8)
            dve.tensor_tensor(rg[:].rearrange("p e (h i) -> p e h i", h=RH), sample_gates(gS),
                              ps[:, 7, :].rearrange("p (e h i) -> p e h i", e=4, h=RH), ALU.mult).then_inc(s("rg_ready"), 1)
            for n, (dh, dl) in enumerate(((hh, hl), (h2h, h2l))):
                dve.wait_ge(s("rg_hi"), 9 + n)
                dve.tensor_tensor(sample_gates(dl), sample_rows(2 * n), sample_gates(dh).bitcast(F32),
                                  ALU.subtract).then_inc(s("rg_lo"), 1)

        def gL(h, n):
            return float(np.exp(np.float32(np.log1p(-np.exp2(np.float32(-5 - h)))) * np.float32(n)))

        def moments(dve, n, src):
            dve.bn_stats(small[:, 52:58], src).then_inc(s("ro_st"), 1)
            dve.wait_ge(s("ro_st"), n + 1)
            dve.bn_aggr(small[:, 10:12], small[:, 52:58]).then_inc(s("ro_mv"), 1)

        def scaled_rows(dve, n, src):
            dve.wait_ge(s("ro_root"), n + 1)
            dve.reciprocal(small[:, 13:14], small[:, 12:13]).then_inc(s("ro_inv"), 1)
            dve.wait_ge(s("ro_inv"), n + 1)
            if n:
                dve.wait_ge(s("rT_ps"), n)
            dve.tensor_scalar(rn[:], src, small[:, 10:11], small[:, 13:14], ALU.subtract,
                              ALU.mult).then_inc(s("rn_ready"), 1)

        def dve_attention(dve, l):
            def maxima(h):
                if h == XH:
                    dve.wait_ge(s("sS_mm"), 8 * l + 8)
                    src, mx, nm = ps[:, 5, 0:N_MEM], small[:, 48:49], small[:, 49:50]
                else:
                    dve.wait_ge(s("sc_ps"), 4 * l + h + 1)
                    src = ps[:, h, :].rearrange("p (t m) -> p t m", t=2)
                    mx, nm = small[:, 16 + 2 * h:18 + 2 * h], small[:, 24 + 2 * h:26 + 2 * h]
                dve.tensor_reduce(mx, src, AX.X, ALU.max).then_inc(s("mx_ready"), 1)
                dve.wait_ge(s("mx_ready"), 5 * l + h + 1)
                dve.tensor_scalar(nm, mx, -XD ** -0.5, None, ALU.mult).then_inc(s("nm_ready"), 1)

            def shares(h):
                sample = h == XH
                dve.wait_ge(s("exp_ready"), 9 * l + (9 if sample else 2 * h + 2))
                sm, rc = (small[:, 50:51], small[:, 51:52]) if sample else \
                    (small[:, 32 + 2 * h:34 + 2 * h], small[:, 40 + 2 * h:42 + 2 * h])
                dve.reciprocal(rc, sm).then_inc(s("rc_ready"), 1)
                dve.wait_ge(s("rc_ready"), 5 * l + h + 1)
                if sample:
                    dve.tensor_scalar(pS[:], pS[:], rc, None, ALU.mult).then_inc(s("p_ready"), 1)
                    return
                for n in (2 * h, 2 * h + 1):
                    dve.tensor_scalar(pr[:, n, :], pr[:, n, :], small[:, 40 + n:41 + n], None, ALU.mult).then_inc(s("p_ready"), 1)

            def heads_low(h):
                dve.wait_ge(s("oh_hi"), 5 * l + h + 1)
                dve.tensor_tensor(hl[:, 2 * h:2 * h + 2, 0:SEQ], ps[:, h, :].rearrange("p (d t) -> p d t", d=2),
                                  hh[:, 2 * h:2 * h + 2, 0:SEQ].bitcast(F32), ALU.subtract).then_inc(s("oh_lo"), 1)

            dve.wait_ge(s("q_ready"), CREDIT + 8 * l + 8)
            dve.wait_ge(s("own_zero"), 2 * l + 1)
            dve.tensor_copy(qB[:].rearrange("p k (b x) -> p k b x", b=DEC_B)[:, :, :, 0:DEC_T],
                            mT[:, :, SEQ:T].rearrange("p k (b t) -> p k b t", t=DEC_T)).then_inc(s("own_dve"), 1)
            for b in range(DEC_B):
                take_keys(dve, l, b, False)
                if b < 4:
                    maxima(b)
                if 1 <= b <= 4:
                    shares(b - 1)
                if b == 7:
                    heads_low(0)
            maxima(XH)
            heads_low(1)
            shares(XH)
            heads_low(2)
            dve.wait_ge(s("pB_act"), l + 1)
            dve.tensor_copy(own_tokens(pB[:, 1, :], P), ps[:, 7, P:2 * P].rearrange("p (h b t) -> p b h t", h=XH, t=DEC_T)) \
                .then_inc(s("own_dve"), 1)
            heads_low(3)
            dve.wait_ge(s("oh_hi"), 5 * l + 5)
            dve.tensor_tensor(sample_heads(hl), ps[:, 7, 0:XD].rearrange("p (d h i) -> p h d i", d=2, h=XH),
                              sample_heads(hh).bitcast(F32), ALU.subtract).then_inc(s("oh_lo"), 1)

        def pe_even(pe, l):
            g = G["in", l]
            first_step(pe, g, 3 * l, normed, s("in_even"), CREDIT)
            products(pe, g, normed, s("in_even"), CREDIT, i0=1, i1=2)
            pe.wait_ge(s("sgu_masked"), 2)
            for k in range(4):
                tr = transpose(pe, ps[:, 7, k * P:(k + 1) * P], sgn[:, k, :])
            tr.then_inc(s("const_ps"), 1)
            pe.wait_ge(s("gT_ready"), 1)
            for k in range(4):
                transpose(pe, ps[0:NS, 5, P + k * NS:P + (k + 1) * NS], bdn[0:NS, k, :], NS)
            transpose(pe, ps[:, 5, 2 * P:2 * P + 64], scn[0:64, :], 64).then_inc(s("const_ps"), 1)

            def gate_sums(i, idx):
                if idx == 0:
                    pe.wait_ge(s("vn_ready"), 1)
                    pe.wait_ge(root_ready, 1)
                    pe.matmul(ps[:, BN, 0:T], ones[:], acc[:, 0, :], start=True, stop=False)
                    pe.matmul(ps[:, BN, 0:T], ones[:], acc[:, 1, :], start=False, stop=True).then_inc(s("v_ps"), 1)
            products(pe, g, normed, s("in_even"), CREDIT, i0=2, i1=3, hook=gate_sums)
            products(pe, g, normed, s("in_even"), CREDIT, i0=3, i1=4)
            pe.wait_ge(s("gT_ready"), 5)
            pe.wait_ge(s("vn_ready"), 6)
            for c in range(3):
                n = P if c < 2 else NS
                for t in range(4):
                    tr = transpose(pe, ps[0:n, 5 + c, t * P:(t + 1) * P], v[:, t, c * P:c * P + n])
                tr.then_inc(s("v_ps"), 1)
            pe.wait_ge(s("sct_ready"), 2)
            transpose(pe, ps[0:8, BN, 0:P], sctP[:].rearrange("p t j -> p (t j)"))
            transpose(pe, ps[0:64, BN, P:2 * P], sctS[:].rearrange("p t r -> p (t r)")).then_inc(s("v_ps"), 1)

            def mix(i, idx):
                if idx:
                    return
                pe.wait_ge(s("vnat_ready"), 3)
                pe.wait_ge(s("sco_ready"), 1)
                for t, bank in enumerate(MIX_BANKS):
                    cut = slice(t * P, (t + 1) * P)
                    for c in range(2):
                        pe.matmul(ps[:, bank, c * CHUNK:(c + 1) * CHUNK], vnat[:, c, cut], sgT[:, t, :], start=True, stop=True)
                    pe.matmul(ps[:, bank, SEQ:T], vnat[0:NS, 2, cut], bdT[0:NS, t, :], start=True, stop=True).then_inc(s("mix_ps"), 1)
            products(pe, g, normed, s("in_even"), CREDIT, i0=4, i1=5, hook=mix)

        def pe_odd(pe, l):
            g = G["in", l]
            first_step(pe, g, 3 * l, normed, s("z_ready"), CREDIT)
            products(pe, g, normed, s("z_ready"), CREDIT, i0=1, i1=4)

            def naturals(i, idx):
                if idx or i == 4:
                    return
                for t in range(4):
                    e = 4 * (i - 5) + t
                    pe.wait_ge(s("v4T_ready"), e + 1)
                    if e >= 2:
                        pe.wait_ge(s("vR_ready"), e - 1)
                    bank = 5 + e % 2
                    for c in range(2):
                        transpose(pe, ps[:, bank, c * P:(c + 1) * P], vt[:, t, c * P:(c + 1) * P])
                    transpose(pe, ps[:, bank, 2 * P:3 * P], v4T[:, t, :, :].rearrange("p r i -> p (r i)")).then_inc(s("vR_ps"), 1)
            for i in range(4, 9):
                products(pe, g, normed, s("z_ready"), CREDIT, i0=i, i1=i + 1, hook=naturals)
            products(pe, g, normed, s("z_ready"), CREDIT, i0=9, i1=10)
            pe.wait_ge(s("kdup"), 1)
            for h in range(RH):
                for dt in range(2):
                    mm = pe.matmul(ps[0:64, 7, h * NS:(h + 1) * NS], k4T[:, 2 * h + dt, 0:2, :].rearrange("p r i -> p (r i)"),
                                   mT[:, 2 * h + dt, SEQ:T], start=dt == 0, stop=dt == 1)
            mm.then_inc(s("scS_ps"), 1)
            products(pe, g, normed, s("z_ready"), CREDIT, i0=10, i1=11)
            pe.wait_ge(s("k4T_full"), 1)
            pe.wait_ge(s("vR_ready"), 16)
            for r in range(2):
                for k in range(4):
                    tr = transpose(pe, ps[:, 5 + r, k * P:(k + 1) * P], k4T[:, 4 * r + k, :, :].rearrange("p r i -> p (r i)"))
                tr.then_inc(s("k4_ps"), 1)

            def turn_keys(n):
                c, hf = divmod(n, 2)
                for k in range(4):
                    tr = transpose(pe, ps[:, KR_BANKS[n], k * P:(k + 1) * P], sq[:, 4 * hf + k, c * P:(c + 1) * P])
                tr.then_inc(s("kR_ps"), 1)

            def before_heads(i, idx):
                if idx:
                    return
                pe.wait_ge(s("K4_ready"), 2)
                pe.wait_ge(s("scS_ready"), 1)
                for n in range(3):
                    turn_keys(n)
                pe.wait_ge(root_ready, 2 * 3 * l + 1)
                for h in range(RH):
                    pe.matmul(ps[h * NS:(h + 1) * NS, BN, :], scS[0:64, h, :], V4[0:64, h * RDV:(h + 1) * RDV].bitcast(F32),
                              start=True, stop=False, skip_group_check=True, tile_position=(0, h * NS))
            products(pe, g, normed, s("z_ready"), CREDIT, i0=11, i1=12, hook=before_heads)
            pe.wait_ge(s("kR_ready"), 3)
            turn_keys(3)

            def sample_states(b, tiles):
                for k in tiles:
                    h = k // 2
                    n = 8 * b + k
                    pe.wait_ge(s(f"SR_in{b % 2 * 2 + h // 2}"), 16 * (b // 2) + 16)
                    pe.matmul(ps[h * NS:(h + 1) * NS, BN, :], QM[:, k, b * NS:(b + 1) * NS], state(b, h)[:, k % 2, :], start=False,
                              stop=b == DEC_B - 1 and k % 2 == 1, skip_group_check=True, tile_position=(0, h * NS))
                    if k == 0:
                        pe.wait_ge(s("K4m_ready"), b + 1)
                    if n >= 2:
                        pe.wait_ge(s("SR_new"), n - 1)
                    pe.matmul(ps[:, 2 + k % 2, :], K4m[:, b % 2, k * P:(k + 1) * P], V4[:, h * RDV:(h + 1) * RDV],
                              start=True, stop=True).then_inc(s("SU_ps"), 1)

            pe.wait_ge(s("z_ready"), CREDIT + 48)
            pe.wait_ge(s("QM_step"), 3)
            for n, (h, c) in enumerate(UNITS):
                tok = slice(c * CHUNK, (c + 1) * CHUNK)
                if n:
                    pe.wait_ge(s("rs_ready"), n)
                for dt in range(2):
                    mm = pe.matmul(ps[:, 5, 0:P], sq[:, 2 * h + dt, tok], mT[:, 2 * h + dt, tok], start=dt == 0, stop=dt == 1)
                mm.then_inc(s("rs_ps"), 1)
                sample_states(n, (0, 1))
                if n:
                    if c == 1:
                        pe.wait_ge(s("S1_ready"), h + 1)
                    else:
                        pe.wait_ge(s("S2_ready"), 2 * h)
                for dt in range(2):
                    pe.matmul(ps[:, dt, :], kR[:, c, h * RDK + dt * P:h * RDK + dt * P + P], vR[:, c, h * RDV:(h + 1) * RDV],
                              start=True, stop=True).then_inc(s("S_ps"), 1)
                sample_states(n, (2, 3))
                pe.wait_ge(s("rs_ready"), n + 1)
                if n:
                    pe.wait_ge(s("rn_ready"), n)
                pe.wait_ge(s("kR_ready"), 4)
                mm = pe.matmul(ps[:, 6, :], scr[:, n % 2, :], vR[:, c, h * RDV:(h + 1) * RDV], start=True, stop=c == 0)
                if c == 1:
                    pe.wait_ge(s("qd_ready"), h + 1)
                    pe.wait_ge(s("S1_ready"), h + 1)
                    for dt in range(2):
                        mm = pe.matmul(ps[:, 6, :], qd[:, dt, :], S1[:, dt, :], start=False, stop=dt == 1)
                mm.then_inc(s("ro_ps"), 1)
                sample_states(n, (4, 5, 6, 7))
                pe.wait_ge(s("rn_ready"), n + 1)
                if n:
                    pe.wait_ge(s("rg_ready"), n)
                for k in range(4):
                    tr = transpose(pe, ps[:, 7, k * P:(k + 1) * P], rn[:, k * P:(k + 1) * P])
                tr.then_inc(s("rT_ps"), 1)
            pe.wait_ge(s("rn_ready"), 9)
            pe.wait_ge(s("rg_ready"), 8)
            for k in range(4):
                tr = transpose(pe, ps[:, 7, k * P:(k + 1) * P], rn[:, k * P:(k + 1) * P])
            tr.then_inc(s("rT_ps"), 1)

        def pe_attention(pe, l):
            def keys(b):
                pe.wait_ge(s(f"cache{b % 4}"), 64 * l + 16 * (b // 4) + 16)
                for r in range(4):
                    n = 4 * b + r
                    if n >= 3:
                        pe.wait_ge(s("kTb_dve" if (n - 3) % 2 else "kTb_act"), 16 * l + (n - 3) // 2 + 1)
                    for t in (2 * r, 2 * r + 1):
                        for m in range(2):
                            c = (t % 2) * N_MEM + m * P
                            tr = transpose(pe, ps[:, KBANKS[n % 3], c:c + P], ring[:, b % 4, m, t * P:(t + 1) * P])
                    tr.then_inc(s("kTb_ps"), 1)

            def sample_scores(b):
                pe.wait_ge(s("kTb_act"), 16 * l + 2 * b + 2)
                pe.wait_ge(s("kTb_dve"), 16 * l + 2 * b + 2)
                if b == 0:
                    pe.wait_ge(s("own_dve"), 2 * l + 1)
                for t in range(DT):
                    h = t // 2
                    mm = pe.matmul(ps[h * NS:(h + 1) * NS, 5, 0:N_MEM], qB[:, t, b * NS:(b + 1) * NS], kTb[:, b % 2, t, :],
                                   start=b == 0 and t % 2 == 0, stop=b == DEC_B - 1 and t % 2 == 1,
                                   skip_group_check=True, tile_position=(0, h * NS))
                mm.then_inc(s("sS_mm"), 1)

            def turn_shares(h):
                pe.wait_ge(s("p_ready"), 9 * l + 2 * h + 2)
                for m in range(2):
                    for tt in range(2):
                        tr = transpose(pe, ps[:, h, m * SEQ + tt * P:m * SEQ + (tt + 1) * P], pr[:, 2 * h + tt, m * P:(m + 1) * P])
                tr.then_inc(s("pT_ps"), 1)

            def values(h):
                pe.wait_ge(s("pT_ready"), 4 * l + h + 1)
                for dt in range(2):
                    for m in range(2):
                        mm = pe.matmul(ps[:, h, dt * SEQ:(dt + 1) * SEQ], vN[:, m, (2 * h + dt) * P:(2 * h + dt + 1) * P],
                                       prT[:, h, m, :], start=m == 0, stop=m == 1)
                mm.then_inc(s("o_ps"), 1)

            pe.wait_ge(s("q_ready"), CREDIT + 8 * l + 8)
            pe.wait_ge(s("kT_ready"), 4 * l + 4)
            pe.wait_ge(root_ready, 2 * (3 * l + 1) + 1)
            for h in range(XH):
                for tt in range(2):
                    for dt in range(2):
                        mm = pe.matmul(ps[:, h, tt * N_MEM:(tt + 1) * N_MEM], mT[:, 2 * h + dt, tt * P:(tt + 1) * P],
                                       kT[:, 2 * h + dt, :], start=dt == 0, stop=dt == 1)
                mm.then_inc(s("sc_ps"), 1)
            keys(0)
            for b in range(DEC_B):
                if b < DEC_B - 1:
                    keys(b + 1)
                if b >= 4:
                    turn_shares(b - 4)
                sample_scores(b)
                if b >= 5:
                    values(b - 5)
            values(3)
            pe.wait_ge(s("p_ready"), 9 * l + 9)
            for m in range(2):
                tr = transpose(pe, ps[:, 7, m * P:(m + 1) * P], pS[:, m * P:(m + 1) * P])
            tr.then_inc(s("pT_ps"), 1)
            pe.wait_ge(s("pB_act"), l + 1)
            pe.wait_ge(s("own_dve"), 2 * l + 2)
            for b in range(DEC_B):
                n = DEC_B + b
                pe.wait_ge(s(f"cache{n % 4}"), 64 * l + 16 * (n // 4) + 16)
                for h in range(XH):
                    for m in range(2):
                        mm = pe.matmul(ps[h * NS:(h + 1) * NS, 6, 0:XD], pB[:, m, b * P + h * NS:b * P + (h + 1) * NS],
                                       ring[:, n % 4, m, h * XD:(h + 1) * XD], start=b == 0 and m == 0,
                                       stop=b == DEC_B - 1 and m == 1, skip_group_check=True, tile_position=(0, h * NS))
                mm.then_inc(s("oS_mm"), 1)
            pe.wait_ge(s("oS_out"), l + 1)
            for d in range(2):
                tr = transpose(pe, ps[:, 7, d * P:(d + 1) * P], pS[:, d * P:(d + 1) * P])
            tr.then_inc(s("o_ps"), 1)

        block = ctx.enter_context(nc.Block())

        @block.sync
        def _(sp):
            sp.dma_start(ident[:], a["c_ident"]).then_inc(s("x_in"), 16)
            sp.dma_start(xn[:, 0:2, :], a["x_prompt"][0].rearrange("(r p) d -> p r d", p=P)).then_inc(s("x_in"), 16)
            sp.dma_start(xn[0:NS, 2, :], a["x_sample"].rearrange("b t d -> (b t) d")).then_inc(s("x_in"), 16)
            for n, name in enumerate(GAINS):
                sp.dma_start(rowsn[2 * DT * n:2 * DT * (n + 1), :], a[name].rearrange("l (t p) -> (l t) p", p=P)).then_inc(s("gain_in"), 16)
            rows = 2 * DT * len(GAINS)
            sp.dma_start(rowsn[rows:rows + 4, :], a["sgu_vnorm"][0].rearrange("(t p) -> t p", p=P)).then_inc(s("gain_in"), 16)
            sp.dma_start(rowsn[rows + 4:rows + 16, :], a["conv_short"][0].rearrange("j (t p) -> (j t) p", p=P)).then_inc(s("gain_in"), 16)
            sp.sem_inc(landed[0], 16)
            sp.sem_inc(landed[1], 16)
            for g in order:
                load_weights(sp, g)

        @block.gpsimd
        def _(pool):
            stores[0] = 0

            def store(dst, src):
                pool.dma_start(dst, src).then_inc(s("stored"), 16)
                stores[0] += 16

            cf = a["conv_ffn"].rearrange("l j (t p) -> (l j t) p", p=P)
            pool.dma_start(cwn[:, 0:2, :], cf[0:2 * P].rearrange("(r p) c -> p r c", p=P)).then_inc(s("taps_in"), 16)
            pool.dma_start(cwn[0:8, 2, :], cf[2 * P:2 * P + 8]).then_inc(s("taps_in"), 16)
            pool.dma_start(scn[0:64, :], a["state_shortconv"][0].rearrange("b j (t p) -> t (b j) p", p=P)).then_inc(s("taps_in"), 16)
            pool.dma_start(sgn[:], a["sgu_w"][0].rearrange("g t s -> t g s")).then_inc(s("sgu_in"), 16)
            pool.memset(bdn[0:NS], 0.0).then_inc(s("bd_zero"), 1)
            pool.wait_ge(s("bd_zero"), 1)
            for b in range(DEC_B):
                r = slice(DEC_T * b, DEC_T * b + DEC_T)
                pool.dma_start(bdn[r, :, r], a["sgu_w"][0, :, 0:DEC_T, 0:DEC_T]
                               .rearrange("g t s -> t g s")).then_inc(s("bd_in"), 16)
            bias = a["sgu_b"][0]
            for c in range(SEQ // CHUNK):
                pool.dma_start(sbias[:, :, c * CHUNK:(c + 1) * CHUNK],
                               bias.unsqueeze(0).to_broadcast([P, 4, CHUNK])).then_inc(s("bias_in"), 16)
            for b in range(DEC_B):
                c = SEQ + DEC_T * b
                pool.dma_start(sbias[:, :, c:c + DEC_T],
                               bias[:, 0:DEC_T].unsqueeze(0).to_broadcast([P, 4, DEC_T])).then_inc(s("bias_in"), 16)
            pool.wait_ge(s("sgu_in"), 16)
            pool.affine_select(out=sgn[:], in_=sgn[:], compare_op=ALU.is_ge, fill=0.0, base=0,
                               pattern=[[0, 4], [-1, P]], channel_multiplier=1).then_inc(s("sgu_masked"), 1)
            pool.wait_ge(s("bd_in"), 16 * DEC_B)
            pool.affine_select(out=bdn[0:NS], in_=bdn[0:NS], compare_op=ALU.is_ge, fill=0.0, base=0,
                               pattern=[[0, 4], [-1, NS]], channel_multiplier=1).then_inc(s("sgu_masked"), 1)

            for l in L:
                if l == 1:
                    pool_retention(pool, store)
                if l == 0:
                    pool.wait_ge(s("const_ps"), 4)
                else:
                    pool.wait_ge(s("rg_lo"), 10)
                pool.dma_start(memn[:], a["mem_prompt"][0].rearrange("(r p) d -> p r d", p=P)).then_inc(s("mem_in"), 16)
                if l == 0:
                    pool.wait_ge(s("vnat_ready"), 3)
                    store(sgu_v[0].rearrange("b t d -> (b t) d"), vnat[0:NS, 2, :])
                    pool.wait_ge(s("sco_ready"), 1)
                    store(sc_prompt[0, 0].rearrange("j (t p) -> t j p", p=P), sco[0:8, 0, :])
                    store(sc_sample[0].rearrange("b j (t p) -> t (b j) p", p=P), sco[0:64, 1, :])
                    pool.wait_ge(s("stored"), stores[0])
                    pool.wait_ge(s("even_lo"), 8)
                else:
                    pool.wait_ge(w_used, CREDIT + 2 * (G["out", l].first + G["out", l].chunks))

                def cache(n):
                    src = a["cache_mem_k" if n < DEC_B else "cache_mem_v"][l, n % DEC_B]
                    pool.dma_start(ring[:, n % 4], src.rearrange("(r p) h d -> p r (h d)", p=P)).then_inc(s(f"cache{n % 4}"), 16)
                for n in range(4):
                    cache(n)
                pool.memset(qB[:], 0.0).then_inc(s("own_zero"), 1)
                scale_branch(pool, 3 * l)
                pool.wait_ge(s("k_nat"), CREDIT + 8 * l + 8)
                pool.dma_start(mem_k[l, 0].rearrange("(r p) h d -> p r (h d)", p=P), kN[:]).then_inc(s("kv_stored"), 16)
                pool.wait_ge(s("v_nat"), CREDIT + 8 * l + 8)
                pool.dma_start(mem_v[l, 0].rearrange("(r p) h d -> p r (h d)", p=P), vN[:]).then_inc(s("kv_stored"), 16)
                pool.wait_ge(s("sc_ps"), 4 * l + 4)
                pool.memset(pB[:], 0.0).then_inc(s("own_zero"), 1)
                for n in range(4, 2 * DEC_B):
                    if n - 4 < DEC_B:
                        pool.wait_ge(s("kTb_ps"), 32 * l + 4 * (n - 3))
                    else:
                        pool.wait_ge(s("oS_mm"), 8 * l + n - 4 - DEC_B + 1)
                    cache(n)

                pool.wait_ge(s("oh_lo"), 5 * l + 5)
                pool.wait_ge(s("oS_mm"), 8 * l + 8)
                pool.wait_ge(s("kv_stored"), 32 * l + 32)
                rows = a["state_ffn_conv"][l].rearrange("b j (t p) -> t (b j) p", p=P)
                for r in range(6):
                    n = min(8, 2 * FT - 8 * r)
                    pool.dma_start(stn[0:16 * n, r, :], rows[8 * r:8 * r + n]).then_inc(s("st_in"), 16)
                scale_branch(pool, 3 * l + 1)
                pool.wait_ge(s("stT_ready"), 2 * l + 2)

                def prefix(i):
                    for t in range(4):
                        pool.wait_ge(s("conv_done"), i * 4 + 44 * l + t + 1)
                        pool.tensor_copy(zb[:, t, PG:, 0:2],
                                         stT[:, bass.ds(i * 2 + FT * (t // 2) + t % 2, 1), :]
                                         .rearrange("p o (b j) -> p (o b) j", j=2)).then_inc(s("prefix"), 1)

                def tail(i, half):
                    for t in (2 * half, 2 * half + 1):
                        pool.wait_ge(s("up_taken"), CREDIT + i * 4 + 44 * l + t + 1)
                        col = i * 2 + FT * (t // 2) + t % 2
                        pool.tensor_copy(tlS[:, bass.ds(col, 1), :].rearrange("p o (b j) -> p (o b) j", j=2),
                                         zb[:, t, PG:, 4:6])
                        pool.tensor_copy(tlP[:, bass.ds(col, 1), :], zb[:, t, PG - 1:PG, 4:6]).then_inc(s("tails"), 1)

                def inner_low(i):
                    for j in range(2):
                        pool.wait_ge(s("a_hi"), i * 2 + 22 * l + j + 1)
                        pool.tensor_tensor(aL[:, i * 2 + j, :], pd[:, j, :], aH[:, i * 2 + j, :].bitcast(F32),
                                           ALU.subtract).then_inc(s("a_lo"), 1)

                def inner(i):
                    for j in range(2):
                        pool.wait_ge(s("gelu"), i * 2 + 22 * l + j + 1)
                        pool.wait_ge(s("conv_done"), CREDIT + i * 4 + 44 * l + 3 + j)
                        pool.wait_ge(s("a_lo"), i * 2 + 22 * l + j + 1)
                        pool.tensor_tensor(pd[:, j, :], ge[:, j, :], cb[:, 2 + j, :], ALU.mult).then_inc(s("prod"), 1)

                def step(i, first=False):
                    prefix(i)
                    tail(i, 0)
                    if not first:
                        inner_low(i - 1)
                    tail(i, 1)
                    inner(i)
                step(0, first=True)
                with pool.Fori(1, G["up", l].steps) as i:
                    step(i)
                inner_low(G["up", l].steps - 1)
                pool.wait_ge(s("tlo_ready"), 2 * l + 2)
                rows = fc_sample[l].rearrange("b j (t p) -> t (b j) p", p=P)
                for r in range(6):
                    n = min(8, 2 * FT - 8 * r)
                    store(rows[8 * r:8 * r + n], tlo[0:16 * n, r, :])
                store(fc_prompt[l, 0].rearrange("j (t p) -> t j p", p=P), tlo[0:4 * FT, 6, :])
                pool.wait_ge(s("stored"), stores[0])

                scale_branch(pool, 3 * l + 2)

            for half in range(2):
                cut = slice(512 * half, 512 * half + 512)
                pool.wait_ge(s("y_out"), 3 * half + 3)
                store(y_prompt[0].rearrange("(r p) d -> p r d", p=P)[:, :, cut], yn[:, 0:2, cut])
                store(y_sample.rearrange("b t d -> (b t) d")[:, cut], yn[0:NS, 2, cut])
            pool.wait_ge(s("stored"), stores[0])

        @block.scalar
        def _(act):
            for t in range(DT):
                act.wait_ge(s("xt_ps"), t + 1)
                act.activation(xT[:, t, :], ps[:, t % 4, 0:T], ACT.Copy).then_inc(x_ready, 1)
            act.wait_ge(s("const_ps"), 1)
            act.activation(gT[:], ps[:, 5, 0:P], ACT.Copy).then_inc(s("gT_ready"), 1)
            act.wait_ge(s("gT_ready"), 1)
            act.wait_ge(s("const_ps"), 2)
            act.activation(cwT[:, 0:2 * P + 8], ps[:, 6, 0:2 * P + 8], ACT.Copy).then_inc(s("gT_ready"), 1)
            act.wait_ge(s("set_up"), 2)
            split(act, order[0], 0, 0, True)
            gained_high(act, 0, squares=False)
            split(act, order[0], 0, 1, True)
            for t in range(DT):
                act.activation(sq[:, t, :], xT[:, t, :], ACT.Square).then_inc(sq_ready, 1)

            for l in L:
                q = 3 * l
                take_root(act, 2 * q)
                (act_even if l % 2 == 0 else act_odd)(act, l)

                def mem_squares():
                    act.wait_ge(s("mem_in"), 16 * l + 16)
                    for r in range(2):
                        act.activation(kN[:, r, :], memn[:, r, :], ACT.Square,
                                       accum_out=small[:, 1 + r:2 + r]).then_inc(s("mem_sq"), 1)
                    act.wait_ge(s("mem_sq"), 2 * l + 2)
                    act.activation(small[:, 3:5], small[:, 1:3], ACT.Sqrt, bias=eps_col, scale=1.0 / D).then_inc(s("mem_root"), 1)

                def mem_high(t0=0, t1=6):
                    for t in range(t0, t1):
                        act.wait_ge(s("memT_ps"), 4 * l + t // 2 + 1)
                        act.activation(mh[:, t, :], ps[:, 5 + t // 2 % 3, (t % 2) * N_MEM:(t % 2 + 1) * N_MEM],
                                       ACT.Copy, scale=memgain(l, t)).then_inc(s("mem_hi"), 1)
                branch_out_act(act, G["out", l], q, mem_squares, mem_high)
                mem_high(6, 8)
                held(act, G["out", l], True)

                def natural_out(name, dst):
                    def evac(i, half):
                        for j in range(2):
                            tiles_ready(act, G[name, l], i, half, j)
                            act.activation(dst[:, j, bass.ds(i * 2 * CW + half * CW, CW)],
                                           ps[:, 2 * half + j, 0:CW], ACT.Copy).then_inc(s(f"{name}_nat"), 1)
                    return evac
                gk, keys_out = G["k", l], natural_out("k", kN)
                keys_out(0, 0)
                split(act, *target(gk, 0, 0, False), True)
                take_root(act, 2 * q + 1)
                keys_out(0, 1)
                split(act, *target(gk, 0, 1, False), True)
                gained_high(act, q + 1)
                run(act, gk, True, keys_out, 1, 2)
                take_root(act, 2 * q + 2)
                run(act, G["v", l], True, natural_out("v", vN))
                for r in range(4):
                    act.wait_ge(s("kT_ps"), 4 * l + r + 1)
                    act.activation(kT[:, 2 * r:2 * r + 2, :],
                                   ps[:, 5 + r % 3, :].rearrange("p (t m) -> p t m", t=2), ACT.Copy).then_inc(s("kT_ready"), 1)

                run(act, G["q", l], True, nothing)
                act_attention(act, l)
                branch_out_act(act, G["o", l], q + 1)
                take_root(act, 2 * q + 3)
                held(act, G["o", l], True)

                act.wait_ge(s("kv_stored"), 32 * l + 32)
                gained_high(act, q + 2)
                for r in range(2):
                    act.wait_ge(s("stT_ps"), 2 * l + r + 1)
                    n = (32, 12)[r]
                    act.activation(stT[:, 32 * r:32 * r + n, :],
                                   ps[:, 5 + r, 0:16 * n].rearrange("p (t r) -> p t r", r=16), ACT.Copy).then_inc(s("stT_ready"), 1)
                take_root(act, 2 * q + 4)

                gu = G["up", l]

                def inner_high(i):
                    for j in range(2):
                        act.wait_ge(s("prod"), i * 2 + 22 * l + j + 3)
                        act.activation(aH[:, i * 2 + j, :], pd[:, j, :], ACT.Copy).then_inc(s("a_hi"), 1)

                def last_tap(i, half):
                    for j in range(2):
                        t = 2 * half + j
                        act.wait_ge(s("up_taken"), CREDIT + i * 4 + 44 * l + t + 1)
                        act.wait_ge(s("prod"), i * 2 + 22 * l + 2)
                        act.activation(zb[:, t, 1:PG, 0:2], zb[:, t, 0:PG - 1, 4:6], ACT.Copy)
                        act.activation(groups(cb[:, t, :]), zb[:, t, :, 2:PAD], ACT.Copy,
                                       scale=ftap(l, 2, i * 2 + FT * half + j)).then_inc(s("conv_in"), 1)

                def step(i, first=False, last=False):
                    split(act, *target(gu, i, 0, last), True)
                    if not first:
                        inner_high(i - 1)
                    last_tap(i, 0)
                    split(act, *target(gu, i, 1, last), True)
                    for j in range(2):
                        act.wait_ge(s("conv_done"), CREDIT + i * 4 + 44 * l + j + 1)
                        act.activation(ge[:, j, :], cb[:, j, :], ACT.Gelu_apprx_tanh).then_inc(s("gelu"), 1)
                    last_tap(i, 1)
                step(0, first=True)
                with act.Fori(1, gu.steps - 1) as i:
                    step(i)
                step(gu.steps - 1, last=True)
                inner_high(gu.steps - 1)
                for r in range(3):
                    act.wait_ge(s("tlo_ps"), 2 * l + min(r, 1) + 1)
                    if r == 0:
                        act.activation(tlo[:, 0:4, :], ps[:, 5, :].rearrange("p (r c) -> p r c", c=P), ACT.Copy)
                    elif r == 1:
                        act.activation(tlo[:, 4, :], ps[:, 6, 0:P], ACT.Copy)
                        act.activation(tlo[0:64, 5, :], ps[0:64, 6, P:2 * P], ACT.Copy).then_inc(s("tlo_ready"), 1)
                    else:
                        act.activation(tlo[0:4 * FT, 6, :], ps[0:4 * FT, 6, 2 * P:3 * P], ACT.Copy).then_inc(s("tlo_ready"), 1)
                branch_out_act(act, G["down", l], q + 2)
                take_root(act, 2 * q + 5)
                held(act, G["down", l], True)
                if l + 1 < DEPTH:
                    gained_high(act, q + 3)

            for n in range(6):
                half, r = divmod(n, 3)
                rows = P if r < 2 else NS
                act.wait_ge(s("y_ps"), n + 1)
                act.activation(yn[0:rows, r, 512 * half:512 * half + 512], ps[0:rows, n % 4, :], ACT.Copy).then_inc(s("y_out"), 1)

        @block.vector
        def _(dve):
            dve.memset(ones[:], 1.0).then_inc(s("set_up"), 1)
            dve.memset(small[:, 0:1], EPS).then_inc(s("set_up"), 1)
            dve.memset(zz[:, :, 0, 0:2], 0.0).then_inc(s("set_up"), 1)
            dve.sem_inc(lo_ready, CREDIT)
            split(dve, order[0], 0, 0, False)
            for l in L:
                q = 3 * l
                if l == 0:
                    for t in range(DT):
                        gained_low(dve, q, t)
                    split(dve, order[0], 0, 1, False)
                    sums(dve, 2 * q, 0)
                    sums(dve, 2 * q, 1)
                invert(dve, 2 * q)
                (dve_even if l % 2 == 0 else dve_odd)(dve, l)

                def mem_scale():
                    dve.wait_ge(s("mem_root"), l + 1)
                    dve.reciprocal(small[:, 5:7], small[:, 3:5]).then_inc(s("mem_inv"), 1)
                    dve.wait_ge(s("mem_inv"), l + 1)
                    for r in range(2):
                        dve.tensor_scalar(memn[:, r, :], memn[:, r, :], small[:, 5 + r:6 + r], None,
                                          ALU.mult).then_inc(s("mem_scaled"), 1)

                def mem_low(t0=0, t1=6):
                    for t in range(t0, t1):
                        dve.wait_ge(s("mem_hi"), 8 * l + 2 * (t // 2) + 2)
                        dve.scalar_tensor_tensor(out=ml[:, t, :], in0=ps[:, 5 + t // 2 % 3, (t % 2) * N_MEM:(t % 2 + 1) * N_MEM],
                                                 scalar=memgain(l, t), in1=mh[:, t, :].bitcast(F32), op0=ALU.mult,
                                                 op1=ALU.subtract).then_inc(s("mem_lo"), 1)
                branch_out_dve(dve, G["out", l], q, mem_scale, mem_low)
                mem_low(6, 8)
                held(dve, G["out", l], False)

                split(dve, *target(G["k", l], 0, 0, False), False)
                add_branch(dve, q, lambda: split(dve, *target(G["k", l], 0, 1, False), False), late=False)
                run(dve, G["k", l], False, nothing, 1, 2)
                invert(dve, 2 * q + 2)
                run(dve, G["v", l], False, nothing)

                def evac(i, half):
                    for j in range(2):
                        t = 2 * half + j
                        tiles_ready(dve, G["q", l], i, half, j)
                        dve.tensor_tensor(mT[:, i * 4 + t, :], ps[:, t, 0:T], rstd[:], ALU.mult).then_inc(s("q_ready"), 1)
                run(dve, G["q", l], False, evac)
                dve_attention(dve, l)
                branch_out_dve(dve, G["o", l], q + 1)
                add_branch(dve, q + 1, lambda: held(dve, G["o", l], False))
                dve.memset(zb[:, :, 0, 0:2], 0.0).then_inc(s("zb_zero"), 1)

                invert(dve, 2 * q + 4)

                gu = G["up", l]

                def step(i, last=False):
                    for half in range(2):
                        pair = [(2 * half + j, i * 2 + FT * half + j) for j in range(2)]
                        for t, tile in pair:
                            tiles_ready(dve, gu, i, half, t % 2)
                            dve.wait_ge(s("conv_done"), i * 4 + 44 * l + t + 1)
                            dve.wait_ge(s("tails"), i * 4 + 44 * l + t + 1)
                            dve.tensor_tensor(zb[:, t, :, 2:PAD], groups(ps[:, t, 0:T]), groups(rstd[:]), ALU.mult).then_inc(s("up_taken"), 1)
                        split(dve, *target(gu, i, half, last), False)
                        for t, tile in pair:
                            if t == 0:
                                dve.wait_ge(s("zb_zero"), l + 1)
                            dve.wait_ge(s("conv_in"), CREDIT + i * 4 + 44 * l + t + 1)
                            dve.wait_ge(s("prefix"), i * 4 + 44 * l + t + 1)
                            dve.scalar_tensor_tensor(out=groups(cb[:, t, :]), in0=zb[:, t, :, 1:5], scalar=ftap(l, 1, tile),
                                                     in1=groups(cb[:, t, :]), op0=ALU.mult, op1=ALU.add).then_inc(s("conv_mid"), 1)
                        for t, tile in pair:
                            dve.wait_ge(s("conv_mid"), i * 4 + 44 * l + t + 1)
                            dve.scalar_tensor_tensor(out=groups(cb[:, t, :]), in0=zb[:, t, :, 0:4], scalar=ftap(l, 0, tile),
                                                     in1=groups(cb[:, t, :]), op0=ALU.mult, op1=ALU.add).then_inc(s("conv_done"), 1)
                with dve.Fori(0, gu.steps - 1) as i:
                    step(i)
                step(gu.steps - 1, last=True)
                branch_out_dve(dve, G["down", l], q + 2)
                add_branch(dve, q + 2, lambda: held(dve, G["down", l], False))

        @block.tensor
        def _(pe):
            for name in ("in_even", "q_ready", "k_nat", "v_nat", "z_ready"):
                pe.sem_inc(s(name), CREDIT)
            for name in ("conv_in", "conv_done", "tails", "up_taken", "turned"):
                pe.sem_inc(s(name), CREDIT)
            for name in ("prod", "a_lo"):
                pe.sem_inc(s(name), 2)
            pe.sem_inc(sq_ready, CREDIT)
            pe.sem_inc(w_used, CREDIT)
            pe.wait_ge(s("x_in"), 48)
            for t in range(DT):
                if t >= 4:
                    pe.wait_ge(x_ready, t - 3)
                for r in range(3):
                    n = P if r < 2 else NS
                    tr = transpose(pe, ps[:, t % 4, r * P:r * P + n], xn[0:n, r, t * P:(t + 1) * P], n)
                tr.then_inc(s("xt_ps"), 1)
            pe.wait_ge(s("gain_in"), 16 * (len(GAINS) + 2))
            transpose(pe, ps[:, 5, 0:P], rowsn[:]).then_inc(s("const_ps"), 1)
            pe.wait_ge(s("taps_in"), 48)
            for r in range(3):
                n = P if r < 2 else 8
                tr = transpose(pe, ps[:, 6, r * P:r * P + n], cwn[0:n, r, :], n)
            tr.then_inc(s("const_ps"), 1)
            pe.wait_ge(s("set_up"), 1)

            for l in L:
                q = 3 * l
                if l == 0:
                    pe.wait_ge(x_ready, 8)
                (pe_even if l % 2 == 0 else pe_odd)(pe, l)

                def turn_memory(r):
                    if r == 0:
                        pe.wait_ge(s("mem_scaled"), 2 * l + 2)
                    if r == 3:
                        pe.wait_ge(s("mem_lo"), 8 * l + 2)
                    for t in (2 * r, 2 * r + 1):
                        for m in range(2):
                            c = (t % 2) * N_MEM + m * P
                            tr = transpose(pe, ps[:, 5 + r % 3, c:c + P], memn[:, m, t * P:(t + 1) * P])
                    tr.then_inc(s("memT_ps"), 1)

                def half_way(i, idx):
                    if idx == G["out", l].nk - 1:
                        for r in range(3):
                            turn_memory(r)
                mixed = (lambda k: (hh[:, k, :], hl[:, k, :]) if k < 4 else (bh[:, k - 4, :], bl[:, k - 4, :])) if l % 2 == 0 else \
                    (lambda k: (hh[:, k, :], hl[:, k, :]) if k < 8 else (h2h[:, k - 8, :], h2l[:, k - 8, :]))
                first_sq = CREDIT + 8 * (2 * q + 1)
                if l % 2 == 0:
                    pe.wait_ge(s("in_even"), CREDIT + 20)
                    products(pe, G["out", l], mixed, sq_ready, first_sq, i0=0, i1=1, turn=4,
                             need=lambda k: pe.wait_ge(s("even_lo"), (k + 4) % 8 + 1))
                else:
                    products(pe, G["out", l], mixed, sq_ready, first_sq, i0=0, i1=1,
                             need=lambda k: pe.wait_ge(s("rg_lo"), 9 + k // 8))
                products(pe, G["out", l], mixed, sq_ready, first_sq, i0=1, i1=2, hook=half_way)
                turn_memory(3)

                mem = lambda k: (mh[:, k, :], ml[:, k, :])
                pe.wait_ge(sq_ready, first_sq + 6)
                products(pe, G["k", l], mem, s("k_nat"), CREDIT + 8 * l, natural=True, i0=0, i1=1,
                         need=lambda k: pe.wait_ge(s("mem_lo"), 8 * l + k + 1),
                         hook=lambda i, idx: ssq(pe, 2 * q + 1) if idx == 0 else None)
                products(pe, G["k", l], mem, s("k_nat"), CREDIT + 8 * l, natural=True, i0=1, i1=2)
                ssq(pe, 2 * q + 2)
                pe.wait_ge(s("k_nat"), CREDIT + 8 * l + 8)
                products(pe, G["v", l], mem, s("v_nat"), CREDIT + 8 * l, natural=True)
                for r in range(4):
                    if r == 3:
                        pe.wait_ge(s("kT_ready"), 4 * l + 1)
                    for t in (2 * r, 2 * r + 1):
                        for m in range(2):
                            c = (t % 2) * N_MEM + m * P
                            tr = transpose(pe, ps[:, 5 + r % 3, c:c + P], kN[:, m, t * P:(t + 1) * P])
                    tr.then_inc(s("kT_ps"), 1)

                pe.wait_ge(h_lo, DT * (q + 2))
                pe.wait_ge(s("v_nat"), CREDIT + 8 * l + 8)
                products(pe, G["q", l], normed, s("q_ready"), CREDIT + 8 * l)
                pe_attention(pe, l)
                pe.wait_ge(s("oh_lo"), 5 * l + 5)
                out_pe(pe, G["o", l], q + 1, normed)

                for r in range(6):
                    n = min(8, 2 * FT - 8 * r) * 16
                    if r == 0:
                        pe.wait_ge(s("st_in"), 96 * l + 96)
                    tr = transpose(pe, ps[:, 5 + r // 4, (r % 4) * P:(r % 4) * P + n], stn[0:n, r, :], n)
                    if r in (3, 5):
                        tr.then_inc(s("stT_ps"), 1)
                first_step(pe, G["up", l], q + 2, normed, s("up_taken"), CREDIT + 44 * l)
                products(pe, G["up", l], normed, s("up_taken"), CREDIT + 44 * l, i0=1)
                pe.wait_ge(s("tails"), CREDIT + 44 * l + 44)
                for r in range(7):
                    if r < 6:
                        n = min(8, 2 * FT - 8 * r) * 16
                        src = tlS[:, 8 * r:8 * r + n // 16, :].rearrange("p t r -> p (t r)")
                    else:
                        n = 4 * FT
                        src = tlP[:].rearrange("p t j -> p (t j)")
                    c = (r % 4) * P
                    tr = transpose(pe, ps[0:n, 5 + r // 4, c:c + P], src)
                    if r in (3, 6):
                        tr.then_inc(s("tlo_ps"), 1)
                pe.wait_ge(s("up_taken"), CREDIT + 44 * l + 44)
                inner = lambda k: (aH[:, k, :], aL[:, k, :])
                first_sq = CREDIT + 8 * (2 * q + 5)
                products(pe, G["down", l], inner, sq_ready, first_sq, i0=0, i1=1,
                         need=lambda k: pe.wait_ge(s("a_lo"), 22 * l + 2 + k + 1))
                products(pe, G["down", l], inner, sq_ready, first_sq, i0=1, i1=2)
                pe.wait_ge(w_used, CREDIT + 2 * (G["down", l].first + G["down", l].chunks))
                pe.sem_inc(s("a_free"), 1)
                ssq(pe, 2 * q + 5)

            for n in range(6):
                half, r = divmod(n, 3)
                rows = P if r < 2 else NS
                if n >= 4:
                    pe.wait_ge(s("y_out"), n - 3)
                for t in range(4):
                    pe.wait_ge(x_ready, 8 * 6 + 4 * half + t + 1)
                    tr = transpose(pe, ps[0:rows, n % 4, t * P:(t + 1) * P],
                                   xT[:, 4 * half + t, r * P:r * P + rows])
                tr.then_inc(s("y_ps"), 1)

def constants():
    f = np.float32
    half = RDK // 2
    pos = np.concatenate([np.arange(SEQ), np.tile(PAST + np.arange(DEC_T), DEC_B)]).astype(f)
    inv = f(10000.0) ** (-np.arange(half, dtype=f) / f(half))
    ang = inv[:, None] * pos[None, :]
    rope = np.stack([np.cos(ang), np.sin(ang)], axis=1).astype(f)
    lg = np.log1p(-np.exp2(f(-5) - np.arange(RH, dtype=f))).astype(f)
    sc = f(RDK ** -0.5)

    def decay(n, h):
        d = np.arange(n, dtype=f)[None, :] - np.arange(n, dtype=f)[:, None]
        return np.where(d >= 0, np.exp(lg[h] * np.maximum(d, 0)), 0).astype(f) * sc

    ret = np.zeros((P, 8 * P + 4), f)
    retS = np.zeros((P, 12 * NS + 8), f)
    tok = np.arange(NS)
    same = (tok[:, None] // DEC_T == tok[None, :] // DEC_T)
    for h in range(RH):
        ret[:, h * P:(h + 1) * P] = decay(CHUNK, h)
        ret[:, (4 + h) * P:(5 + h) * P] = np.exp(lg[h] * (np.arange(CHUNK, dtype=f) + 1)) * sc
        ret[:, 8 * P + h] = np.exp(lg[h] * (CHUNK - 1 - np.arange(CHUNK, dtype=f)))
        small = np.tile(decay(DEC_T, h), (DEC_B, DEC_B)) * same
        retS[0:2 * NS, h * NS:(h + 1) * NS] = np.tile(small, (2, 1))
        retS[:, (4 + h) * NS:(5 + h) * NS] = np.exp(lg[h] * (tok % DEC_T + 1).astype(f)) * sc
        retS[:, (8 + h) * NS:(9 + h) * NS] = np.exp(lg[h] * (DEC_T - 1 - tok % DEC_T).astype(f))
    for b in range(DEC_B):
        retS[:, 12 * NS + b] = (np.arange(P) % NS) // DEC_T == b
    return {"c_ident": np.eye(P, dtype=f), "c_rope": rope, "c_ret": ret, "c_retS": retS}


OUTS = [(1, SEQ, D), (DEC_B, DEC_T, D), (DEPTH, 1, N_MEM, XH, XD), (DEPTH, 1, N_MEM, XH, XD),
        (1, 1, 2, 512), (1, DEC_B, 2, 512), (1, DEC_B, DEC_T, 512), (1, 1, RH, RDK, RDV),
        (1, DEC_B, RH, RDK, RDV), (DEPTH, 1, 2, 2 * DFF), (DEPTH, DEC_B, 2, 2 * DFF)]


def kernel(**inputs):
    import concourse.bacc as bacc
    from concourse.bass_utils import run_bass_kernel_spmd

    nc = bacc.Bacc("TRN2", target_bir_lowering=False, num_devices=1)
    arrays = {k: np.ascontiguousarray(v) for k, v in inputs.items()}
    arrays.update(constants())
    a = {k: nc.dram_tensor(k, v.shape, F32, kind="ExternalInput").ap() for k, v in arrays.items()}
    outs = [nc.dram_tensor(f"out_{i}", shape, F32, kind="ExternalOutput").ap() for i, shape in enumerate(OUTS)]
    build(nc, a, outs)
    r = run_bass_kernel_spmd(nc, [arrays], core_ids=[0]).results[0]
    return tuple(r[f"out_{i}"] for i in range(len(OUTS)))
```
